# Optimizing a Trainium2 kernel written in Bass

```python
import math
import jax
import jax.numpy as jnp
from jax import lax
import numpy as np

D_MODEL = 1024
BATCH = 1
SEQ = 512
DEPTH = 2

EPS = 1e-6
ROPE_THETA = 500000.0
Q_BLOCK = 128
D_FF = 2816
NEG_BIG = -1e30
FORCE_SCORE = 1e9

A_HEADS = 6
A_Q_RANK = 192
A_KV_RANK = 128
A_NOPE = 64
A_ROPE = 32
A_V = 64

B_HEADS = 6
B_KV_GROUPS = 2
B_HPG = B_HEADS // B_KV_GROUPS
B_DH = 64
B_ROT = B_DH // 4
CMP_LEN = 32
CMP_STRIDE = 16
SLC_LEN = 64
SLC_TOPN = 16
WINDOW = 512

C_HEADS = 4
C_DH = 32
C_ROT = C_DH // 4

MIX_WIDTH = A_HEADS * A_V + B_HEADS * B_DH + C_HEADS * 2 * C_DH
A_COLS = A_Q_RANK + A_KV_RANK + A_ROPE
B_COLS = B_HEADS * B_DH + 6 * B_KV_GROUPS * B_DH + 3 * B_HEADS
C_COLS = 3 * C_HEADS * 2 * C_DH
IN_COLS = A_COLS + B_COLS + C_COLS


def rmsnorm(x, g):
    xf = x.astype(jnp.float32)
    y = xf * lax.rsqrt(jnp.mean(xf * xf, axis=-1, keepdims=True) + EPS)
    return (y * g.astype(jnp.float32)).astype(x.dtype)

def rope_tables(positions, rot_dim):
    inv_freq = 1.0 / (ROPE_THETA ** (jnp.arange(0, rot_dim, 2, dtype=jnp.float32) / rot_dim))
    ang = positions.astype(jnp.float32)[..., None] * inv_freq
    return (jnp.cos(ang), jnp.sin(ang))

def apply_rope(x, cs):
    cos, sin = cs
    B, T, r2 = cos.shape
    shape = (B,) + (1,) * (x.ndim - 3) + (T, r2)
    cos = cos.reshape(shape)
    sin = sin.reshape(shape)
    xf = x.astype(jnp.float32)
    x1, x2 = xf[..., :r2], xf[..., r2:]
    return jnp.concatenate([x1 * cos - x2 * sin, x1 * sin + x2 * cos], axis=-1).astype(x.dtype)

def partial_rope(x, cs):
    r = 2 * cs[0].shape[-1]
    return jnp.concatenate([apply_rope(x[..., :r], cs), x[..., r:]], axis=-1)

def swiglu(x, wg, wu, wd):
    return (jax.nn.silu(x @ wg) * (x @ wu)) @ wd

def causal_block_attention(q, k, v, scale):
    B, H, T, dk = q.shape
    nb = T // Q_BLOCK
    q_blocks = jnp.moveaxis(q.reshape(B, H, nb, Q_BLOCK, dk), 2, 0)
    kpos = jnp.arange(T)

    def one_block(args):
        qi, i = args
        s = jnp.einsum('bhqd,bhkd->bhqk', qi, k, preferred_element_type=jnp.float32) * scale
        qpos = i * Q_BLOCK + jnp.arange(Q_BLOCK)
        s = jnp.where(kpos[None, :] <= qpos[:, None], s, -jnp.inf)
        p = jax.nn.softmax(s, axis=-1)
        return jnp.einsum('bhqk,bhkd->bhqd', p.astype(v.dtype), v)

    o = lax.map(one_block, (q_blocks, jnp.arange(nb)))
    return jnp.moveaxis(o, 0, 2).reshape(B, H, T, v.shape[-1])

def mla_mixer(h, cs_a, q_norm, kv_norm, w_uq, w_ukv):
    B, T, _ = h.shape
    c_q, c_kv, k_pe = jnp.split(h, [A_Q_RANK, A_Q_RANK + A_KV_RANK], axis=-1)
    q = (rmsnorm(c_q, q_norm) @ w_uq).reshape(B, T, A_HEADS, A_NOPE + A_ROPE).transpose(0, 2, 1, 3)
    kv = (rmsnorm(c_kv, kv_norm) @ w_ukv).reshape(B, T, A_HEADS, A_NOPE + A_V).transpose(0, 2, 1, 3)
    q = jnp.concatenate([q[..., :A_NOPE], apply_rope(q[..., A_NOPE:], cs_a)], axis=-1)
    k_pe = apply_rope(k_pe[:, None], cs_a)
    k = jnp.concatenate([kv[..., :A_NOPE], jnp.broadcast_to(k_pe, (B, A_HEADS, T, A_ROPE))], axis=-1)
    v = kv[..., A_NOPE:]
    o = causal_block_attention(q, k, v, (A_NOPE + A_ROPE) ** -0.5)
    return o.transpose(0, 2, 1, 3).reshape(B, T, A_HEADS * A_V)

def nsa_mixer(h, cs_b, pe_k, pe_v, phi_k1, phi_k2, phi_v1, phi_v2):
    B, T, _ = h.shape
    G, Hg, DH = B_KV_GROUPS, B_HPG, B_DH
    qw, kvw = B_HEADS * DH, G * DH
    offs = [qw + j * kvw for j in range(7)]
    q, kc, vc, ks, vs, kw, vw, gate_logits = jnp.split(h, offs, axis=-1)

    def split_kv(t):
        return t.reshape(B, T, G, DH).transpose(0, 2, 1, 3)

    q = partial_rope(q.reshape(B, T, G, Hg, DH).transpose(0, 2, 3, 1, 4), cs_b)
    kc, ks, kw = [partial_rope(split_kv(t), cs_b) for t in (kc, ks, kw)]
    vc, vs, vw = [split_kv(t) for t in (vc, vs, vw)]
    scale = DH ** -0.5
    tpos = jnp.arange(T)
    nb = T // Q_BLOCK

    n_cmp = (T - CMP_LEN) // CMP_STRIDE + 1
    cmp_idx = jnp.arange(n_cmp)[:, None] * CMP_STRIDE + jnp.arange(CMP_LEN)[None, :]

    def compress(t, pe, w1, w2):
        blk = (t[:, :, cmp_idx] + pe).reshape(B, G, n_cmp, CMP_LEN * DH)
        return jax.nn.silu(blk @ w1) @ w2

    k_cmp = compress(kc, pe_k, phi_k1, phi_k2)
    v_cmp = compress(vc, pe_v, phi_v1, phi_v2)
    s_cmp = jnp.einsum('bghtd,bgcd->bghtc', q, k_cmp, preferred_element_type=jnp.float32) * scale
    cmp_mask = cmp_idx[:, -1][None, :] <= tpos[:, None]
    p_cmp = jax.nn.softmax(jnp.where(cmp_mask, s_cmp, NEG_BIG), axis=-1) * cmp_mask
    o_cmp = jnp.einsum('bghtc,bgcd->bghtd', p_cmp.astype(v_cmp.dtype), v_cmp)

    n_slc = T // SLC_LEN
    top_n = min(SLC_TOPN, n_slc)
    blk_start = jnp.arange(n_slc) * SLC_LEN
    overlap = ((cmp_idx[:, 0][:, None] < blk_start[None, :] + SLC_LEN)
               & (cmp_idx[:, -1][:, None] >= blk_start[None, :])).astype(jnp.float32)
    imp = jnp.einsum('bghtc,cm->bgtm', p_cmp, overlap)
    cur = (tpos // SLC_LEN)[:, None]
    m = jnp.arange(n_slc)[None, :]
    forced = (m == 0) | (m == cur) | (m == cur - 1)
    score = jnp.where(forced, FORCE_SCORE, jnp.where(m <= cur, imp, -1.0))
    sel = lax.top_k(score, top_n)[1]

    ks_blk = ks.reshape(B, G, n_slc, SLC_LEN, DH)
    vs_blk = vs.reshape(B, G, n_slc, SLC_LEN, DH)
    q_blocks = jnp.moveaxis(q.reshape(B, G, Hg, nb, Q_BLOCK, DH), 3, 0)
    sel_blocks = jnp.moveaxis(sel.reshape(B, G, nb, Q_BLOCK, top_n), 2, 0)
    gather_blocks = jax.vmap(jax.vmap(lambda blocks, ids: blocks[ids]))

    def slc_block(args):
        qi, si, i = args
        kg = gather_blocks(ks_blk, si).reshape(B, G, Q_BLOCK, top_n * SLC_LEN, DH)
        vg = gather_blocks(vs_blk, si).reshape(B, G, Q_BLOCK, top_n * SLC_LEN, DH)
        kpos = (si[..., None] * SLC_LEN + jnp.arange(SLC_LEN)).reshape(B, G, Q_BLOCK, top_n * SLC_LEN)
        qpos = i * Q_BLOCK + jnp.arange(Q_BLOCK)
        valid = kpos <= qpos[:, None]
        s = jnp.einsum('bghqd,bgqkd->bghqk', qi, kg, preferred_element_type=jnp.float32) * scale
        p = jax.nn.softmax(jnp.where(valid[:, :, None], s, -jnp.inf), axis=-1)
        return jnp.einsum('bghqk,bgqkd->bghqd', p.astype(vg.dtype), vg)

    o_slc = lax.map(slc_block, (q_blocks, sel_blocks, jnp.arange(nb)))
    o_slc = jnp.moveaxis(o_slc, 0, 3).reshape(B, G, Hg, T, DH)

    kw_pad = jnp.pad(kw, ((0, 0), (0, 0), (WINDOW, 0), (0, 0)))
    vw_pad = jnp.pad(vw, ((0, 0), (0, 0), (WINDOW, 0), (0, 0)))
    band = jnp.arange(nb)[:, None] * Q_BLOCK + jnp.arange(WINDOW + Q_BLOCK)[None, :]
    kband = kw_pad[:, :, band]
    vband = vw_pad[:, :, band]
    kpos_w = band - WINDOW
    qpos_w = tpos.reshape(nb, Q_BLOCK)
    dist = qpos_w[:, :, None] - kpos_w[:, None, :]
    wmask = (dist >= 0) & (dist < WINDOW) & (kpos_w[:, None, :] >= 0)
    qwb = q.reshape(B, G, Hg, nb, Q_BLOCK, DH)
    s_w = jnp.einsum('bghnqd,bgnkd->bghnqk', qwb, kband, preferred_element_type=jnp.float32) * scale
    p_w = jax.nn.softmax(jnp.where(wmask, s_w, -jnp.inf), axis=-1)
    o_win = jnp.einsum('bghnqk,bgnkd->bghnqd', p_w.astype(vband.dtype), vband).reshape(B, G, Hg, T, DH)

    g = jax.nn.sigmoid(gate_logits.astype(jnp.float32)).reshape(B, T, G, Hg, 3)
    g = g.transpose(0, 2, 3, 1, 4).astype(q.dtype)
    o = g[..., 0:1] * o_cmp + g[..., 1:2] * o_slc + g[..., 2:3] * o_win
    return o.transpose(0, 3, 1, 2, 4).reshape(B, T, B_HEADS * DH)

def diff_mixer(h, cs_c, lq1, lk1, lq2, lk2, sub_norm, layer_idx):
    B, T, _ = h.shape
    q, k, v = jnp.split(h, 3, axis=-1)
    q = partial_rope(q.reshape(B, T, C_HEADS, 2, C_DH).transpose(0, 2, 3, 1, 4), cs_c)
    k = partial_rope(k.reshape(B, T, C_HEADS, 2, C_DH).transpose(0, 2, 3, 1, 4), cs_c)
    v = v.reshape(B, T, C_HEADS, 2 * C_DH).transpose(0, 2, 1, 3)
    lam_init = 0.8 - 0.6 * math.exp(-0.3 * layer_idx)
    f32 = jnp.float32
    lam = (jnp.exp(jnp.sum(lq1.astype(f32) * lk1.astype(f32)))
           - jnp.exp(jnp.sum(lq2.astype(f32) * lk2.astype(f32))) + lam_init)
    scale = C_DH ** -0.5
    o1 = causal_block_attention(q[:, :, 0], k[:, :, 0], v, scale)
    o2 = causal_block_attention(q[:, :, 1], k[:, :, 1], v, scale)
    o = o1.astype(f32) - lam * o2.astype(f32)
    o = (rmsnorm(o, sub_norm) * (1.0 - lam_init)).astype(h.dtype)
    return o.transpose(0, 2, 1, 3).reshape(B, T, C_HEADS * 2 * C_DH)

def first_inputs(seed: int = 0) -> dict:
    key = jax.random.key(seed)
    keys = iter(jax.random.split(key, 40))
    f32 = jnp.float32
    L = DEPTH

    def nrm(shape, fan_in):
        return jax.random.normal(next(keys), shape, f32) * (fan_in ** -0.5)

    def gain(shape):
        return 1.0 + 0.02 * jax.random.normal(next(keys), shape, f32)

    def small(shape, s):
        return s * jax.random.normal(next(keys), shape, f32)

    x = jax.random.normal(next(keys), (BATCH, SEQ, D_MODEL), f32)
    offset = jax.random.randint(next(keys), (BATCH, 1), 0, 1024, dtype=jnp.int32)
    positions = offset + jnp.arange(SEQ, dtype=jnp.int32)[None, :]
    return {
        'x': x,
        'positions': positions,
        'ffn1_norm': gain((L, D_MODEL)),
        'ffn1_wg': nrm((L, D_MODEL, D_FF), D_MODEL),
        'ffn1_wu': nrm((L, D_MODEL, D_FF), D_MODEL),
        'ffn1_wd': nrm((L, D_FF, D_MODEL), D_FF),
        'mix_norm': gain((L, D_MODEL)),
        'w_in': nrm((L, D_MODEL, IN_COLS), D_MODEL),
        'mla_q_norm': gain((L, A_Q_RANK)),
        'mla_kv_norm': gain((L, A_KV_RANK)),
        'mla_w_uq': nrm((L, A_Q_RANK, A_HEADS * (A_NOPE + A_ROPE)), A_Q_RANK),
        'mla_w_ukv': nrm((L, A_KV_RANK, A_HEADS * (A_NOPE + A_V)), A_KV_RANK),
        'nsa_pe_k': small((L, CMP_LEN, B_DH), 0.1),
        'nsa_pe_v': small((L, CMP_LEN, B_DH), 0.1),
        'nsa_phi_k1': nrm((L, CMP_LEN * B_DH, B_DH), CMP_LEN * B_DH),
        'nsa_phi_k2': nrm((L, B_DH, B_DH), B_DH),
        'nsa_phi_v1': nrm((L, CMP_LEN * B_DH, B_DH), CMP_LEN * B_DH),
        'nsa_phi_v2': nrm((L, B_DH, B_DH), B_DH),
        'diff_lq1': small((L, C_DH), 0.1),
        'diff_lk1': small((L, C_DH), 0.1),
        'diff_lq2': small((L, C_DH), 0.1),
        'diff_lk2': small((L, C_DH), 0.1),
        'diff_sub_norm': gain((L, 2 * C_DH)),
        'w_out': nrm((L, MIX_WIDTH, D_MODEL), MIX_WIDTH),
        'ffn2_norm': gain((L, D_MODEL)),
        'ffn2_wg': nrm((L, D_MODEL, D_FF), D_MODEL),
        'ffn2_wu': nrm((L, D_MODEL, D_FF), D_MODEL),
        'ffn2_wd': nrm((L, D_FF, D_MODEL), D_FF),
        'final_norm': gain((D_MODEL,)),
    }

def first_block(x, positions, ffn1_norm, ffn1_wg, ffn1_wu, ffn1_wd, mix_norm, w_in,
              mla_q_norm, mla_kv_norm, mla_w_uq, mla_w_ukv,
              nsa_pe_k, nsa_pe_v, nsa_phi_k1, nsa_phi_k2, nsa_phi_v1, nsa_phi_v2,
              diff_lq1, diff_lk1, diff_lq2, diff_lk2, diff_sub_norm, w_out,
              ffn2_norm, ffn2_wg, ffn2_wu, ffn2_wd, final_norm):
    cs_a = rope_tables(positions, A_ROPE)
    cs_b = rope_tables(positions, B_ROT)
    cs_c = rope_tables(positions, C_ROT)
    for l in range(DEPTH):
        x = x + 0.5 * swiglu(rmsnorm(x, ffn1_norm[l]), ffn1_wg[l], ffn1_wu[l], ffn1_wd[l])
        h = rmsnorm(x, mix_norm[l]) @ w_in[l]
        h_a, h_b, h_c = jnp.split(h, [A_COLS, A_COLS + B_COLS], axis=-1)
        o_a = mla_mixer(h_a, cs_a, mla_q_norm[l], mla_kv_norm[l], mla_w_uq[l], mla_w_ukv[l])
        o_b = nsa_mixer(h_b, cs_b, nsa_pe_k[l], nsa_pe_v[l], nsa_phi_k1[l], nsa_phi_k2[l],
                        nsa_phi_v1[l], nsa_phi_v2[l])
        o_c = diff_mixer(h_c, cs_c, diff_lq1[l], diff_lk1[l], diff_lq2[l], diff_lk2[l],
                         diff_sub_norm[l], l)
        o = jnp.concatenate([o_a, o_b, o_c], axis=-1)
        x = x + o @ w_out[l]
        x = x + 0.5 * swiglu(rmsnorm(x, ffn2_norm[l]), ffn2_wg[l], ffn2_wu[l], ffn2_wd[l])
    return rmsnorm(x, final_norm)


DEPTH_2 = 1

D_MIX = D_MODEL
ATTN_HEAD_DIM = 64
ATTN_HEADS = (D_MIX // 2) // ATTN_HEAD_DIM
ATTN_WIDTH = ATTN_HEADS * ATTN_HEAD_DIM
DILATED_PATTERNS = ((128, 1), (512, 4), (2048, 16))
ALIBI_MAX_BIAS = 8.0
HGRN_KEY_DIM = 128
HGRN_VAL_DIM = 128
HGRN_HEADS = (D_MIX - ATTN_WIDTH) // HGRN_VAL_DIM
HGRN_WIDTH = HGRN_HEADS * HGRN_VAL_DIM
HGRN_FDIM = HGRN_HEADS * HGRN_KEY_DIM
HGRN_CHUNK = 64
IN_SPLITS = (ATTN_WIDTH, ATTN_WIDTH, ATTN_WIDTH, HGRN_FDIM, HGRN_FDIM, HGRN_FDIM, HGRN_WIDTH, HGRN_WIDTH)
D_IN = 3 * ATTN_WIDTH + 3 * HGRN_FDIM + 2 * HGRN_WIDTH
N_EXPERTS = 16
CAPACITY_FACTOR = 2
D_FF_EXPERT = D_MODEL
NORM_EPS = 1e-6
NEG_INF = -1e30


def rms_norm(x, w):
    xf = x.astype(jnp.float32)
    y = xf * lax.rsqrt(jnp.mean(xf * xf, axis=-1, keepdims=True) + NORM_EPS)
    return (y * w.astype(jnp.float32)).astype(x.dtype)

def alibi_slopes(n_heads):
    return jnp.exp2(-ALIBI_MAX_BIAS * jnp.arange(1, n_heads + 1, dtype=jnp.float32) / n_heads)

def dilated_window_attention(q, k, v, window, dilation, slopes):
    B, S, H, Dh = q.shape
    half = window // (2 * dilation)
    blk = half
    span = dilation * blk
    Sp = -(-S // span) * span
    L = Sp // dilation
    nb = L // blk

    def to_sub(t):
        t = jnp.pad(t, ((0, 0), (0, Sp - S), (0, 0), (0, 0)))
        return t.reshape(B, L, dilation, H, Dh).transpose(0, 2, 1, 3, 4)

    def windows(t):
        t = jnp.pad(t, ((0, 0), (0, 0), (blk, blk), (0, 0), (0, 0))).reshape(B, dilation, nb + 2, blk, H, Dh)
        return jnp.concatenate([t[:, :, :-2], t[:, :, 1:-1], t[:, :, 2:]], axis=3)

    qs = to_sub(q).reshape(B, dilation, nb, blk, H, Dh)
    ks = windows(to_sub(k))
    vs = windows(to_sub(v))

    qi = jnp.arange(blk)
    kj = jnp.arange(3 * blk)
    delta = kj[None, :] - blk - qi[:, None]
    band = jnp.abs(delta) <= half
    l_k = jnp.arange(nb)[:, None] * blk - blk + kj[None, :]
    pos_k = l_k[None] * dilation + jnp.arange(dilation)[:, None, None]
    key_ok = (l_k[None] >= 0) & (pos_k < S)
    mask = band[None, None, None] & key_ok[:, :, None, None, :]
    bias = -slopes[:, None, None] * (dilation * jnp.abs(delta)).astype(jnp.float32)[None]

    s = jnp.einsum('brnqhd,brnkhd->brnhqk', qs, ks)
    s = jnp.where(mask, s + bias, NEG_INF)
    m = jnp.max(s, axis=-1, keepdims=True)
    e = jnp.exp(s - m)
    den = jnp.sum(e, axis=-1)
    num = jnp.einsum('brnhqk,brnkhd->brnqhd', e, vs)

    def back_stat(t):
        t = t.transpose(0, 1, 2, 4, 3).reshape(B, dilation, L, H)
        return t.transpose(0, 2, 1, 3).reshape(B, Sp, H)[:, :S]

    num = num.reshape(B, dilation, L, H, Dh).transpose(0, 2, 1, 3, 4).reshape(B, Sp, H, Dh)[:, :S]
    return back_stat(m[..., 0]), back_stat(den), num

def dilated_attention_mixer(q, k, v, q_norm_w, k_norm_w):
    B, S, _ = q.shape
    shp = (B, S, ATTN_HEADS, ATTN_HEAD_DIM)
    qh = rms_norm(q.reshape(shp), q_norm_w).astype(jnp.float32) * (ATTN_HEAD_DIM ** -0.5)
    kh = rms_norm(k.reshape(shp), k_norm_w).astype(jnp.float32)
    vh = v.reshape(shp).astype(jnp.float32)
    slopes = alibi_slopes(ATTN_HEADS)
    ms, dens, nums = [], [], []
    for window, dilation in DILATED_PATTERNS:
        m, den, num = dilated_window_attention(qh, kh, vh, window, dilation, slopes)
        ms.append(m)
        dens.append(den)
        nums.append(num)
    m_all = jnp.stack(ms)
    scale = jnp.exp(m_all - jnp.max(m_all, axis=0, keepdims=True))
    numer = jnp.sum(scale[..., None] * jnp.stack(nums), axis=0)
    denom = jnp.sum(scale * jnp.stack(dens), axis=0)
    return (numer / denom[..., None]).reshape(B, S, ATTN_WIDTH)

def chunked_gated_recurrence(q, k, v, log_f):
    B, S, H, Dk = q.shape
    Dv = v.shape[-1]
    C = HGRN_CHUNK
    n = S // C

    def to_chunks(t):
        return t.reshape(B, n, C, H, t.shape[-1]).transpose(1, 0, 3, 2, 4)

    incl = jnp.tril(jnp.ones((C, C), dtype=bool))[:, :, None]

    def step(state, inp):
        qb, kb, vb, gb = inp
        b = jnp.cumsum(gb, axis=2)
        o_inter = jnp.einsum('bhck,bhkv->bhcv', qb * jnp.exp(b), state)
        diff = b[:, :, :, None, :] - b[:, :, None, :, :]
        decay = jnp.exp(jnp.where(incl, diff, -jnp.inf))
        a = jnp.einsum('bhtk,bhsk,bhtsk->bhts', qb, kb, decay)
        o_intra = jnp.einsum('bhts,bhsv->bhtv', a, vb)
        b_last = b[:, :, -1:, :]
        k_dec = kb * jnp.exp(b_last - b)
        state = jnp.exp(b_last[:, :, 0, :])[..., None] * state + jnp.einsum('bhsk,bhsv->bhkv', k_dec, vb)
        return state, o_inter + o_intra

    init = jnp.zeros((B, H, Dk, Dv), jnp.float32)
    _, out = lax.scan(step, init, (to_chunks(q), to_chunks(k), to_chunks(v), to_chunks(log_f)))
    return out.transpose(1, 0, 3, 2, 4).reshape(B, S, H, Dv)

def hgrn2_mixer(q, f_fwd, f_bwd, i, g, lb_fwd, lb_bwd, out_norm_w):
    B, S, _ = q.shape

    def heads(t, d):
        return t.reshape(B, S, HGRN_HEADS, d).astype(jnp.float32)

    qh = jax.nn.silu(heads(q, HGRN_KEY_DIM))
    vh = heads(i, HGRN_VAL_DIM)

    def gates(f_raw, lb):
        lb = lb.reshape(HGRN_HEADS, HGRN_KEY_DIM)
        z = heads(f_raw, HGRN_KEY_DIM)
        f = lb + (1.0 - lb) * jax.nn.sigmoid(z)
        return (1.0 - lb) * jax.nn.sigmoid(-z), jnp.log(f)

    k_f, lf_f = gates(f_fwd, lb_fwd)
    k_b, lf_b = gates(f_bwd, lb_bwd)
    o_f = chunked_gated_recurrence(qh, k_f, vh, lf_f)
    flip = lambda t: jnp.flip(t, axis=1)
    o_b = flip(chunked_gated_recurrence(flip(qh), flip(k_b), flip(vh), flip(lf_b)))
    o = rms_norm(o_f + o_b, out_norm_w) * jax.nn.silu(heads(g, HGRN_VAL_DIM))
    return o.reshape(B, S, HGRN_WIDTH)

def expert_choice_moe(h, w_router, w_gate, w_up, w_down):
    B, S, D = h.shape
    cap = max(1, CAPACITY_FACTOR * S // N_EXPERTS)
    logits = jnp.einsum('bsd,de->bse', h, w_router).astype(jnp.float32)
    aff = jax.nn.softmax(logits, axis=-1)
    gate, idx = lax.top_k(aff.transpose(0, 2, 1), cap)
    xin = jax.vmap(lambda hb, ib: hb[ib])(h, idx)
    hid = jax.nn.silu(jnp.einsum('becd,edf->becf', xin, w_gate)) * jnp.einsum('becd,edf->becf', xin, w_up)
    y = jnp.einsum('becf,efd->becd', hid, w_down) * gate[..., None].astype(h.dtype)
    bidx = jnp.arange(B)[:, None, None]
    return jnp.zeros_like(h).at[bidx, idx].add(y)

def second_inputs(seed: int = 0) -> dict:
    key = jax.random.key(seed)
    ks = jax.random.split(key, 16)
    f32 = jnp.float32
    nrm = lambda k, shape, fan_in: jax.random.normal(k, shape, f32) * (fan_in ** -0.5)
    gain = lambda k, shape: 1.0 + 0.02 * jax.random.normal(k, shape, f32)
    return {
        "x": jax.random.normal(ks[0], (BATCH, SEQ, D_MODEL), f32),
        "norm1_w": gain(ks[1], (DEPTH_2, D_MODEL)),
        "w_in": nrm(ks[2], (DEPTH_2, D_MODEL, D_IN), D_MODEL),
        "attn_q_norm_w": gain(ks[3], (DEPTH_2, ATTN_HEAD_DIM)),
        "attn_k_norm_w": gain(ks[4], (DEPTH_2, ATTN_HEAD_DIM)),
        "hgrn_lb_fwd": 1.0 + 0.1 * jax.random.normal(ks[5], (DEPTH_2 + 1, HGRN_FDIM), f32),
        "hgrn_lb_bwd": 1.0 + 0.1 * jax.random.normal(ks[6], (DEPTH_2 + 1, HGRN_FDIM), f32),
        "hgrn_out_norm_w": gain(ks[7], (DEPTH_2, HGRN_VAL_DIM)),
        "w_out": nrm(ks[8], (DEPTH_2, D_MIX, D_MODEL), D_MIX),
        "norm2_w": gain(ks[9], (DEPTH_2, D_MODEL)),
        "w_router": nrm(ks[10], (DEPTH_2, D_MODEL, N_EXPERTS), D_MODEL),
        "w_expert_gate": nrm(ks[11], (DEPTH_2, N_EXPERTS, D_MODEL, D_FF_EXPERT), D_MODEL),
        "w_expert_up": nrm(ks[12], (DEPTH_2, N_EXPERTS, D_MODEL, D_FF_EXPERT), D_MODEL),
        "w_expert_down": nrm(ks[13], (DEPTH_2, N_EXPERTS, D_FF_EXPERT, D_MODEL), D_FF_EXPERT),
    }

def second_block(x, norm1_w, w_in, attn_q_norm_w, attn_k_norm_w, hgrn_lb_fwd, hgrn_lb_bwd,
              hgrn_out_norm_w, w_out, norm2_w, w_router, w_expert_gate, w_expert_up, w_expert_down):
    lb_f_all = jnp.cumsum(jax.nn.softmax(hgrn_lb_fwd.astype(jnp.float32), axis=0), axis=0)
    lb_b_all = jnp.cumsum(jax.nn.softmax(hgrn_lb_bwd.astype(jnp.float32), axis=0), axis=0)
    split_at = np.cumsum(IN_SPLITS)[:-1].tolist()
    for l in range(DEPTH_2):
        h = rms_norm(x, norm1_w[l])
        proj = jnp.einsum('bsd,de->bse', h, w_in[l])
        aq, ak, av, hq, hf_f, hf_b, hi, hg = jnp.split(proj, split_at, axis=-1)
        a_out = dilated_attention_mixer(aq, ak, av, attn_q_norm_w[l], attn_k_norm_w[l])
        b_out = hgrn2_mixer(hq, hf_f, hf_b, hi, hg, lb_f_all[l], lb_b_all[l], hgrn_out_norm_w[l])
        mixed = jnp.concatenate([a_out.astype(x.dtype), b_out.astype(x.dtype)], axis=-1)
        x = x + jnp.einsum('bsm,md->bsd', mixed, w_out[l])
        x = x + expert_choice_moe(rms_norm(x, norm2_w[l]), w_router[l], w_expert_gate[l],
                                  w_expert_up[l], w_expert_down[l])
    return x


def setup_inputs(seed=0):
    out = dict(first_inputs(seed))
    for name, value in second_inputs(seed + 1).items():
        if name != "x":
            out[name + "_2"] = value
    return out


def reference(
    x, positions, ffn1_norm, ffn1_wg, ffn1_wu, ffn1_wd, mix_norm, w_in, mla_q_norm, mla_kv_norm,
    mla_w_uq, mla_w_ukv, nsa_pe_k, nsa_pe_v, nsa_phi_k1, nsa_phi_k2, nsa_phi_v1, nsa_phi_v2,
    diff_lq1, diff_lk1, diff_lq2, diff_lk2, diff_sub_norm, w_out, ffn2_norm, ffn2_wg, ffn2_wu,
    ffn2_wd, final_norm, norm1_w_2, w_in_2, attn_q_norm_w_2, attn_k_norm_w_2, hgrn_lb_fwd_2,
    hgrn_lb_bwd_2, hgrn_out_norm_w_2, w_out_2, norm2_w_2, w_router_2, w_expert_gate_2,
    w_expert_up_2, w_expert_down_2,
):
    x = first_block(
        x, positions, ffn1_norm, ffn1_wg, ffn1_wu, ffn1_wd, mix_norm, w_in, mla_q_norm,
        mla_kv_norm, mla_w_uq, mla_w_ukv, nsa_pe_k, nsa_pe_v, nsa_phi_k1, nsa_phi_k2,
        nsa_phi_v1, nsa_phi_v2, diff_lq1, diff_lk1, diff_lq2, diff_lk2, diff_sub_norm, w_out,
        ffn2_norm, ffn2_wg, ffn2_wu, ffn2_wd, final_norm,
    )
    return second_block(
        x, norm1_w_2, w_in_2, attn_q_norm_w_2, attn_k_norm_w_2, hgrn_lb_fwd_2, hgrn_lb_bwd_2,
        hgrn_out_norm_w_2, w_out_2, norm2_w_2, w_router_2, w_expert_gate_2, w_expert_up_2,
        w_expert_down_2,
    )


_drawn_inputs = setup_inputs


def setup_inputs(seed=0):
    import zlib

    import numpy as np

    out = dict(_drawn_inputs(seed))
    spreads = {}
    factors = {'ffn1_norm': 3.199,
     'mla_q_norm': 8.0,
     'mla_kv_norm': 5.676,
     'nsa_pe_k': 7.491,
     'diff_lk2': 2.71,
     'diff_sub_norm': 3.958,
     'ffn2_norm': 3.801,
     'norm1_w_2': 3.356,
     'attn_q_norm_w_2': 7.552,
     'attn_k_norm_w_2': 8.0,
     'hgrn_lb_fwd_2': 7.317,
     'hgrn_lb_bwd_2': 8.0,
     'hgrn_out_norm_w_2': 5.171,
     'norm2_w_2': 4.223}
    for name, (base, spread) in spreads.items():
        noise = np.random.default_rng([zlib.crc32(name.encode()), seed]).standard_normal(out[name].shape)
        drawn = base * np.exp(spread * noise) if base else spread * noise
        out[name] = jnp.asarray(drawn.astype(out[name].dtype))
    for name, factor in factors.items():
        out[name] = (out[name] * factor).astype(out[name].dtype)
    return out
```

```python
import math

import numpy as np

import concourse.bass as bass
from concourse import mybir

F32 = mybir.dt.float32
I32 = mybir.dt.int32
ALU = mybir.AluOpType
ACT = mybir.ActivationFunctionType
AX = mybir.AxisListType

P = 128
D = 1024
T = 512
LAYERS = 2
KC = D // P
NT = T // P
D_FF = 2816
FFN_ITEMS = D_FF // P
EPS = 1e-6
THETA = 500000.0
NEG = -1e30

A_HEADS, A_QR, A_NOPE, A_ROPE = 6, 192, 64, 32
A_DK = A_NOPE + A_ROPE
B_GROUPS, B_HPG, B_DH = 2, 3, 64
B_HEADS = B_GROUPS * B_HPG
B_ROT = B_DH // 4
CMP_LEN, CMP_STRIDE = 32, 16
N_CMP = (T - CMP_LEN) // CMP_STRIDE + 1
C_HEADS, C_DH = 4, 32
C_ROT = C_DH // 4
A_COLS = A_QR + 128 + A_ROPE
B_COLS = B_HEADS * B_DH + 6 * B_GROUPS * B_DH + 3 * B_HEADS

E_HEADS, E_DH = 8, 64
H_HEADS, H_DK = 4, 128
N_EXPERTS = 16
CAP = 2 * T // N_EXPERTS
MOE_ITEMS = D // P
PATTERNS = ((128, 1), (512, 4), (2048, 16))
LEVELS = (64, 32, 16, 8, 4, 2, 1)

SLOTS = 4
ITEM = 3 * D
WCOLS = ITEM // KC
MIX_ITEMS = 13
SECOND_ITEMS = 14
FFN_TRIPS = FFN_ITEMS // SLOTS - 1

ROUND = 12582912.0
TWO_PI = (6.28125, 0.0019350051879882812, 3.0199159819e-07)
SIN_MAX = 3.1415925

COL_FFN1, COL_MIX, COL_FFN2 = 0, 16, 32
COL_FINAL, COL_N1, COL_N2 = 48, 56, 64
COL_MLAQ, COL_MLAKV = 72, 76
COL_DQ, COL_DK = 78, 79
COL_LB = 80
COL_PE = 96
COL_ROUTER = COL_PE + LAYERS * 2 * CMP_LEN
N_COLS = COL_ROUTER + KC * N_EXPERTS
ROW_LAM = 0
ROW_SUB = LAYERS * 4 * C_DH
ROW_OUT = ROW_SUB + LAYERS * 2 * C_DH
N_ROWS = ROW_OUT + H_DK
C_ID, C_BLK, C_TRI = 0, 128, 256
C_RA, C_RB, C_RC = 384, 512, 640
C_CMP = 768
C_ROWM = C_CMP + NT * N_CMP
C_INV = C_ROWM + 1
C_IOTA = C_INV + 3
N_CONST = C_IOTA + CAP
C2_DIST, C2_MULT = 0, 896
C2_LVL = 1792
N_CONST2 = C2_LVL + 2 * len(LEVELS) * 64


def constants():
    c = np.zeros((P, N_CONST), np.float32)
    c[:, C_ID:C_ID + P] = np.eye(P)
    for b in range(2):
        c[64 * b:64 * b + 64, C_BLK + 64 * b:C_BLK + 64 * b + 64] = 1
    p = np.arange(P)
    c[:, C_TRI:C_TRI + P] = np.where(p[None, :] <= p[:, None], 0, NEG)
    for at, period, first, half in ((C_RA, P, 64, 16), (C_RB, 64, 0, 8), (C_RC, 32, 0, 4)):
        for b in range(0, P, period):
            for i in range(half):
                c[b + first + half + i, at + b + first + i] = -1
                c[b + first + i, at + b + first + half + i] = 1
    for i in range(NT):
        last = np.arange(N_CMP) * CMP_STRIDE + CMP_LEN - 1
        c[:, C_CMP + i * N_CMP:C_CMP + (i + 1) * N_CMP] = np.where(last[None] <= (i * P + p)[:, None], 0, NEG)
    c[:, C_ROWM] = p >= CMP_LEN - 1
    for n, (period, first, rot) in enumerate(((P, 64, A_ROPE), (64, 0, B_ROT), (32, 0, C_ROT))):
        inv = (1.0 / (np.float32(THETA) ** (np.arange(0, rot, 2, dtype=np.float32) / np.float32(rot)))).astype(np.float32)
        for b in range(0, P, period):
            c[b + first:b + first + rot, C_INV + n] = np.concatenate([inv, inv])
    c[:, C_IOTA:C_IOTA + CAP] = np.arange(CAP)
    d = np.zeros((P, N_CONST2), np.float32)
    dist = np.abs(p[:, None] - np.arange(896)[None] + 384)
    mult = np.zeros(dist.shape)
    for window, dil in PATTERNS:
        mult += (dist % dil == 0) & (dist <= window // 2)
    d[:, C2_DIST:C2_DIST + 896] = dist
    d[:, C2_MULT:C2_MULT + 896] = np.where(mult > 0, np.log(np.maximum(mult, 1)), NEG)
    for back in range(2):
        for n, m in enumerate(LEVELS):
            blk = np.arange(64) // m
            half = (p % (2 * m) >= m) if back else (p % (2 * m) < m)
            at = C2_LVL + (back * len(LEVELS) + n) * 64
            d[:, at:at + 64] = (p[:, None] // (2 * m) == blk[None]) & half[:, None]
    return c, d


class Count:

    def __init__(self):
        self.at, self.own, self.reg, self.rate, self.mark = {}, {}, None, {}, {}

    def value(self, sem, v):
        if self.reg is None:
            return max(v, 0)
        assert v > 0
        return self.reg * self.rate[sem.name] + v

    def next(self, sem, n=1, lag=0):
        self.at[sem.name] = self.at.get(sem.name, 0) + n
        return self.value(sem, self.at[sem.name] - lag)

    def skip(self, sem, n=1):
        self.at[sem.name] = self.at.get(sem.name, 0) + n

    def one(self, sem, n=1):
        self.own[sem.name] = self.own.get(sem.name, 0) + n
        return n

    def made(self, sem, lag=0):
        return self.value(sem, self.own.get(sem.name, 0) - lag)

    def loop(self, reg, rate):
        self.reg, self.rate = reg, {s.name: n for s, n in rate.items()}
        self.mark = (dict(self.at), dict(self.own))

    def looped(self, trips):
        for now, then in zip((self.at, self.own), self.mark):
            for k in now:
                d = now[k] - then.get(k, 0)
                assert d == 0 or d == self.rate[k], (k, d)
                now[k] += d * (trips - 1)
        self.reg = None


def program(nc, ffn_w, mix_w, second_w, moe_w, x_in, pos_in, cols_in, rows_in, const_in, const2_in, out):
    sb = lambda name, n, dt=F32: nc.alloc_sbuf_tensor(name, [P, n], dt).ap()
    x = sb("x", KC * T).rearrange("p (k t) -> p k t", k=KC)
    h = sb("h", KC * T).rearrange("p (k t) -> p k t", k=KC)
    ring = sb("ring", SLOTS * ITEM).rearrange("p (s n) -> p s n", s=SLOTS)
    mix = sb("mix", 18432)
    const = sb("const", N_CONST)
    table = sb("table", 3072)
    cols = sb("cols", N_COLS)
    rows = sb("rows", N_ROWS)
    prob = sb("prob", 2 * T).rearrange("p (b n) -> p b n", b=2)
    probT = sb("probT", 2 * T).rearrange("p (b n) -> p b n", b=2)
    sq = sb("sq", 2 * T).rearrange("p (b n) -> p b n", b=2)
    rms = sb("rms", T)
    small = sb("small", 384)
    ones = sb("ones", P)

    bank = [nc.alloc_psum_tensor(f"bank{i}", [P, T], F32).ap() for i in range(8)]

    def new(*names):
        made = [nc.alloc_semaphore(n) for n in names]
        return made if len(names) > 1 else made[0]

    consts_in, second_in, stored = new("consts_in", "second_in", "stored")
    w_in = [new(f"w_in{s}") for s in range(SLOTS)]
    met = {e: new(f"met_{e}") for e in ("pe", "act", "dve", "pool")}
    step_dve, step_act, for_act, for_dve = new("step_dve", "step_act", "for_act", "for_dve")
    sq_ready, sq_used, ms_ready, rms_ready, normed = new("sq_ready", "sq_used", "ms_ready", "rms_ready", "normed")
    up_ready, silu_ready, gu_ready, down_ready, down_used = new("up_ready", "silu_ready", "gu_ready", "down_ready", "down_used")
    y_ready, y_copied = new("y_ready", "y_copied")
    prod_ready, taken_act, taken_dve = new("prod_ready", "taken_act", "taken_dve")
    rot_ready, cos_done, rope_done = new("rot_ready", "cos_done", "rope_done")
    fold_ready, fold_copied = new("fold_ready", "fold_copied")
    cmp_ready, cmp_bias, cmp_hid = new("cmp_ready", "cmp_bias", "cmp_hid")
    scores_ready, max_ready, probs_ready = new("scores_ready", "max_ready", "probs_ready")
    pT_ready, pT_copied, pv_ready, o_done = new("pT_ready", "pT_copied", "pv_ready", "o_done")
    scan_ready, fac_ready, qk_ready, off_ready, off_copied = new("scan_ready", "fac_ready", "qk_ready", "off_ready", "off_copied")
    diff_ready, decay_ready, lvl_ready, lvl_mm, lvl_put = new("diff_ready", "decay_ready", "lvl_ready", "lvl_mm", "lvl_put")
    keys_ready, diag_mm, diag_put, head_mm, head_out = new("keys_ready", "diag_mm", "diag_put", "head_mm", "head_out")
    logit_ready, logit_max, logit_exp, aff_ready = new("logit_ready", "logit_max", "logit_exp", "aff_ready")
    affT_ready, slotT_ready, slot_ready = new("affT_ready", "slotT_ready", "slot_ready")

    def view(at, n, **k):
        v = mix[:, at:at + n]
        return v.rearrange("p (a n) -> p a n", **k) if k else v

    def chunks(at, n):
        return view(at, n * T, a=n)

    cst = lambda at, n=1, r=slice(0, P): const[r, at:at + n]
    ident = cst(C_ID, P)
    col = lambda at, r=slice(0, P): cols[r, at:at + 1]

    QA, KA = chunks(0, 6), chunks(3072, 6)
    VA = view(6144, NT * 384, a=NT)
    CQ, CKV, KPE = chunks(7680, 2), chunks(8704, 1), chunks(9216, 1)
    QB, KB = chunks(9728, 3), chunks(11264, 4)
    VB = view(13312, NT * 256, a=NT)
    GATE = view(14336, NT * 18, a=NT)
    KCMP, VCMP, HID = view(14408, N_CMP), view(14440, 2 * 64, a=2), view(14568, 2 * N_CMP, a=2)
    QC, KCc = chunks(14640, 2), chunks(15664, 2)
    VC = view(16688, NT * 256, a=NT)
    assert 16688 + 1024 <= 18432
    LAM, CB = small[:, 0:4], small[:, 4:8]
    O = h.rearrange("p k t -> p (k t)").rearrange("p (i n) -> p i n", i=NT)
    OT = chunks(0, KC)
    SILU, GU = chunks(0, 2), chunks(1024, 2)
    NM, DEN, RDEN, WGT = small[:, 8:12], small[:, 12:16], small[:, 16:20], small[:, 20:24]
    SUBSQ = view(4096, 2048)
    MS16 = small[:, 64:80]
    SLOTT = sq[:, 0]
    ANGLE = [[mix[:, 2560 + 1024 * n + 512 * q:3072 + 1024 * n + 512 * q] for q in range(2)] for n in range(3)]
    COS = [table[:, 1024 * n:1024 * n + 512] for n in range(3)]
    SIN = [table[:, 1024 * n + 512:1024 * n + 1024] for n in range(3)]

    QD, KD = chunks(0, 4), chunks(2048, 4)
    VD = view(4096, NT * 512, a=NT)
    HQ, ZF, ZB = chunks(6144, 4), chunks(8192, 4), chunks(10240, 4)
    VI, GG = view(12288, NT * 512, a=NT), view(14336, NT * 512, a=NT)
    Z = [ZF, ZB]
    K2 = [QD, KD]
    MM = view(4096, 2 * T, a=2)
    EE = view(5120, 2 * T, a=2)
    AT = view(16384, T, a=NT)
    QT = view(16896, T, a=NT)
    KT = view(17408, T, a=NT)
    KSUM = view(17920, T, a=NT)
    BC = prob.rearrange("p b n -> p (b n)")[:, 0:516].rearrange("p (i n) -> p i n", i=NT)
    DD = probT
    QX = sq.rearrange("p b n -> p (b n)")[:, 0:384].rearrange("p (i n) -> p i n", i=3)
    AO = [table[:, 0:768].rearrange("p (i n) -> p i n", i=6), table[:, 768:1536].rearrange("p (i n) -> p i n", i=6)]
    ET, LB, OMLB, LBT = small[:, 24:28], small[:, 32:40], small[:, 40:48], small[:, 48:56]
    XIN = view(0, 8192, a=KC)
    HTOK = view(8192, 4096, a=NT)
    GT = view(12288, 4096, a=8)
    SEL = h.rearrange("p k t -> p (k t)").rearrange("p (i n) -> p i n", i=NT)
    AFF = small[:, 128:192].rearrange("p (i e) -> p i e", i=NT)
    SLOT = small[:, 192:256].rearrange("p (i e) -> p i e", i=NT)
    RW = cols[:, COL_ROUTER:COL_ROUTER + KC * N_EXPERTS].rearrange("p (k e) -> p k e", k=KC)
    MG = sq
    MGU = probT
    YS = prob.rearrange("p b n -> p (b n)")

    def job(terms, p0, rows_, n, dst, scale=None, need=(), free=0, add=False):
        return dict(terms=terms, p0=p0, rows=rows_, n=n, dst=dst, scale=scale, need=need, free=free, add=add)

    def wslot(item, width):
        return ring[:, item % SLOTS, 0:KC * width].rearrange("p (k n) -> p k n", k=KC)

    def feat(item, width, c0, m, dst, p0=0, scale=None):
        w = wslot(item, width)
        return job([(w[:, k, c0:c0 + m], h[:, k, :]) for k in range(KC)], p0, m, T, dst, scale)

    def toks(item, width, c0, n, dsts):
        w = wslot(item, width)
        return [job([(h[:, k, i * P:(i + 1) * P], w[:, k, c0:c0 + n]) for k in range(KC)], 0, P, n, dsts[i]) for i in range(NT)]

    def with_items(jobs, item):
        jobs[0]["need"] = (item,)
        jobs[-1]["free"] = 1
        return jobs

    def project_one(b):
        r = []
        r += with_items([feat(b, 352, 0, 128, CQ[:, 0]), feat(b, 352, 128, 64, CQ[0:64, 1]),
                         feat(b, 352, 192, 128, CKV[:, 0]), feat(b, 352, 320, 32, KPE[64:96, 0], p0=64)], b)
        r += with_items([feat(b + 1, 384, 128 * j, 128, QB[:, j], scale=B_DH ** -0.5) for j in range(3)], b + 1)
        r += with_items([feat(b + 2, 384, 128 * j, 128, KB[:, j]) for j in range(3)], b + 2)
        r += with_items([feat(b + 3, 384, 0, 128, KB[:, 3])] + toks(b + 3, 384, 128, 256, [VB[:, i] for i in range(NT)]), b + 3)
        r += with_items([feat(b + 4, 274, 128 * j, 128, QC[:, j], scale=C_DH ** -0.5) for j in range(2)]
                        + toks(b + 4, 274, 256, 18, [GATE[:, i] for i in range(NT)]), b + 4)
        r += with_items([feat(b + 5, 256, 128 * j, 128, KCc[:, j]) for j in range(2)], b + 5)
        r += with_items(toks(b + 6, 256, 0, 256, [VC[:, i] for i in range(NT)]), b + 6)
        return r

    def project_mla(b):
        w = ring[:, (b + 7) % SLOTS, :]
        uq = w[:, 0:1152].rearrange("p (k n) -> p k n", k=2)
        ukv = w[:, 1152:1920].rearrange("p (m n) -> p m n", m=A_HEADS)
        r = []
        for m in range(A_HEADS):
            r.append(job([(uq[:, 0, 96 * m:96 * m + 96], CQ[:, 0]), (uq[0:64, 1, 96 * m:96 * m + 96], CQ[0:64, 1])],
                         0, 96, T, QA[0:96, m], scale=A_DK ** -0.5))
        for m in range(A_HEADS):
            r.append(job([(ukv[:, m, 0:64], CKV[:, 0])], 0, 64, T, KA[0:64, m]))
        for i in range(NT):
            r.append(job([(CKV[:, 0, i * P:(i + 1) * P], ukv[:, :, 64:128])], 0, P, 384, VA[:, i]))
        return with_items(r, b + 7)

    def project_out(b):
        r = []
        for n, width in enumerate((384, 384, 256)):
            w = wslot(b + n, width)
            r += with_items([job([(w[:, k, c:c + P], OT[:, k, :]) for k in range(KC)], 0, P, T, x[:, 3 * n + c // P], add=True)
                             for c in range(0, width, P)], b + n)
        return r

    def project_second(b):
        dst = [QD, KD, None, HQ, ZF, ZB, None, None]
        tok = {2: VD, 6: VI, 7: GG}
        r = []
        for n in range(11):
            jobs = []
            for c in range(384 * n, min(384 * n + 384, 4096), P):
                s, o = divmod(c, 512)
                width = 384 if n < 10 else 256
                if dst[s] is not None:
                    jobs.append(feat(b + n, width, c - 384 * n, P, dst[s][:, o // P]))
                else:
                    jobs += toks(b + n, width, c - 384 * n, P, [tok[s][:, i, o:o + P] for i in range(NT)])
            r += with_items(jobs, b + n)
        return r

    def causal(q, k, v, i, out_, mode, gate=None):
        n = (i + 1) * P
        return dict(q=q[:, i * P:(i + 1) * P], k=k[:, 0:n], n=n, mask=(cst(C_TRI, P), i * P), v=[v(j) for j in range(i + 1)],
                    rows=P, out=out_, mode=mode, gate=gate, i=i, bias=None)

    def mixer_tiles():
        r = []
        for m in range(A_HEADS):
            for i in range(NT):
                r.append(causal(QA[0:96, m], KA[0:96, m], lambda j, m=m: VA[:, j, 64 * m:64 * m + 64], i,
                                O[:, i, 64 * m:64 * m + 64], "set"))
        for g in range(B_GROUPS):
            s = slice(64 * g, 64 * g + 64)
            for j in range(B_HPG):
                m = g * B_HPG + j
                c0 = 384 + 64 * m
                for i in range(NT):
                    r.append(dict(q=QB[s, j, i * P:(i + 1) * P], k=KCMP[s, :], n=N_CMP, mask=(cst(C_CMP + i * N_CMP, N_CMP), 0),
                                  v=[VCMP[0:N_CMP, g, :]], rows=N_CMP, out=O[:, i, c0:c0 + 64], mode="gated",
                                  gate=GATE[:, i, 3 * m:3 * m + 1], i=i, bias=None))
                for w in (1, 2):
                    for i in range(NT):
                        r.append(causal(QB[s, j], KB[s, 1 + w], lambda t, w=w: VB[:, t, 128 * (w - 1) + 64 * g:128 * (w - 1) + 64 * g + 64],
                                        i, O[:, i, c0:c0 + 64], "add", GATE[:, i, 3 * m + w:3 * m + w + 1]))
        for m in range(C_HEADS):
            for comp in range(2):
                r0 = 64 * (m % 2) + 32 * comp
                s = slice(r0, r0 + 32)
                for i in range(NT):
                    r.append(causal(QC[s, m // 2], KCc[s, m // 2], lambda j, m=m: VC[:, j, 64 * m:64 * m + 64], i,
                                    O[:, i, 768 + 64 * m:832 + 64 * m], "add" if comp else "set", LAM[:, 3:4] if comp else None))
        return r

    def dilated_tiles():
        r = []
        for m in range(E_HEADS):
            s = slice(64 * (m % 2), 64 * (m % 2) + 64)
            for i in range(NT):
                r.append(dict(q=QD[s, m // 2, i * P:(i + 1) * P], k=KD[s, m // 2], n=T, mask=None,
                              v=[VD[:, j, 64 * m:64 * m + 64] for j in range(NT)], rows=P,
                              out=O[:, i, 64 * m:64 * m + 64], mode="set", gate=None, i=i, bias=m))
        return r

    HB = view(16384, 2 * 896, a=2)
    SB = sq

    def norm_x(at):
        return [dict(src=[x[:, k] for k in range(KC)], dst=[h[:, k] for k in range(KC)], gain=[col(at + k) for k in range(KC)],
                     rows=[P] * KC, ones=ones, width=D)]

    def norm_final():
        return [dict(norm_x(COL_FINAL)[0], dst=[x[:, k] for k in range(KC)])]

    def norm_mla(l):
        a = COL_MLAQ + 2 * l
        return [dict(src=[CQ[:, 0], CQ[0:64, 1]], dst=[CQ[:, 0], CQ[0:64, 1]], gain=[col(a), col(a + 1, slice(0, 64))],
                     rows=[P, 64], ones=ones, width=A_QR),
                dict(src=[CKV[:, 0]], dst=[CKV[:, 0]], gain=[col(COL_MLAKV + l)], rows=[P], ones=ones, width=128)]

    def norm_heads():
        return [dict(src=[X[:, j]], dst=[X[:, j]], gain=[col(g)], rows=[P], ones=cst(C_BLK, P), width=64)
                for X, g in ((QD, COL_DQ), (KD, COL_DK)) for j in range(4)]

    def ropes_first():
        r = [(QB[:, j], cst(C_RB, P), COS[1], SIN[1]) for j in range(3)]
        r += [(KB[:, j], cst(C_RB, P), COS[1], SIN[1]) for j in (0, 2, 3)]
        r += [(X[:, j], cst(C_RC, P), COS[2], SIN[2]) for X in (QC, KCc) for j in range(2)]
        s = slice(64, 96)
        r += [(KPE[s, 0], const[s, C_RA + 64:C_RA + 96], COS[0][s, :], SIN[0][s, :])]
        return r

    def ropes_mla():
        s = slice(0, 96)
        return [(QA[s, m], const[s, C_RA:C_RA + 96], COS[0][s, :], SIN[0][s, :]) for m in range(A_HEADS)]

    def meet(e, c, own):
        e.drain().then_inc(met[own], c.one(met[own]))
        for s in met.values():
            e.wait_ge(s, c.own[met[own].name])


    PAIRS = [[(1, 0), (2, 1), (3, 2), (2, 0), (3, 1), (3, 0)], [(0, 1), (1, 2), (2, 3), (0, 2), (1, 3), (0, 3)]]

    def cum(d):
        o = 1 - d
        return BC[:, :, o:o + P]

    def halves(buf, m):
        v = buf.rearrange("p (j w) -> p j w", w=2 * m)
        return v[:, :, 0:m], v[:, :, m:2 * m]

    def gathered():
        return [job([(HTOK[:, i, P * q:P * q + P], SEL[:, i, 512 * s:512 * s + 512]) for i in range(NT)],
                    0, P, 512, XIN[:, q, 512 * s:512 * s + 512]) for q in range(KC) for s in range(2)]

    block_cm = nc.Block()
    block = block_cm.__enter__()
    per_layer = 2 * FFN_ITEMS + MIX_ITEMS
    base_second = LAYERS * per_layer
    base_moe = base_second + SECOND_ITEMS
    assert base_moe % SLOTS == 0

    released, counts = [], {}

    def release(sem_, n):
        counts[sem_.name] = counts.get(sem_.name, 0) + n
        return sem_, counts[sem_.name]

    def release_jobs(jobs):
        for j in jobs:
            r = release(prod_ready, 1)
            if j["free"]:
                released.append(r)

    for l in range(LAYERS):
        released += [release(down_ready, KC) for n in range(FFN_ITEMS)]
        release_jobs(project_one(0))
        release_jobs(project_mla(0))
        released += [release(cmp_ready, 2 * B_GROUPS + 1)] * 2
        release_jobs(project_out(0))
        released += [release(down_ready, KC) for n in range(FFN_ITEMS)]
    release_jobs(project_second(0))
    release_jobs(project_out(0))
    assert len(released) == base_moe
    released += [release(y_ready, 1) for n in range(N_EXPERTS * MOE_ITEMS)]

    @block.sync
    def _(sp):
        for dst, src in ((cols, cols_in), (rows, rows_in), (const, const_in)):
            sp.dma_start(dst, src).then_inc(consts_in, 16)
        sp.dma_start(x, x_in).then_inc(consts_in, 16)
        sp.dma_start(mix[:, 0:T].bitcast(I32), pos_in).then_inc(consts_in, 16)

        def load(n, src):
            if n >= SLOTS:
                sp.wait_ge(*released[n - SLOTS])
            sp.dma_start(ring[:, n % SLOTS, :], src).then_inc(w_in[n % SLOTS], 16)

        def load_loop(n, src, trips):
            with sp.Fori(1, 1 + trips) as i:
                for r in range(SLOTS):
                    done, v = released[n + r]
                    each = released[n + r + 1][1] - v
                    sp.wait_ge(done, (i - 1) * (SLOTS * each) + v)
                    sp.dma_start(ring[:, (n + r) % SLOTS, :],
                                 src[bass.ds(i * SLOTS + r, 1)].rearrange("a p n -> (a p) n")).then_inc(w_in[(n + r) % SLOTS], 16)

        def load_ffn(n, src):
            for r in range(SLOTS):
                load(n + r, src[r])
            load_loop(n, src, FFN_TRIPS)
            for r in range(SLOTS * (FFN_TRIPS + 1), FFN_ITEMS):
                load(n + r, src[r])

        for l in range(LAYERS):
            b = l * per_layer
            load_ffn(b, ffn_w[2 * l])
            for r in range(MIX_ITEMS):
                load(b + FFN_ITEMS + r, mix_w[l, r])
            load_ffn(b + FFN_ITEMS + MIX_ITEMS, ffn_w[2 * l + 1])
        for r in range(SECOND_ITEMS):
            load(base_second + r, second_w[r])
        for r in range(SLOTS):
            load(base_moe + r, moe_w[r])
        load_loop(base_moe, moe_w, N_EXPERTS * MOE_ITEMS // SLOTS - 1)
        sp.wait_ge(down_used, LAYERS * 2 * FFN_ITEMS * KC + (N_EXPERTS // 2) * KC)
        sp.dma_start(out, x).then_inc(stored, 16)
        sp.wait_ge(stored, 16)

    @block.gpsimd
    def _(pool):
        c = Count()
        pool.memset(ones, 1.0)
        pool.wait_ge(consts_in, 80)
        meet(pool, c, "pool")
        meet(pool, c, "pool")

        def ropes(list_):
            for X, R, cos, sin in list_:
                pool.wait_ge(cos_done, c.made(cos_done))
                pool.wait_ge(rot_ready, c.next(rot_ready))
                pool.tensor_tensor(X, X, cos, ALU.mult).then_inc(cos_done, c.one(cos_done))

        for l in range(LAYERS):
            for stage in ("norm", "FFN", "norm", "projections"):
                meet(pool, c, "pool")
            ropes(ropes_first())
            meet(pool, c, "pool")
            for m in range(A_HEADS):
                pool.tensor_copy(KA[64:96, m], KPE[64:96, 0])
            meet(pool, c, "pool")
            ropes(ropes_mla())
            for stage in ("MLA rotations", "attention", "sub-norm", "transposes", "output projection", "norm", "FFN"):
                meet(pool, c, "pool")
        pool.dma_start(table[:, 0:N_CONST2], const2_in).then_inc(second_in, 16)
        pool.wait_ge(second_in, 16)
        for stage in ("final norm", "norm", "projections", "head norms", "attention", "gates"):
            meet(pool, c, "pool")
        for m in range(H_HEADS):
            pool.wait_ge(head_mm, c.next(head_mm, 1, lag=1))
            pool.memset(AT, 0.0).then_inc(keys_ready, 1)
            pool.tensor_tensor(KSUM, K2[0][:, m].rearrange("p (i n) -> p i n", i=NT),
                               K2[1][:, m].rearrange("p (i n) -> p i n", i=NT), ALU.add).then_inc(keys_ready, 1)
        for stage in ("HGRN2", "out norm", "transposes", "output projection", "norm", "router", "selection",
                      "gather", "scatter matrices", "transposes", "experts"):
            meet(pool, c, "pool")

    @block.scalar
    def _(act):
        c = Count()
        meet(act, c, "act")

        def norm(groups):
            for g in groups:
                for s, r in zip(g["src"], g["rows"]):
                    b = c.own.get(sq_ready.name, 0) % 2
                    act.wait_ge(sq_used, c.next(sq_used, 1, lag=2))
                    act.activation(sq[0:r, b], s, ACT.Square).then_inc(sq_ready, c.one(sq_ready))
                act.wait_ge(ms_ready, c.next(ms_ready))
                act.activation(rms, rms, ACT.Sqrt).then_inc(rms_ready, 1)

        def gemm(jobs):
            for n, j in enumerate(jobs):
                if n % 2:
                    c.skip(prod_ready)
                    continue
                act.wait_ge(prod_ready, c.next(prod_ready))
                act.activation(j["dst"], bank[n % 4][j["p0"]:j["p0"] + j["rows"], 0:j["n"]], ACT.Copy,
                               scale=j["scale"] or 1.0).then_inc(taken_act, 1)

        def transposed(dst):
            for q in range(KC):
                act.wait_ge(fold_ready, c.next(fold_ready))
                act.activation(dst[q], bank[4 + q % 2], ACT.Copy).then_inc(fold_copied, 1)

        def silu(n):
            act.wait_ge(gu_ready, c.next(gu_ready, 1, lag=2))
            act.wait_ge(up_ready, c.next(up_ready))
            act.activation(SILU[:, n % 2], bank[n % 2], ACT.Silu).then_inc(silu_ready, 1)

        def ffn():
            for n in range(SLOTS):
                silu(n)
            with act.Fori(0, FFN_TRIPS) as i:
                c.loop(i, {gu_ready: SLOTS, up_ready: SLOTS})
                for r in range(SLOTS):
                    silu(r)
                c.looped(FFN_TRIPS)
            for n in range(SLOTS * (FFN_TRIPS + 1), FFN_ITEMS):
                silu(n)

        def attention(tiles):
            for a, t in enumerate(tiles):
                act.wait_ge(max_ready, c.next(max_ready))
                act.wait_ge(pT_ready, c.next(pT_ready, 1, lag=2))
                src = SB[:, a % 2, 0:t["n"]] if t["bias"] is not None else bank[a % 2][:, 0:t["n"]]
                act.activation(prob[:, a % 2, 0:t["n"]], src, ACT.Exp, bias=NM[:, a % 4:a % 4 + 1],
                               accum_out=DEN[:, a % 4:a % 4 + 1]).then_inc(probs_ready, 1)

        def root(v):
            act.wait_ge(for_act, c.next(for_act))
            act.activation(v, v, ACT.Sqrt).then_inc(for_dve, 1)

        for n in range(3):
            for q in range(2):
                act.wait_ge(for_act, c.next(for_act))
                act.activation((SIN, COS)[q][n], ANGLE[n][q], ACT.Sin)
        meet(act, c, "act")

        for l in range(LAYERS):
            norm(norm_x(COL_FFN1 + 8 * l))
            meet(act, c, "act")
            ffn()
            meet(act, c, "act")
            norm(norm_x(COL_MIX + 8 * l))
            meet(act, c, "act")
            gemm(project_one(0))
            meet(act, c, "act")
            norm(norm_mla(l))
            act.wait_ge(for_act, c.next(for_act))
            act.activation(LAM[:, 0:2], LAM[:, 0:2], ACT.Exp).then_inc(for_dve, 1)
            act.activation(GATE, GATE, ACT.Sigmoid).then_inc(for_dve, 1)
            meet(act, c, "act")
            gemm(project_mla(0))
            meet(act, c, "act")
            for part in range(2):
                for g in range(B_GROUPS):
                    s = slice(64 * g, 64 * g + 64)
                    act.wait_ge(cmp_bias, c.next(cmp_bias))
                    act.activation(HID[s, part], bank[4 + 2 * part + g][s, 0:N_CMP], ACT.Silu,
                                   bias=CB[s, part:part + 1]).then_inc(cmp_hid, 1)
            meet(act, c, "act")
            attention(mixer_tiles())
            meet(act, c, "act")
            root(MS16)
            meet(act, c, "act")
            transposed([OT[:, q] for q in range(KC)])
            meet(act, c, "act")
            c.skip(prod_ready, KC)
            meet(act, c, "act")
            norm(norm_x(COL_FFN2 + 8 * l))
            meet(act, c, "act")
            ffn()
            meet(act, c, "act")
        norm(norm_final())
        meet(act, c, "act")
        norm(norm_x(COL_N1))
        meet(act, c, "act")
        gemm(project_second(0))
        meet(act, c, "act")
        norm(norm_heads())
        meet(act, c, "act")
        attention(dilated_tiles())
        meet(act, c, "act")

        act.wait_ge(for_act, c.next(for_act))
        act.activation(LBT, LBT, ACT.Exp).then_inc(for_dve, 1)
        for d in range(2):
            act.activation(K2[d], Z[d], ACT.Sigmoid, scale=-1.0).then_inc(step_act, c.one(step_act))
        act.wait_ge(step_act, c.made(step_act))
        for d in range(2):
            act.activation(Z[d], Z[d], ACT.Sigmoid).then_inc(for_dve, 1)
        act.activation(HQ, HQ, ACT.Silu)
        act.activation(GG, GG, ACT.Silu)
        for d in range(2):
            act.wait_ge(for_act, c.next(for_act))
            act.activation(Z[d], Z[d], ACT.Ln)
        meet(act, c, "act")

        for m in range(H_HEADS):
            for d in range(2):
                act.wait_ge(lvl_ready, c.next(lvl_ready, 0))
                act.wait_ge(scan_ready, c.next(scan_ready))
                act.activation(EE[:, 0].rearrange("p (i n) -> p i n", i=NT), cum(d), ACT.Exp)
                act.activation(ET, BC[:, :, P], ACT.Exp)
                act.wait_ge(diff_ready, c.next(diff_ready))
                act.activation(EE[:, 1], DD[:, 0], ACT.Exp).then_inc(fac_ready, 1)
                act.wait_ge(off_ready, c.next(off_ready))
                if m and d == 0:
                    act.wait_ge(head_mm, c.next(head_mm, 0))
                act.activation(AO[d][:, 0:3].rearrange("p i n -> p (i n)"), bank[0][:, 0:384], ACT.Copy)
                act.activation(AO[d][:, 3:6].rearrange("p i n -> p (i n)"), bank[1][:, 0:384], ACT.Copy).then_inc(off_copied, 1)
                for n, w in enumerate(LEVELS):
                    act.wait_ge(diff_ready, c.next(diff_ready))
                    act.wait_ge(lvl_ready, c.next(lvl_ready, 1, lag=2))
                    for src, dst, sign in zip(halves(DD[:, n % 2], w), halves(EE[:, n % 2], w), (-1.0, 1.0)):
                        last = act.activation(dst, src, ACT.Exp, scale=sign)
                    last.then_inc(decay_ready, 1)
            act.wait_ge(head_mm, c.next(head_mm))
            act.activation(O[:, :, 512 + P * m:512 + P * m + P], bank[7].rearrange("p (i n) -> p i n", i=NT),
                           ACT.Copy).then_inc(head_out, 1)
        meet(act, c, "act")
        root(MS16)
        meet(act, c, "act")
        transposed([OT[:, q] for q in range(KC)])
        meet(act, c, "act")
        meet(act, c, "act")
        norm(norm_x(COL_N2))
        meet(act, c, "act")
        act.wait_ge(logit_max, c.next(logit_max))
        for i in range(NT):
            act.activation(AFF[:, i], bank[0][:, 16 * i:16 * i + 16], ACT.Exp, bias=NM[:, i:i + 1],
                           accum_out=DEN[:, i:i + 1]).then_inc(logit_exp, 1)
        transposed([HTOK[:, :, P * q:P * q + P] for q in range(KC)])
        meet(act, c, "act")
        meet(act, c, "act")
        c.skip(prod_ready, KC)
        gemm(gathered())
        meet(act, c, "act")
        meet(act, c, "act")
        transposed([GT[:, q] for q in range(KC)])
        meet(act, c, "act")
        with act.Fori(0, N_EXPERTS // 2) as i:
            c.loop(i, {gu_ready: 16, up_ready: 16, y_ready: 16})
            for n in range(16):
                act.wait_ge(gu_ready, c.next(gu_ready, 1, lag=2))
                act.wait_ge(up_ready, c.next(up_ready))
                act.activation(MG[:, n % 2, 0:64], bank[n % 2][:, 0:64], ACT.Silu).then_inc(silu_ready, 1)
            act.wait_ge(y_ready, c.next(y_ready, 16))
            act.activation(YS[:, 0:T], bank[2], ACT.Copy).then_inc(y_copied, 1)
            c.looped(N_EXPERTS // 2)
        meet(act, c, "act")

    @block.tensor
    def _(pe):
        c = Count()
        mm = nc.tensor.matmul
        meet(pe, c, "pe")
        meet(pe, c, "pe")

        def norm(groups):
            for g in groups:
                pe.wait_ge(ms_ready, c.next(ms_ready, 1, lag=1))
                for k, (s, r) in enumerate(zip(g["src"], g["rows"])):
                    b = c.at.get(sq_ready.name, 0) % 2
                    pe.wait_ge(sq_ready, c.next(sq_ready))
                    mm(bank[7], g["ones"][0:r, :], sq[0:r, b], start=k == 0, stop=k == len(g["src"]) - 1).then_inc(sq_used, 1)

        def arrived(n):
            pe.wait_ge(w_in[n % SLOTS], c.next(w_in[n % SLOTS], 16))

        def gemm(jobs, split=True):
            for n, j in enumerate(jobs):
                for item in j["need"]:
                    arrived(item)
                if split:
                    taken = (taken_act, taken_dve)[n % 2]
                    pe.wait_ge(taken, c.next(taken, 1, lag=2))
                else:
                    pe.wait_ge(taken_dve, c.next(taken_dve, 1, lag=4))
                o = bank[n % 4][j["p0"]:j["p0"] + j["rows"], 0:j["n"]]
                for k, (w, r) in enumerate(j["terms"]):
                    last = mm(o, w, r, start=k == 0, stop=k == len(j["terms"]) - 1)
                last.then_inc(prod_ready, 1)

        def transposed(src):
            for q in range(KC):
                pe.wait_ge(fold_copied, c.next(fold_copied, 1, lag=2))
                for i in range(NT):
                    last = nc.tensor.transpose(bank[4 + q % 2][:, P * i:P * i + P], src(q, i), ident)
                last.then_inc(fold_ready, 1)

        def ropes(list_):
            for n, (X, R, cos, sin) in enumerate(list_):
                pe.wait_ge(rope_done, c.next(rope_done, 1, lag=4))
                p0, r = X.start_partition(), X.shape[0]
                mm(bank[n % 4][p0:p0 + r, :], R, X, start=True, stop=True).then_inc(rot_ready, 1)

        def ffn(base):
            def up(n):
                s = (base + n) % SLOTS
                arrived(base + n)
                w = ring[:, s, 0:2048].rearrange("p (a k n) -> p a k n", a=2, k=KC)
                for a in range(2):
                    for k in range(KC):
                        last = mm(bank[n % 2 + 2 * a], w[:, a, k, :], h[:, k, :], start=k == 0, stop=k == KC - 1)
                last.then_inc(up_ready, 1)

            def down(n):
                w = ring[:, (base + n) % SLOTS, 2048:3072]
                pe.wait_ge(gu_ready, c.next(gu_ready))
                for q in range(KC):
                    pe.wait_ge(down_used, c.next(down_used, 1, lag=4))
                    mm(bank[4 + q % 4], w[:, P * q:P * q + P], GU[:, n % 2], start=True, stop=True).then_inc(down_ready, 1)

            up(0)
            for n in range(SLOTS):
                up(n + 1)
                down(n)
            with pe.Fori(0, FFN_TRIPS) as i:
                c.loop(i, {gu_ready: SLOTS, down_used: SLOTS * KC, **{s: 16 for s in w_in}})
                for r in range(SLOTS):
                    up(r + 1)
                    down(r)
                c.looped(FFN_TRIPS)
            for n in range(SLOTS * (FFN_TRIPS + 1), FFN_ITEMS):
                if n + 1 < FFN_ITEMS:
                    up(n + 1)
                down(n)

        def attention(tiles):
            def scores(a):
                t = tiles[a]
                o = bank[a % 2]
                last = mm(o[:, 0:t["n"]], t["q"], t["k"], start=True, stop=True)
                if t["mask"] is not None:
                    m, at = t["mask"]
                    last = mm(o[:, at:at + m.shape[1]], ident, m, start=False, stop=True, skip_group_check=True)
                last.then_inc(scores_ready, 1)

            def turn(a):
                t = tiles[a]
                pe.wait_ge(probs_ready, c.next(probs_ready))
                for j in range(len(t["v"])):
                    last = nc.tensor.transpose(bank[2 + a % 2][0:t["rows"], P * j:P * j + P],
                                               prob[:, a % 2, P * j:P * j + t["rows"]], ident)
                last.then_inc(pT_ready, 1)

            def values(a):
                t = tiles[a]
                pe.wait_ge(pT_copied, c.next(pT_copied))
                pe.wait_ge(o_done, c.next(o_done, 1, lag=2))
                for j, v in enumerate(t["v"]):
                    last = mm(bank[4 + a % 2][:, 0:64], probT[0:t["rows"], a % 2, P * j:P * j + P], v,
                              start=j == 0, stop=j == len(t["v"]) - 1)
                last.then_inc(pv_ready, 1)

            for a in range(len(tiles) + 2):
                if a < len(tiles):
                    scores(a)
                if 0 <= a - 1 < len(tiles):
                    turn(a - 1)
                if a >= 2:
                    values(a - 2)

        for l in range(LAYERS):
            b = l * per_layer
            norm(norm_x(COL_FFN1 + 8 * l))
            meet(pe, c, "pe")
            ffn(b)
            meet(pe, c, "pe")
            b += FFN_ITEMS
            norm(norm_x(COL_MIX + 8 * l))
            meet(pe, c, "pe")
            gemm(project_one(b))
            meet(pe, c, "pe")
            norm(norm_mla(l))
            ropes(ropes_first())
            meet(pe, c, "pe")
            gemm(project_mla(b))
            meet(pe, c, "pe")
            ropes(ropes_mla())
            w = [ring[:, (b + 8 + part) % SLOTS, :] for part in range(2)]
            for part in range(2):
                arrived(b + 8 + part)
                for g in range(B_GROUPS):
                    s = slice(64 * g, 64 * g + 64)
                    o = bank[4 + 2 * part + g]
                    for i in range(CMP_LEN):
                        mm(o[s, 0:N_CMP], w[part][s, 64 * i:64 * i + 64], KB[s, part, i:i + CMP_STRIDE * (N_CMP - 1) + 1:CMP_STRIDE],
                           start=i == 0, stop=i == CMP_LEN - 1)
                    pe0 = COL_PE + (2 * l + part) * CMP_LEN
                    for i in range(CMP_LEN):
                        last = mm(o[s, 32:33], w[part][s, 64 * i:64 * i + 64], cols[s, pe0 + i:pe0 + i + 1],
                                  start=i == 0, stop=i == CMP_LEN - 1)
                    last.then_inc(cmp_ready, 1)
            pe.wait_ge(cmp_hid, c.next(cmp_hid, 4))
            for g in range(B_GROUPS):
                s = slice(64 * g, 64 * g + 64)
                mm(bank[4][s, 64:64 + N_CMP], w[0][s, 2048:2112], HID[s, 0], start=True, stop=True)
                last = mm(bank[5 + g][0:N_CMP, 64:128], HID[s, 1], w[1][s, 2048:2112], start=True, stop=True)
            last.then_inc(cmp_ready, 1)
            meet(pe, c, "pe")
            attention(mixer_tiles())
            meet(pe, c, "pe")
            meet(pe, c, "pe")
            transposed(lambda q, i: O[:, i, P * q:P * q + P])
            meet(pe, c, "pe")
            gemm(project_out(b + 10), split=False)
            meet(pe, c, "pe")
            norm(norm_x(COL_FFN2 + 8 * l))
            meet(pe, c, "pe")
            ffn(b + MIX_ITEMS)
            meet(pe, c, "pe")
        norm(norm_final())
        meet(pe, c, "pe")
        norm(norm_x(COL_N1))
        meet(pe, c, "pe")
        gemm(project_second(base_second))
        meet(pe, c, "pe")
        norm(norm_heads())
        meet(pe, c, "pe")
        attention(dilated_tiles())
        meet(pe, c, "pe")
        meet(pe, c, "pe")

        for m in range(H_HEADS):
            for d in range(2):
                pe.wait_ge(qk_ready, c.next(qk_ready))
                pe.wait_ge(off_copied, c.next(off_copied, 1, lag=1))
                for n, (I, J) in enumerate(PAIRS[d]):
                    q = QT[:, I] if n < 3 else QX[:, n - 3]
                    last = mm(bank[n // 3][:, P * (n % 3):P * (n % 3) + P], KT[:, J], q, start=True, stop=True)
                last.then_inc(off_ready, 1)
                for n, w in enumerate(LEVELS):
                    pe.wait_ge(lvl_ready, c.next(lvl_ready))
                    pe.wait_ge(lvl_put, c.next(lvl_put, 1, lag=2))
                    for i in range(NT):
                        blk = MM[:, n % 2, P * i:P * i + P]
                        last = mm(bank[2 + n % 2][:, 64 * i:64 * i + 64], blk, halves(blk, w)[1 - d], start=True, stop=True)
                    last.then_inc(lvl_mm, 1)
            pe.wait_ge(keys_ready, c.next(keys_ready, 2))
            for i in range(NT):
                last = mm(bank[6][:, P * i:P * i + P], KSUM[:, i], HQ[:, m, P * i:P * i + P], start=True, stop=True)
            last.then_inc(diag_mm, 1)
            pe.wait_ge(diag_put, c.next(diag_put))
            pe.wait_ge(off_copied, c.next(off_copied, 0))
            pe.wait_ge(head_out, c.next(head_out, 1, lag=1))
            for I in range(NT):
                terms = [(AT[:, I], I)] + [(AO[d][:, n], J) for d in range(2) for n, (i, J) in enumerate(PAIRS[d]) if i == I]
                for k, (w, J) in enumerate(terms):
                    last = mm(bank[7][:, P * I:P * I + P], w, VI[:, J, P * m:P * m + P], start=k == 0, stop=k == len(terms) - 1)
            last.then_inc(head_mm, 1)
        meet(pe, c, "pe")
        meet(pe, c, "pe")
        transposed(lambda q, i: O[:, i, P * q:P * q + P])
        meet(pe, c, "pe")
        gemm(project_out(base_second + 11), split=False)
        meet(pe, c, "pe")
        norm(norm_x(COL_N2))
        meet(pe, c, "pe")
        for i in range(NT):
            for k in range(KC):
                last = mm(bank[0][:, 16 * i:16 * i + 16], h[:, k, P * i:P * i + P], RW[:, k, :], start=k == 0, stop=k == KC - 1)
        last.then_inc(logit_ready, 1)
        transposed(lambda q, i: h[:, q, P * i:P * i + P])
        pe.wait_ge(aff_ready, c.next(aff_ready))
        for i in range(NT):
            last = nc.tensor.transpose(bank[1][0:16, P * i:P * i + P], AFF[:, i], ident)
        last.then_inc(affT_ready, 1)
        pe.wait_ge(slotT_ready, c.next(slotT_ready))
        for i in range(NT):
            last = nc.tensor.transpose(bank[2][:, 16 * i:16 * i + 16], SLOTT[0:16, P * i:P * i + P], ident[0:16, 0:16])
        last.then_inc(slot_ready, 1)
        meet(pe, c, "pe")
        meet(pe, c, "pe")
        gemm(gathered())
        meet(pe, c, "pe")
        meet(pe, c, "pe")
        transposed(lambda q, i: SEL[:, i, P * q:P * q + P])
        meet(pe, c, "pe")
        with pe.Fori(0, N_EXPERTS // 2) as i:
            c.loop(i, {gu_ready: 16, y_copied: 2, down_used: KC, **{s: 64 for s in w_in}})

            def up(n):
                arrived(n)
                w = ring[:, n % SLOTS, 0:2048].rearrange("p (a k n) -> p a k n", a=2, k=KC)
                for a in range(2):
                    for k in range(KC):
                        last = mm(bank[n % 2][:, 64 * a:64 * a + 64], w[:, a, k, :],
                                  XIN[:, k, bass.ds(i * P + 64 * (n // MOE_ITEMS), 64)], start=k == 0, stop=k == KC - 1)
                last.then_inc(up_ready, 1)

            up(0)
            for n in range(16):
                if n < 15:
                    up(n + 1)
                e = n // MOE_ITEMS
                pe.wait_ge(gu_ready, c.next(gu_ready))
                for s in range(2):
                    last = mm(bank[2 + s][64 * e:64 * e + 64, :], MGU[:, n % 2, 0:64],
                              ring[:, n % SLOTS, 2048 + 512 * s:2560 + 512 * s], start=n % 8 == 0, stop=n % 8 == 7)
                last.then_inc(y_ready, 1)
            pe.wait_ge(y_copied, c.next(y_copied, 2))
            for q in range(KC):
                pe.wait_ge(down_used, c.next(down_used, 1, lag=4))
                mm(bank[4 + q % 4], YS[:, P * q:P * q + P], GT[:, bass.ds(i, 1), :].rearrange("p a n -> p (a n)"),
                   start=True, stop=True).then_inc(down_ready, 1)
            c.looped(N_EXPERTS // 2)
        meet(pe, c, "pe")

    @block.vector
    def _(dve):
        c = Count()
        V = nc.vector
        meet(dve, c, "dve")

        def step(ins):
            ins.then_inc(step_dve, c.one(step_dve))
            dve.wait_ge(step_dve, c.made(step_dve))

        posf, ang, rnd, tmp = (mix[:, 512 * n:512 * n + 512] for n in range(1, 5))
        step(V.tensor_copy(posf, mix[:, 0:T].bitcast(I32)))
        for n in range(3):
            s, k = ANGLE[n]
            step(V.tensor_scalar(ang, posf, cst(C_INV + n), None, ALU.mult))
            step(V.tensor_scalar(rnd, ang, 1 / (2 * math.pi), ROUND, ALU.mult, ALU.add))
            step(V.tensor_scalar(rnd, rnd, -ROUND, None, ALU.add))
            for part in TWO_PI:
                step(V.scalar_tensor_tensor(ang, rnd, -part, ang, ALU.mult, ALU.add))
            step(V.tensor_scalar(tmp, ang, math.pi / 2, None, ALU.add))
            step(V.tensor_scalar(rnd, tmp, math.pi, -2 * math.pi, ALU.is_gt, ALU.mult))
            step(V.tensor_tensor(tmp, tmp, rnd, ALU.add))
            V.tensor_scalar(s, ang, SIN_MAX, -SIN_MAX, ALU.min, ALU.max).then_inc(for_act, 1)
            V.tensor_scalar(k, tmp, SIN_MAX, -SIN_MAX, ALU.min, ALU.max).then_inc(for_act, 1)
            dve.wait_ge(for_act, 2 * n + 2)
        meet(dve, c, "dve")

        def norm(groups):
            for g in groups:
                dve.wait_ge(sq_used, c.next(sq_used, len(g["src"])))
                dve.wait_ge(normed, c.made(normed))
                V.tensor_scalar(rms, bank[7], 1.0 / g["width"], EPS, ALU.mult, ALU.add).then_inc(ms_ready, 1)
                dve.wait_ge(rms_ready, c.next(rms_ready))
                step(V.reciprocal(rms, rms))
                for s, o, gain, r in zip(g["src"], g["dst"], g["gain"], g["rows"]):
                    V.scalar_tensor_tensor(o, s, gain, rms[0:r, :], ALU.mult, ALU.mult).then_inc(normed, c.one(normed))

        def gemm(jobs, split=True):
            for n, j in enumerate(jobs):
                if split and n % 2 == 0:
                    c.skip(prod_ready)
                    continue
                dve.wait_ge(prod_ready, c.next(prod_ready))
                src = bank[n % 4][j["p0"]:j["p0"] + j["rows"], 0:j["n"]]
                if j["add"]:
                    ins = V.tensor_tensor(j["dst"], src, j["dst"], ALU.add)
                elif j["scale"]:
                    ins = V.tensor_scalar(j["dst"], src, j["scale"], None, ALU.mult)
                else:
                    ins = V.tensor_copy(j["dst"], src)
                ins.then_inc(taken_dve, 1)

        def ropes(list_):
            for n, (X, R, cos, sin) in enumerate(list_):
                p0, r = X.start_partition(), X.shape[0]
                t = sq[p0:p0 + r, n % 2]
                dve.wait_ge(rot_ready, c.next(rot_ready))
                step(V.tensor_tensor(t, bank[n % 4][p0:p0 + r, :], sin, ALU.mult))
                dve.wait_ge(cos_done, c.next(cos_done))
                V.tensor_tensor(X, X, t, ALU.add).then_inc(rope_done, c.one(rope_done))

        def hidden(n, silu_, up_, dst):
            dve.wait_ge(silu_ready, c.next(silu_ready))
            V.tensor_tensor(dst, silu_, up_, ALU.mult).then_inc(gu_ready, c.one(gu_ready))

        def add_down(scale):
            for q in range(KC):
                dve.wait_ge(down_ready, c.next(down_ready))
                dve.wait_ge(down_used, c.made(down_used, lag=KC - 1))
                V.scalar_tensor_tensor(x[:, q], bank[4 + q % 4], scale, x[:, q], ALU.mult, ALU.add).then_inc(down_used, c.one(down_used))

        def ffn():
            def both(n):
                hidden(n + 1, SILU[:, (n + 1) % 2], bank[2 + (n + 1) % 2], GU[:, (n + 1) % 2])
                add_down(0.5)
            hidden(0, SILU[:, 0], bank[2], GU[:, 0])
            for n in range(SLOTS):
                both(n)
            with dve.Fori(0, FFN_TRIPS) as i:
                c.loop(i, {silu_ready: SLOTS, gu_ready: SLOTS, down_ready: SLOTS * KC, down_used: SLOTS * KC})
                for r in range(SLOTS):
                    both(r)
                c.looped(FFN_TRIPS)
            for n in range(SLOTS * (FFN_TRIPS + 1), FFN_ITEMS - 1):
                both(n)
            add_down(0.5)

        def attention(tiles):
            def maximum(a):
                t = tiles[a]
                src = bank[a % 2][:, 0:t["n"]]
                if t["bias"] is not None:
                    hb = HB[:, t["bias"] % 2]
                    if t["i"] == 0:
                        step(V.scalar_tensor_tensor(hb, table[:, C2_DIST:C2_DIST + 896], -(2.0 ** -(t["bias"] + 1)),
                                                    table[:, C2_MULT:C2_MULT + 896], ALU.mult, ALU.add))
                    at = 384 - P * t["i"]
                    dve.wait_ge(scores_ready, c.next(scores_ready))
                    step(V.scalar_tensor_tensor(SB[:, a % 2], src, E_DH ** -0.5, hb[:, at:at + T], ALU.mult, ALU.add))
                    src = SB[:, a % 2]
                else:
                    dve.wait_ge(scores_ready, c.next(scores_ready))
                V.tensor_reduce(NM[:, a % 4:a % 4 + 1], src, AX.X, ALU.max, negate=True).then_inc(max_ready, 1)

            def copied(a):
                t = tiles[a]
                n = P * len(t["v"])
                dve.wait_ge(pT_ready, c.next(pT_ready))
                V.tensor_copy(probT[0:t["rows"], a % 2, 0:n], bank[2 + a % 2][0:t["rows"], 0:n]).then_inc(pT_copied, 1)
                V.reciprocal(RDEN[:, a % 4:a % 4 + 1], DEN[:, a % 4:a % 4 + 1]).then_inc(step_dve, c.one(step_dve))

            def result(a):
                t = tiles[a]
                r = RDEN[:, a % 4:a % 4 + 1]
                src = bank[4 + a % 2][:, 0:64]
                if t["mode"] == "add":
                    w = WGT[:, a % 4:a % 4 + 1]
                    dve.wait_ge(step_dve, c.made(step_dve))
                    step(V.tensor_tensor(w, r, t["gate"], ALU.mult))
                    dve.wait_ge(pv_ready, c.next(pv_ready))
                    dve.wait_ge(o_done, c.made(o_done, lag=3))
                    ins = V.scalar_tensor_tensor(t["out"], src, w, t["out"], ALU.mult, ALU.add)
                else:
                    dve.wait_ge(step_dve, c.made(step_dve))
                    dve.wait_ge(pv_ready, c.next(pv_ready))
                    if t["mode"] == "gated":
                        ins = V.tensor_scalar(t["out"], src, r, t["gate"], ALU.mult, ALU.mult)
                    else:
                        ins = V.tensor_scalar(t["out"], src, r, None, ALU.mult)
                ins.then_inc(o_done, c.one(o_done))

            for a in range(len(tiles) + 2):
                if a < len(tiles):
                    maximum(a)
                if 0 <= a - 1 < len(tiles):
                    copied(a - 1)
                if a >= 2:
                    result(a - 2)

        def head_norm(col0, heads, n, gain, factor, gate=None):
            v = O[:, :, col0:col0 + heads * n].rearrange("p i (m n) -> p i m n", m=heads)
            sqv = SUBSQ[:, 0:NT * heads * n]
            step(V.tensor_tensor(sqv.rearrange("p (i m n) -> p i m n", i=NT, m=heads), v, v, ALU.mult))
            step(V.tensor_reduce(MS16, sqv.rearrange("p (a n) -> p a n", n=n), AX.X, ALU.add))
            V.tensor_scalar(MS16, MS16, 1.0 / n, EPS, ALU.mult, ALU.add).then_inc(for_act, 1)
            dve.wait_ge(for_dve, c.next(for_dve))
            step(V.reciprocal(MS16, MS16))
            g = SUBSQ[:, 0:n]
            step(V.tensor_scalar(g, gain, factor, None, ALU.mult))
            r = MS16.rearrange("p (i m) -> p i m", i=NT).unsqueeze(3).to_broadcast([P, NT, heads, n])
            step(V.tensor_tensor(v, v, r, ALU.mult))
            step(V.tensor_tensor(v, v, g.unsqueeze(1).unsqueeze(1).to_broadcast([P, NT, heads, n]), ALU.mult))
            if gate is not None:
                o = O[:, :, col0:col0 + heads * n]
                step(V.tensor_tensor(o, o, gate, ALU.mult))

        for l in range(LAYERS):
            lam_init = 0.8 - 0.6 * math.exp(-0.3 * l)
            norm(norm_x(COL_FFN1 + 8 * l))
            meet(dve, c, "dve")
            ffn()
            meet(dve, c, "dve")
            norm(norm_x(COL_MIX + 8 * l))
            meet(dve, c, "dve")
            gemm(project_one(0))
            meet(dve, c, "dve")
            norm(norm_mla(l))
            r0 = ROW_LAM + 4 * C_DH * l
            lp = small[:, 256:256 + 2 * C_DH]
            step(V.tensor_tensor(lp, rows[:, r0:r0 + 2 * C_DH], rows[:, r0 + 2 * C_DH:r0 + 4 * C_DH], ALU.mult))
            V.tensor_reduce(LAM[:, 0:2], lp.rearrange("p (a n) -> p a n", a=2), AX.X, ALU.add).then_inc(for_act, 1)
            ropes(ropes_first())
            dve.wait_ge(for_dve, c.next(for_dve))
            step(V.tensor_tensor(LAM[:, 2:3], LAM[:, 0:1], LAM[:, 1:2], ALU.subtract))
            V.tensor_scalar(LAM[:, 3:4], LAM[:, 2:3], -1.0, -lam_init, ALU.mult, ALU.add)
            dve.wait_ge(for_dve, c.next(for_dve))
            g0 = GATE[:, 0, 0:3 * B_HEADS:3]
            V.tensor_scalar(g0, g0, cst(C_ROWM), None, ALU.mult)
            meet(dve, c, "dve")
            gemm(project_mla(0))
            meet(dve, c, "dve")
            ropes(ropes_mla())
            for part in range(2):
                for g in range(B_GROUPS):
                    s = slice(64 * g, 64 * g + 64)
                    dve.wait_ge(cmp_ready, c.next(cmp_ready))
                    V.tensor_copy(CB[s, part:part + 1], bank[4 + 2 * part + g][s, 32:33]).then_inc(cmp_bias, 1)
            dve.wait_ge(cmp_ready, c.next(cmp_ready))
            V.tensor_copy(KCMP, bank[4][:, 64:64 + N_CMP])
            for g in range(B_GROUPS):
                V.tensor_copy(VCMP[0:N_CMP, g], bank[5 + g][0:N_CMP, 64:128])
            meet(dve, c, "dve")
            attention(mixer_tiles())
            meet(dve, c, "dve")
            head_norm(768, C_HEADS, 2 * C_DH, rows[:, ROW_SUB + 64 * l:ROW_SUB + 64 * l + 64], 1.0 - lam_init)
            meet(dve, c, "dve")
            meet(dve, c, "dve")
            gemm(project_out(0), split=False)
            meet(dve, c, "dve")
            norm(norm_x(COL_FFN2 + 8 * l))
            meet(dve, c, "dve")
            ffn()
            meet(dve, c, "dve")
        norm(norm_final())
        meet(dve, c, "dve")
        norm(norm_x(COL_N1))
        meet(dve, c, "dve")
        gemm(project_second(0))
        meet(dve, c, "dve")
        norm(norm_heads())
        meet(dve, c, "dve")
        attention(dilated_tiles())
        meet(dve, c, "dve")

        V.tensor_tensor(LBT, cols[:, COL_LB + 8:COL_LB + 16], cols[:, COL_LB:COL_LB + 8], ALU.subtract).then_inc(for_act, 1)
        dve.wait_ge(for_dve, c.next(for_dve))
        step(V.tensor_scalar(LBT, LBT, 1.0, None, ALU.add))
        step(V.reciprocal(LB, LBT))
        step(V.tensor_scalar(OMLB, LB, -1.0, 1.0, ALU.mult, ALU.add))
        for d in range(2):
            dve.wait_ge(for_dve, c.next(for_dve))
            for m in range(H_HEADS):
                u = 4 * d + m
                V.tensor_scalar(K2[d][:, m], K2[d][:, m], OMLB[:, u:u + 1], None, ALU.mult)
                last = V.tensor_scalar(Z[d][:, m], Z[d][:, m], OMLB[:, u:u + 1], LB[:, u:u + 1], ALU.mult, ALU.add)
            last.then_inc(for_act, 1)
        V.memset(BC[:, :, 0:1], 0.0)
        meet(dve, c, "dve")

        for m in range(H_HEADS):
            q = HQ[:, m]
            for d in range(2):
                k = K2[d][:, m]
                for i in range(NT):
                    last = V.tensor_tensor_scan(BC[:, i, 1:P + 1], ones, Z[d][:, m, P * i:P * i + P], 0.0, ALU.mult, ALU.add)
                last.then_inc(scan_ready, c.one(scan_ready))
                dve.wait_ge(scan_ready, c.made(scan_ready))
                V.tensor_tensor(DD[:, 0].rearrange("p (i n) -> p i n", i=NT), BC[:, :, P:P + 1].to_broadcast([P, NT, P]),
                                cum(d), ALU.subtract).then_inc(diff_ready, c.one(diff_ready))
                dve.wait_ge(fac_ready, c.next(fac_ready))
                if m or d:
                    dve.wait_ge(off_ready, c.next(off_ready, 0))
                V.tensor_tensor(QT.rearrange("p i n -> p (i n)"), q, EE[:, d], ALU.mult).then_inc(step_dve, c.one(step_dve))
                V.tensor_tensor(KT.rearrange("p i n -> p (i n)"), k, EE[:, 1 - d], ALU.mult).then_inc(step_dve, c.one(step_dve))
                dve.wait_ge(step_dve, c.made(step_dve))
                step(V.tensor_scalar(QX[:, 0], QT[:, 0 if d else 2], ET[:, 1:2], None, ALU.mult))
                step(V.tensor_scalar(QX[:, 1], QT[:, 1 if d else 3], ET[:, 2:3], None, ALU.mult))
                V.tensor_scalar(QX[:, 2], QX[:, 1 - d], ET[:, 1 + d:2 + d], None, ALU.mult).then_inc(qk_ready, 1)
                dve.wait_ge(off_ready, c.next(off_ready))
                if d == 0:
                    dve.wait_ge(keys_ready, c.next(keys_ready, 2))

                def diff(n):
                    w = LEVELS[n]
                    v = cum(d).rearrange("p i (j w) -> p i j w", w=2 * w)
                    r = w if d else w - 1
                    V.tensor_tensor(DD[:, n % 2].rearrange("p (i j w) -> p i j w", i=NT, w=2 * w), v,
                                    v[:, :, :, r:r + 1].to_broadcast([P, NT, 64 // w, 2 * w]), ALU.subtract).then_inc(diff_ready, c.one(diff_ready))

                def product(n):
                    w = LEVELS[n]
                    dve.wait_ge(decay_ready, c.next(decay_ready))
                    e, o = halves(EE[:, n % 2], w), halves(MM[:, n % 2], w)
                    left, right = (q, k) if d else (k, q)
                    V.tensor_tensor(o[0], halves(left, w)[0], e[0], ALU.mult)
                    V.tensor_tensor(o[1], halves(right, w)[1], e[1], ALU.mult).then_inc(lvl_ready, 1)

                def put(n):
                    w = LEVELS[n]
                    dve.wait_ge(lvl_mm, c.next(lvl_mm))
                    at = C2_LVL + (d * len(LEVELS) + n) * 64
                    mask = table[:, at:at + 64].bitcast(I32).rearrange("p (j w) -> p j w", w=w)
                    o = AT.rearrange("p i (j w) -> p i j w", w=2 * w)
                    o = o[:, :, :, 0:w] if d else o[:, :, :, w:2 * w]
                    dve.wait_ge(lvl_put, c.made(lvl_put))
                    for i in range(NT):
                        ins = V.copy_predicated(o[:, i], mask, bank[2 + n % 2][:, 64 * i:64 * i + 64].rearrange("p (j w) -> p j w", w=w))
                    ins.then_inc(lvl_put, c.one(lvl_put))

                for n in range(len(LEVELS) + 2):
                    if n < len(LEVELS):
                        diff(n)
                    if 0 <= n - 1 < len(LEVELS):
                        product(n - 1)
                    if n >= 2:
                        put(n - 2)
            dve.wait_ge(diag_mm, c.next(diag_mm))
            dve.wait_ge(lvl_put, c.made(lvl_put))
            for i in range(NT):
                ins = V.copy_predicated(AT[:, i], ident.bitcast(I32), bank[6][:, P * i:P * i + P])
            ins.then_inc(diag_put, 1)
            dve.wait_ge(head_mm, c.next(head_mm))
        meet(dve, c, "dve")
        head_norm(512, H_HEADS, P, rows[:, ROW_OUT:ROW_OUT + P], 1.0, GG)
        meet(dve, c, "dve")
        meet(dve, c, "dve")
        gemm(project_out(0), split=False)
        meet(dve, c, "dve")
        norm(norm_x(COL_N2))
        meet(dve, c, "dve")

        dve.wait_ge(logit_ready, c.next(logit_ready))
        for i in range(NT):
            last = V.tensor_reduce(NM[:, i:i + 1], bank[0][:, 16 * i:16 * i + 16], AX.X, ALU.max, negate=True)
        last.then_inc(logit_max, 1)
        dve.wait_ge(logit_exp, c.next(logit_exp, NT))
        step(V.reciprocal(RDEN, DEN))
        for i in range(NT):
            last = V.tensor_scalar(AFF[:, i], AFF[:, i], RDEN[:, i:i + 1], None, ALU.mult)
        last.then_inc(aff_ready, 1)
        best, work, chosen, place = small[0:16, 256:264], rms[0:16, :], probT[0:16, 0], probT[0:16, 1]
        dve.wait_ge(affT_ready, c.next(affT_ready))
        step(V.tensor_copy(work, bank[1][0:16, :]))
        for n in range(CAP // 8):
            step(V.max(best, work))
            step(V.match_replace(work, best, work, NEG))
        step(V.tensor_scalar(chosen, work, NEG / 2, None, ALU.is_lt))
        step(V.tensor_tensor_scan(place, chosen, chosen, 0.0, ALU.add, ALU.max))
        step(V.tensor_tensor(place, place, chosen, ALU.mult))
        V.tensor_scalar(SLOTT[0:16], place, -1.0, None, ALU.add).then_inc(slotT_ready, 1)
        dve.wait_ge(slot_ready, c.next(slot_ready))
        V.tensor_copy(SLOT, bank[2][:, 0:64].rearrange("p (i e) -> p i e", i=NT))
        meet(dve, c, "dve")
        iota = cst(C_IOTA, CAP).unsqueeze(1).to_broadcast([P, N_EXPERTS, CAP])
        for i in range(NT):
            V.tensor_tensor(SEL[:, i].rearrange("p (e n) -> p e n", e=N_EXPERTS),
                            SLOT[:, i].unsqueeze(2).to_broadcast([P, N_EXPERTS, CAP]), iota, ALU.is_equal)
        meet(dve, c, "dve")
        gemm(gathered())
        meet(dve, c, "dve")
        for i in range(NT):
            s = SEL[:, i].rearrange("p (e n) -> p e n", e=N_EXPERTS)
            V.tensor_tensor(s, s, AFF[:, i].unsqueeze(2).to_broadcast([P, N_EXPERTS, CAP]), ALU.mult)
        meet(dve, c, "dve")
        meet(dve, c, "dve")
        with dve.Fori(0, N_EXPERTS // 2) as i:
            c.loop(i, {silu_ready: 16, gu_ready: 16, y_ready: 16, down_ready: KC, down_used: KC})
            for n in range(16):
                hidden(n, MG[:, n % 2, 0:64], bank[n % 2][:, 64:128], MGU[:, n % 2, 0:64])
            dve.wait_ge(y_ready, c.next(y_ready, 16))
            V.tensor_copy(YS[:, T:2 * T], bank[3]).then_inc(y_copied, 1)
            add_down(1.0)
            c.looped(N_EXPERTS // 2)
        meet(dve, c, "dve")

    block_cm.__exit__(None, None, None)


def kernel(**inputs):
    import concourse.bacc as bacc
    from concourse.bass_utils import run_bass_kernel_spmd

    a = {k: np.asarray(v) for k, v in inputs.items()}
    f32 = np.float32

    def tiled(w):
        k, n = w.shape
        return w.reshape(k // P, P, n).transpose(1, 0, 2).reshape(P, -1)

    def columns(v):
        return v.reshape(-1, P).T

    def units(wg, wu, wd):
        n = wg.shape[1] // P
        up = [w.reshape(KC, P, n, P).transpose(2, 1, 0, 3).reshape(n, P, D) for w in (wg, wu)]
        return np.concatenate(up + [wd.reshape(n, P, D)], axis=2)

    ffn_w = np.stack([units(a[f"ffn{f}_wg"][l], a[f"ffn{f}_wu"][l], a[f"ffn{f}_wd"][l]) for l in range(LAYERS) for f in (1, 2)])
    moe_w = np.concatenate([units(a["w_expert_gate_2"][0, e], a["w_expert_up_2"][0, e], a["w_expert_down_2"][0, e])
                            for e in range(N_EXPERTS)])

    def items(list_):
        r = np.zeros((len(list_), P, ITEM), f32)
        for n, v in enumerate(list_):
            r[n, :, :v.shape[1]] = v
        return r

    def by_columns(w):
        return [tiled(w[:, n:n + WCOLS]) for n in range(0, w.shape[1], WCOLS)]

    mixes = []
    for l in range(LAYERS):
        w = a["w_in"][l]
        wb, wc = w[:, A_COLS:A_COLS + B_COLS], w[:, A_COLS + B_COLS:]
        qb = wb[:, :384].reshape(D, B_GROUPS, B_HPG, B_DH).transpose(0, 2, 1, 3).reshape(D, 384)
        kv = [wb[:, 384 + 128 * n:512 + 128 * n] for n in range(6)]
        parts = [w[:, :A_COLS], qb, np.concatenate([kv[0], kv[1], kv[2]], 1), np.concatenate([kv[4], kv[3], kv[5]], 1),
                 np.concatenate([wc[:, :256], wb[:, 1152:]], 1), wc[:, 256:512], wc[:, 512:]]
        uq = np.zeros((256, 576), f32)
        uq[:A_QR] = a["mla_w_uq"][l]
        mla = np.concatenate([tiled(uq), a["mla_w_ukv"][l]], 1)
        phi = [np.tile(np.concatenate([a[f"nsa_phi_{s}1"][l].reshape(CMP_LEN, B_DH, B_DH).transpose(1, 0, 2).reshape(B_DH, -1),
                                       a[f"nsa_phi_{s}2"][l]], 1), (2, 1)) for s in "kv"]
        mixes.append(items([tiled(v) for v in parts] + [mla] + phi + by_columns(a["w_out"][l])))
    second = items(by_columns(a["w_in_2"][0]) + by_columns(a["w_out_2"][0]))

    cols = np.zeros((P, N_COLS), f32)
    for l in range(LAYERS):
        cols[:, COL_FFN1 + 8 * l:COL_FFN1 + 8 * l + 8] = columns(a["ffn1_norm"][l])
        cols[:, COL_MIX + 8 * l:COL_MIX + 8 * l + 8] = columns(a["mix_norm"][l])
        cols[:, COL_FFN2 + 8 * l:COL_FFN2 + 8 * l + 8] = columns(a["ffn2_norm"][l])
        cols[:, COL_MLAQ + 2 * l] = a["mla_q_norm"][l, :P]
        cols[:A_QR - P, COL_MLAQ + 2 * l + 1] = a["mla_q_norm"][l, P:]
        cols[:, COL_MLAKV + l] = a["mla_kv_norm"][l]
        for n, s in enumerate("kv"):
            at = COL_PE + (2 * l + n) * CMP_LEN
            cols[:, at:at + CMP_LEN] = np.tile(a[f"nsa_pe_{s}"][l].T, (2, 1))
    cols[:, COL_FINAL:COL_FINAL + 8] = columns(a["final_norm"])
    cols[:, COL_N1:COL_N1 + 8] = columns(a["norm1_w_2"][0])
    cols[:, COL_N2:COL_N2 + 8] = columns(a["norm2_w_2"][0])
    cols[:, COL_DQ] = np.tile(a["attn_q_norm_w_2"][0], 2)
    cols[:, COL_DK] = np.tile(a["attn_k_norm_w_2"][0], 2)
    for r in range(2):
        for n, s in enumerate(("fwd", "bwd")):
            cols[:, COL_LB + 8 * r + 4 * n:COL_LB + 8 * r + 4 * n + 4] = columns(a[f"hgrn_lb_{s}_2"][r])
    cols[:, COL_ROUTER:] = tiled(a["w_router_2"][0])
    row = np.concatenate([a[f"diff_{s}"][l] for l in range(LAYERS) for s in ("lq1", "lq2", "lk1", "lk2")]
                         + [a["diff_sub_norm"][l] for l in range(LAYERS)] + [a["hgrn_out_norm_w_2"][0]])
    const, const2 = constants()
    arrays = dict(
        ffn_w=ffn_w, mix_w=np.stack(mixes), second_w=second, moe_w=moe_w,
        x_in=np.ascontiguousarray(a["x"][0].T.reshape(KC, P, T).transpose(1, 0, 2)),
        pos_in=np.ascontiguousarray(np.broadcast_to(a["positions"], (P, T))),
        cols_in=cols, rows_in=np.ascontiguousarray(np.broadcast_to(row, (P, N_ROWS))), const_in=const, const2_in=const2)
    nc = bacc.Bacc("TRN2", target_bir_lowering=False, num_devices=1)
    args = [nc.dram_tensor(n, v.shape, mybir.dt.from_np(v.dtype), kind="ExternalInput").ap() for n, v in arrays.items()]
    out = nc.dram_tensor("out", (P, KC, T), F32, kind="ExternalOutput").ap()
    program(nc, *args, out)
    r = run_bass_kernel_spmd(nc, [arrays], core_ids=[0]).results[0]["out"]
    return np.ascontiguousarray(np.asarray(r).transpose(2, 1, 0).reshape(1, T, D))
```

```python
import math

import numpy as np

import concourse.bass as bass
from concourse import mybir

F32 = mybir.dt.float32
F32R = mybir.dt.float32r
BF16 = mybir.dt.bfloat16
I32 = mybir.dt.int32
ALU = mybir.AluOpType
ACT = mybir.ActivationFunctionType
AX = mybir.AxisListType

P = 128
D = 1024
T = 512
LAYERS = 2
KC = D // P
NT = T // P
D_FF = 2816
FFN_ITEMS = D_FF // P
EPS = 1e-6
THETA = 500000.0
NEG = -1e30

A_HEADS, A_QR, A_NOPE, A_ROPE = 6, 192, 64, 32
A_DK = A_NOPE + A_ROPE
B_GROUPS, B_HPG, B_DH = 2, 3, 64
B_HEADS = B_GROUPS * B_HPG
B_ROT = B_DH // 4
CMP_LEN, CMP_STRIDE = 32, 16
N_CMP = (T - CMP_LEN) // CMP_STRIDE + 1
C_HEADS, C_DH = 4, 32
C_ROT = C_DH // 4
A_COLS = A_QR + 128 + A_ROPE
B_COLS = B_HEADS * B_DH + 6 * B_GROUPS * B_DH + 3 * B_HEADS

E_HEADS, E_DH = 8, 64
H_HEADS, H_DK = 4, 128
N_EXPERTS = 16
CAP = 2 * T // N_EXPERTS
MOE_ITEMS = D // P
PATTERNS = ((128, 1), (512, 4), (2048, 16))
LEVELS = (64, 32, 16, 8, 4, 2, 1)

SLOTS = 4
ITEM = 3 * D
WCOLS = ITEM // KC
MOE_SLOTS = 8
MIX_ITEMS = 13
SECOND_ITEMS = 14
FFN_TRIPS = FFN_ITEMS // SLOTS - 1

ROUND = 12582912.0
TWO_PI = (6.28125, 0.0019350051879882812, 3.0199159819e-07)
SIN_MAX = 3.1415925

COL_FFN1, COL_MIX, COL_FFN2 = 0, 16, 32
COL_FINAL, COL_N1, COL_N2 = 48, 56, 64
COL_MLAQ, COL_MLAKV = 72, 76
COL_DQ, COL_DK = 78, 79
COL_LB = 80
COL_PE = 96
COL_ROUTER = COL_PE + LAYERS * 2 * CMP_LEN
N_COLS = COL_ROUTER + KC * N_EXPERTS
ROW_LAM = 0
ROW_SUB = LAYERS * 4 * C_DH
ROW_OUT = ROW_SUB + LAYERS * 2 * C_DH
N_ROWS = ROW_OUT + H_DK
C_ID, C_BLK, C_TRI = 0, 128, 256
C_RA, C_RB, C_RC = 384, 512, 640
C_CMP = 768
C_ROWM = C_CMP + NT * N_CMP
C_INV = C_ROWM + 1
C_IOTA = C_INV + 3
N_CONST = C_IOTA + CAP
C2_DIST, C2_MULT = 0, 896
C2_LVL = 1792
N_CONST2 = C2_LVL + 2 * len(LEVELS) * 64


def constants():
    c = np.zeros((P, N_CONST), np.float32)
    c[:, C_ID:C_ID + P] = np.eye(P)
    for b in range(2):
        c[64 * b:64 * b + 64, C_BLK + 64 * b:C_BLK + 64 * b + 64] = 1
    p = np.arange(P)
    c[:, C_TRI:C_TRI + P] = np.where(p[None, :] <= p[:, None], 0, NEG)
    for at, period, first, half in ((C_RA, P, 64, 16), (C_RB, 64, 0, 8), (C_RC, 32, 0, 4)):
        for b in range(0, P, period):
            for i in range(half):
                c[b + first + half + i, at + b + first + i] = -1
                c[b + first + i, at + b + first + half + i] = 1
    for i in range(NT):
        last = np.arange(N_CMP) * CMP_STRIDE + CMP_LEN - 1
        c[:, C_CMP + i * N_CMP:C_CMP + (i + 1) * N_CMP] = np.where(last[None] <= (i * P + p)[:, None], 0, NEG)
    c[:, C_ROWM] = p >= CMP_LEN - 1
    for n, (period, first, rot) in enumerate(((P, 64, A_ROPE), (64, 0, B_ROT), (32, 0, C_ROT))):
        inv = (1.0 / (np.float32(THETA) ** (np.arange(0, rot, 2, dtype=np.float32) / np.float32(rot)))).astype(np.float32)
        for b in range(0, P, period):
            c[b + first:b + first + rot, C_INV + n] = np.concatenate([inv, inv])
    c[:, C_IOTA:C_IOTA + CAP] = np.arange(CAP)
    d = np.zeros((P, N_CONST2), np.float32)
    dist = np.abs(p[:, None] - np.arange(896)[None] + 384)
    mult = np.zeros(dist.shape)
    for window, dil in PATTERNS:
        mult += (dist % dil == 0) & (dist <= window // 2)
    d[:, C2_DIST:C2_DIST + 896] = dist
    d[:, C2_MULT:C2_MULT + 896] = np.where(mult > 0, np.log(np.maximum(mult, 1)), NEG)
    for back in range(2):
        for n, m in enumerate(LEVELS):
            blk = np.arange(64) // m
            half = (p % (2 * m) >= m) if back else (p % (2 * m) < m)
            at = C2_LVL + (back * len(LEVELS) + n) * 64
            d[:, at:at + 64] = (p[:, None] // (2 * m) == blk[None]) & half[:, None]
    return c, d


class Count:

    def __init__(self):
        self.at, self.own, self.reg, self.rate, self.mark = {}, {}, None, {}, {}

    def value(self, sem, v):
        if self.reg is None:
            return max(v, 0)
        assert v > 0
        return self.reg * self.rate[sem.name] + v

    def next(self, sem, n=1, lag=0):
        self.at[sem.name] = self.at.get(sem.name, 0) + n
        return self.value(sem, self.at[sem.name] - lag)

    def skip(self, sem, n=1):
        self.at[sem.name] = self.at.get(sem.name, 0) + n

    def one(self, sem, n=1):
        self.own[sem.name] = self.own.get(sem.name, 0) + n
        return n

    def made(self, sem, lag=0):
        return self.value(sem, self.own.get(sem.name, 0) - lag)

    def loop(self, reg, rate):
        self.reg, self.rate = reg, {s.name: n for s, n in rate.items()}
        self.mark = (dict(self.at), dict(self.own))

    def looped(self, trips):
        for now, then in zip((self.at, self.own), self.mark):
            for k in now:
                d = now[k] - then.get(k, 0)
                assert d == 0 or d == self.rate[k], (k, d)
                now[k] += d * (trips - 1)
        self.reg = None


def program(nc, ffn_w, mix_w, second_w, moe_w, x_in, pos_in, cols_in, rows_in, const_in, const2_in, out):
    place = {}

    def sb(name, n, dt=F32):
        t = nc.alloc_sbuf_tensor(name, [P, n], dt)
        place[name] = nc.lookup_mloc(t).addr
        return t.ap()

    def rounded(name, over, at, n):
        return nc.alloc_sbuf_tensor_at(name, [P, n], F32R, offset=place[over] + 4 * at).ap()

    x = sb("x", KC * T).rearrange("p (k t) -> p k t", k=KC)
    h = sb("h", KC * T).rearrange("p (k t) -> p k t", k=KC)
    h_hi = rounded("h_hi", "h", 0, KC * T).rearrange("p (k t) -> p k t", k=KC)
    h_lo = sb("h_lo", KC * T, F32R).rearrange("p (k t) -> p k t", k=KC)
    ring = sb("ring", SLOTS * ITEM).rearrange("p (s n) -> p s n", s=SLOTS)
    mix = sb("mix", 18432)
    const = sb("const", N_CONST)
    table = sb("table", 3072)
    cols = sb("cols", N_COLS)
    rows = sb("rows", N_ROWS)
    prob = sb("prob", 3 * T).rearrange("p (b n) -> p b n", b=3)
    share = sb("share", T).rearrange("p (b n) -> p b n", b=2)
    probT = sb("probT", 2 * T).rearrange("p (b n) -> p b n", b=2)
    sq = sb("sq", 2 * T).rearrange("p (b n) -> p b n", b=2)
    rms = sb("rms", T)
    small = sb("small", 320)
    ones = sb("ones", P)

    bank = [nc.alloc_psum_tensor(f"bank{i}", [P, T], F32).ap() for i in range(8)]

    def new(*names):
        made = [nc.alloc_semaphore(n) for n in names]
        return made if len(names) > 1 else made[0]

    consts_in, second_in, stored = new("consts_in", "second_in", "stored")
    w_in = [new(f"w_in{s}") for s in range(SLOTS)]
    moe_in = [new(f"moe_in{s}") for s in range(MOE_SLOTS)]
    met = {e: new(f"met_{e}") for e in ("pe", "act", "dve", "pool")}
    step_dve, step_act, for_act, for_dve = new("step_dve", "step_act", "for_act", "for_dve")
    sq_ready, sq_used, ms_ready, rms_ready, normed = new("sq_ready", "sq_used", "ms_ready", "rms_ready", "normed")
    high_ready, low_ready = new("high_ready", "low_ready")
    w_high, up_split, down_split = new("w_high", "up_split", "down_split")
    up_ready, silu_ready, gu_ready, down_ready, down_used = new("up_ready", "silu_ready", "gu_ready", "down_ready", "down_used")
    y_ready, y_copied = new("y_ready", "y_copied")
    prod_ready, taken_act, taken_dve = new("prod_ready", "taken_act", "taken_dve")
    rot_ready, cos_done, rope_done = new("rot_ready", "cos_done", "rope_done")
    fold_ready, fold_copied = new("fold_ready", "fold_copied")
    cmp_ready, cmp_bias, cmp_hid = new("cmp_ready", "cmp_bias", "cmp_hid")
    scores_ready, max_ready, probs_ready = new("scores_ready", "max_ready", "probs_ready")
    pT_ready, pT_copied, pv_ready, o_done = new("pT_ready", "pT_copied", "pv_ready", "o_done")
    share_used = new("share_used")
    scan_ready, fac_ready, qk_ready, off_ready, off_copied = new("scan_ready", "fac_ready", "qk_ready", "off_ready", "off_copied")
    diff_ready, decay_ready, lvl_ready, lvl_mm, lvl_put = new("diff_ready", "decay_ready", "lvl_ready", "lvl_mm", "lvl_put")
    keys_ready, diag_mm, diag_put, head_mm, head_out = new("keys_ready", "diag_mm", "diag_put", "head_mm", "head_out")
    logit_ready, logit_max, logit_exp, aff_ready = new("logit_ready", "logit_max", "logit_exp", "aff_ready")
    affT_ready, slotT_ready, slot_ready = new("affT_ready", "slotT_ready", "slot_ready")

    def view(at, n, **k):
        v = mix[:, at:at + n]
        return v.rearrange("p (a n) -> p a n", **k) if k else v

    def chunks(at, n):
        return view(at, n * T, a=n)

    cst = lambda at, n=1, r=slice(0, P): const[r, at:at + n]
    ident = cst(C_ID, P)
    mask16 = nc.alloc_sbuf_tensor("mask16", [P, 2 * P + NT * N_CMP], BF16).ap()
    ident16, tri16 = mask16[:, 0:P], mask16[:, P:2 * P]
    cmp16 = lambda i: mask16[:, 2 * P + i * N_CMP:2 * P + (i + 1) * N_CMP]
    col = lambda at, r=slice(0, P): cols[r, at:at + 1]

    QA, KA = chunks(0, 6), chunks(3072, 6)
    VA = view(6144, NT * 384, a=NT)
    CQ, CKV, KPE = chunks(7680, 2), chunks(8704, 1), chunks(9216, 1)
    QB, KB = chunks(9728, 3), chunks(11264, 4)
    VB = view(13312, NT * 256, a=NT)
    GATE = view(14336, NT * 18, a=NT)
    KCMP, VCMP, HID = view(14408, N_CMP), view(14440, 2 * 64, a=2), view(14568, 2 * N_CMP, a=2)
    QC, KCc = chunks(14640, 2), chunks(15664, 2)
    VC = view(16688, NT * 256, a=NT)
    assert 16688 + 1024 <= 18432
    LAM, CB = small[:, 0:4], small[:, 4:8]
    O = h.rearrange("p k t -> p (k t)").rearrange("p (i n) -> p i n", i=NT)
    OT = chunks(0, KC)
    SILU, GU = chunks(0, 2), chunks(1024, 2)
    parts = rounded("ffn_parts", "mix", 2048, 14336)
    W_UP = parts[:, 0:8192].rearrange("p (b s n) -> p b s n", b=2, s=2)
    W_DOWN = parts[:, 8192:12288].rearrange("p (b s n) -> p b s n", b=2, s=2)
    GU_PARTS = parts[:, 12288:14336].rearrange("p (b s n) -> p b s n", b=2, s=2)
    NM, RDEN, WGT = small[:, 8:12], small[:, 12:16], small[:, 16:20]
    DEN = small[:, 264:272]
    SCORES = [bank[n] for n in (0, 1, 6)]
    SUBSQ = view(4096, 2048)
    MS16 = small[:, 64:80]
    SLOTT = sq[:, 0]
    ANGLE = [[mix[:, 2560 + 1024 * n + 512 * q:3072 + 1024 * n + 512 * q] for q in range(2)] for n in range(3)]
    COS = [table[:, 1024 * n:1024 * n + 512] for n in range(3)]
    SIN = [table[:, 1024 * n + 512:1024 * n + 1024] for n in range(3)]

    QD, KD = chunks(0, 4), chunks(2048, 4)
    VD = view(4096, NT * 512, a=NT)
    HQ, ZF, ZB = chunks(6144, 4), chunks(8192, 4), chunks(10240, 4)
    VI, GG = view(12288, NT * 512, a=NT), view(14336, NT * 512, a=NT)
    Z = [ZF, ZB]
    K2 = [QD, KD]
    MM = view(4096, 2 * T, a=2)
    EE = view(5120, 2 * T, a=2)
    AT = view(16384, T, a=NT)
    QT = view(16896, T, a=NT)
    KT = view(17408, T, a=NT)
    KSUM = view(17920, T, a=NT)
    BC = prob.rearrange("p b n -> p (b n)")[:, 0:516].rearrange("p (i n) -> p i n", i=NT)
    DD = probT
    QX = sq.rearrange("p b n -> p (b n)")[:, 0:384].rearrange("p (i n) -> p i n", i=3)
    AO = [table[:, 0:768].rearrange("p (i n) -> p i n", i=6), table[:, 768:1536].rearrange("p (i n) -> p i n", i=6)]
    ET, LB, OMLB, LBT = small[:, 24:28], small[:, 32:40], small[:, 40:48], small[:, 48:56]
    XIN = view(0, 8192, a=KC)
    HTOK = view(8192, 4096, a=NT)
    GT = view(14336, 4096, a=8)
    SEL = h.rearrange("p k t -> p (k t)").rearrange("p (i n) -> p i n", i=NT)
    AFF = small[:, 128:192].rearrange("p (i e) -> p i e", i=NT)
    SLOT = small[:, 192:256].rearrange("p (i e) -> p i e", i=NT)
    RW = cols[:, COL_ROUTER:COL_ROUTER + KC * N_EXPERTS].rearrange("p (k e) -> p k e", k=KC)
    MOE_SLOT = [ring[:, s] for s in range(SLOTS)] + [table, h.rearrange("p k t -> p (k t)")[:, 0:ITEM],
                                                     view(8192, ITEM), view(8192 + ITEM, ITEM)]
    MG = sq
    MGU = probT
    YS = prob.rearrange("p b n -> p (b n)")

    def job(terms, p0, rows_, n, dst, scale=None, need=(), free=0, add=False):
        return dict(terms=terms, p0=p0, rows=rows_, n=n, dst=dst, scale=scale, need=need, free=free, add=add)

    def wslot(item, width):
        return ring[:, item % SLOTS, 0:KC * width].rearrange("p (k n) -> p k n", k=KC)

    def feat(item, width, c0, m, dst, p0=0, scale=None):
        w = wslot(item, width)
        return job([(w[:, k, c0:c0 + m], h[:, k, :]) for k in range(KC)], p0, m, T, dst, scale)

    def toks(item, width, c0, n, dsts):
        w = wslot(item, width)
        return [job([(h[:, k, i * P:(i + 1) * P], w[:, k, c0:c0 + n]) for k in range(KC)], 0, P, n, dsts[i]) for i in range(NT)]

    def with_items(jobs, item):
        jobs[0]["need"] = (item,)
        jobs[-1]["free"] = 1
        return jobs

    def project_one(b):
        r = []
        r += with_items([feat(b, 352, 0, 128, CQ[:, 0]), feat(b, 352, 128, 64, CQ[0:64, 1]),
                         feat(b, 352, 192, 128, CKV[:, 0]), feat(b, 352, 320, 32, KPE[64:96, 0], p0=64)], b)
        r += with_items([feat(b + 1, 384, 128 * j, 128, QB[:, j], scale=B_DH ** -0.5) for j in range(3)], b + 1)
        r += with_items([feat(b + 2, 384, 128 * j, 128, KB[:, j]) for j in range(3)], b + 2)
        r += with_items([feat(b + 3, 384, 0, 128, KB[:, 3])] + toks(b + 3, 384, 128, 256, [VB[:, i] for i in range(NT)]), b + 3)
        r += with_items([feat(b + 4, 274, 128 * j, 128, QC[:, j], scale=C_DH ** -0.5) for j in range(2)]
                        + toks(b + 4, 274, 256, 18, [GATE[:, i] for i in range(NT)]), b + 4)
        r += with_items([feat(b + 5, 256, 128 * j, 128, KCc[:, j]) for j in range(2)], b + 5)
        r += with_items(toks(b + 6, 256, 0, 256, [VC[:, i] for i in range(NT)]), b + 6)
        return r

    def project_mla(b):
        w = ring[:, (b + 7) % SLOTS, :]
        uq = w[:, 0:1152].rearrange("p (k n) -> p k n", k=2)
        ukv = w[:, 1152:1920].rearrange("p (m n) -> p m n", m=A_HEADS)
        r = []
        for m in range(A_HEADS):
            r.append(job([(uq[:, 0, 96 * m:96 * m + 96], CQ[:, 0]), (uq[0:64, 1, 96 * m:96 * m + 96], CQ[0:64, 1])],
                         0, 96, T, QA[0:96, m], scale=A_DK ** -0.5))
        for m in range(A_HEADS):
            r.append(job([(ukv[:, m, 0:64], CKV[:, 0])], 0, 64, T, KA[0:64, m]))
        for i in range(NT):
            r.append(job([(CKV[:, 0, i * P:(i + 1) * P], ukv[:, :, 64:128])], 0, P, 384, VA[:, i]))
        return with_items(r, b + 7)

    def project_out(b):
        r = []
        for n, width in enumerate((384, 384, 256)):
            w = wslot(b + n, width)
            r += with_items([job([(w[:, k, c:c + P], OT[:, k, :]) for k in range(KC)], 0, P, T, x[:, 3 * n + c // P], add=True)
                             for c in range(0, width, P)], b + n)
        return r

    def project_second(b):
        dst = [QD, KD, None, HQ, ZF, ZB, None, None]
        tok = {2: VD, 6: VI, 7: GG}
        r = []
        for n in range(11):
            jobs = []
            for c in range(384 * n, min(384 * n + 384, 4096), P):
                s, o = divmod(c, 512)
                width = 384 if n < 10 else 256
                if dst[s] is not None:
                    jobs.append(feat(b + n, width, c - 384 * n, P, dst[s][:, o // P]))
                else:
                    jobs += toks(b + n, width, c - 384 * n, P, [tok[s][:, i, o:o + P] for i in range(NT)])
            r += with_items(jobs, b + n)
        return r

    def unit(tiles, c0, mode, gate=None, bias=None):
        return dict(tiles=tiles, out=O[:, :, c0:c0 + 64], mode=mode, gate=gate, bias=bias)

    def causal(q, k, v):
        return [dict(q=q[:, i * P:(i + 1) * P], k=k[:, 0:(i + 1) * P], n=(i + 1) * P, mask=(tri16, i * P),
                     v=[v(j) for j in range(i + 1)], rows=P) for i in range(NT)]

    def mixer_units():
        r = []
        for m in range(A_HEADS):
            r.append(unit(causal(QA[0:96, m], KA[0:96, m], lambda j: VA[:, j, 64 * m:64 * m + 64]), 64 * m, "set"))
        for g in range(B_GROUPS):
            s = slice(64 * g, 64 * g + 64)
            for j in range(B_HPG):
                m = g * B_HPG + j
                c0 = 384 + 64 * m
                r.append(unit([dict(q=QB[s, j, i * P:(i + 1) * P], k=KCMP[s, :], n=N_CMP, mask=(cmp16(i), 0),
                                    v=[VCMP[0:N_CMP, g, :]], rows=N_CMP) for i in range(NT)], c0, "set", GATE[:, :, 3 * m]))
                for w in (1, 2):
                    r.append(unit(causal(QB[s, j], KB[s, 1 + w], lambda t: VB[:, t, 128 * (w - 1) + 64 * g:128 * (w - 1) + 64 * g + 64]),
                                  c0, "add", GATE[:, :, 3 * m + w]))
        for m in range(C_HEADS):
            for comp in range(2):
                r0 = 64 * (m % 2) + 32 * comp
                s = slice(r0, r0 + 32)
                r.append(unit(causal(QC[s, m // 2], KCc[s, m // 2], lambda j: VC[:, j, 64 * m:64 * m + 64]),
                              768 + 64 * m, "add" if comp else "set", LAM[:, 3:4].to_broadcast([P, NT]) if comp else None))
        return r

    def share_of(units, n):
        b = sum(u["mode"] == "add" for u in units[:n]) % 2
        return share[:, b].rearrange("p (i n) -> p i n", i=NT)

    def dilated_units():
        r = []
        for m in range(E_HEADS):
            s = slice(64 * (m % 2), 64 * (m % 2) + 64)
            r.append(unit([dict(q=QD[s, m // 2, i * P:(i + 1) * P], k=KD[s, m // 2], n=T, mask=None,
                                v=[VD[:, j, 64 * m:64 * m + 64] for j in range(NT)], rows=P) for i in range(NT)],
                          64 * m, "set", bias=m))
        return r

    HB = view(16384, 2 * 896, a=2)
    SB = sq

    def norm_x(at):
        return [dict(src=[x[:, k] for k in range(KC)], dst=[h[:, k] for k in range(KC)], gain=[col(at + k) for k in range(KC)],
                     rows=[P] * KC, ones=ones, width=D)]

    def norm_final():
        return [dict(norm_x(COL_FINAL)[0], dst=[x[:, k] for k in range(KC)])]

    def norm_mla(l):
        a = COL_MLAQ + 2 * l
        return [dict(src=[CQ[:, 0], CQ[0:64, 1]], dst=[CQ[:, 0], CQ[0:64, 1]], gain=[col(a), col(a + 1, slice(0, 64))],
                     rows=[P, 64], ones=ones, width=A_QR),
                dict(src=[CKV[:, 0]], dst=[CKV[:, 0]], gain=[col(COL_MLAKV + l)], rows=[P], ones=ones, width=128)]

    def norm_heads():
        return [dict(src=[X[:, j]], dst=[X[:, j]], gain=[col(g)], rows=[P], ones=cst(C_BLK, P), width=64)
                for X, g in ((QD, COL_DQ), (KD, COL_DK)) for j in range(4)]

    def ropes_first():
        r = [(QB[:, j], cst(C_RB, P), COS[1], SIN[1]) for j in range(3)]
        r += [(KB[:, j], cst(C_RB, P), COS[1], SIN[1]) for j in (0, 2, 3)]
        r += [(X[:, j], cst(C_RC, P), COS[2], SIN[2]) for X in (QC, KCc) for j in range(2)]
        s = slice(64, 96)
        r += [(KPE[s, 0], const[s, C_RA + 64:C_RA + 96], COS[0][s, :], SIN[0][s, :])]
        return r

    def ropes_mla():
        s = slice(0, 96)
        return [(QA[s, m], const[s, C_RA:C_RA + 96], COS[0][s, :], SIN[0][s, :]) for m in range(A_HEADS)]

    def meet(e, c, own):
        e.drain().then_inc(met[own], c.one(met[own]))
        for s in met.values():
            e.wait_ge(s, c.own[met[own].name])


    PAIRS = [[(1, 0), (2, 1), (3, 2), (2, 0), (3, 1), (3, 0)], [(0, 1), (1, 2), (2, 3), (0, 2), (1, 3), (0, 3)]]

    def cum(d):
        o = 1 - d
        return BC[:, :, o:o + P]

    def halves(buf, m):
        v = buf.rearrange("p (j w) -> p j w", w=2 * m)
        return v[:, :, 0:m], v[:, :, m:2 * m]

    def gathered():
        return [job([(HTOK[:, i, P * q:P * q + P], SEL[:, i, 512 * s:512 * s + 512]) for i in range(NT)],
                    0, P, 512, XIN[:, q, 512 * s:512 * s + 512]) for q in range(KC) for s in range(2)]

    block_cm = nc.Block()
    block = block_cm.__enter__()
    per_layer = 2 * FFN_ITEMS + MIX_ITEMS
    base_second = LAYERS * per_layer
    base_moe = base_second + SECOND_ITEMS
    STAGES_BEFORE_ROUTER = 2 + 13 * LAYERS + 11
    STAGES_BEFORE_MOE = STAGES_BEFORE_ROUTER + 5
    assert base_moe % SLOTS == 0

    released, counts = [], {}

    def release(sem_, n):
        counts[sem_.name] = counts.get(sem_.name, 0) + n
        return sem_, counts[sem_.name]

    def release_jobs(jobs):
        for j in jobs:
            r = release(prod_ready, 1)
            if j["free"]:
                released.append(r)

    for l in range(LAYERS):
        released += [release(down_split, 1) for n in range(FFN_ITEMS)]
        release_jobs(project_one(0))
        release_jobs(project_mla(0))
        released += [release(cmp_ready, 2 * B_GROUPS + 1)] * 2
        release_jobs(project_out(0))
        released += [release(down_split, 1) for n in range(FFN_ITEMS)]
    release_jobs(project_second(0))
    release_jobs(project_out(0))
    assert len(released) == base_moe

    @block.sync
    def _(sp):
        for dst, src in ((cols, cols_in), (rows, rows_in), (const, const_in)):
            sp.dma_start(dst, src).then_inc(consts_in, 16)
        sp.dma_start(x, x_in).then_inc(consts_in, 16)
        sp.dma_start(mix[:, 0:T].bitcast(I32), pos_in).then_inc(consts_in, 16)

        def load(n, src):
            if n >= SLOTS:
                sp.wait_ge(*released[n - SLOTS])
            sp.dma_start(ring[:, n % SLOTS, :], src).then_inc(w_in[n % SLOTS], 16)

        def load_loop(n, src, trips):
            with sp.Fori(1, 1 + trips) as i:
                for r in range(SLOTS):
                    done, v = released[n + r]
                    each = released[n + r + 1][1] - v
                    sp.wait_ge(done, (i - 1) * (SLOTS * each) + v)
                    sp.dma_start(ring[:, (n + r) % SLOTS, :],
                                 src[bass.ds(i * SLOTS + r, 1)].rearrange("a p n -> (a p) n")).then_inc(w_in[(n + r) % SLOTS], 16)

        def load_ffn(n, src):
            for r in range(SLOTS):
                load(n + r, src[r])
            load_loop(n, src, FFN_TRIPS)
            for r in range(SLOTS * (FFN_TRIPS + 1), FFN_ITEMS):
                load(n + r, src[r])

        for l in range(LAYERS):
            b = l * per_layer
            load_ffn(b, ffn_w[2 * l])
            for r in range(MIX_ITEMS):
                load(b + FFN_ITEMS + r, mix_w[l, r])
            load_ffn(b + FFN_ITEMS + MIX_ITEMS, ffn_w[2 * l + 1])
        for r in range(SECOND_ITEMS):
            load(base_second + r, second_w[r])
        for r in range(MOE_SLOTS):
            if r < SLOTS:
                sp.wait_ge(*released[base_moe + r - SLOTS])
            elif r == SLOTS:
                sp.wait_ge(met["dve"], STAGES_BEFORE_ROUTER)
            elif r == SLOTS + 1:
                for s in met.values():
                    sp.wait_ge(s, STAGES_BEFORE_MOE)
            sp.dma_start(MOE_SLOT[r], moe_w[r]).then_inc(moe_in[r], 16)
        with sp.Fori(1, N_EXPERTS * MOE_ITEMS // MOE_SLOTS) as i:
            for r in range(MOE_SLOTS):
                sp.wait_ge(y_ready, i * MOE_SLOTS + (r + 1 - MOE_SLOTS))
                sp.dma_start(MOE_SLOT[r], moe_w[bass.ds(i * MOE_SLOTS + r, 1)].rearrange("a p n -> (a p) n")).then_inc(moe_in[r], 16)
        sp.wait_ge(down_used, LAYERS * 2 * FFN_ITEMS * KC + (N_EXPERTS // 2) * KC)
        sp.dma_start(out, x).then_inc(stored, 16)
        sp.wait_ge(stored, 16)

    @block.gpsimd
    def _(pool):
        c = Count()
        pool.memset(ones, 1.0)
        pool.wait_ge(consts_in, 80)
        meet(pool, c, "pool")
        meet(pool, c, "pool")

        def ropes(list_):
            for X, R, cos, sin in list_:
                pool.wait_ge(cos_done, c.made(cos_done))
                pool.wait_ge(rot_ready, c.next(rot_ready))
                pool.tensor_tensor(X, X, cos, ALU.mult).then_inc(cos_done, c.one(cos_done))

        def low_parts():
            for k in range(KC):
                pool.wait_ge(high_ready, c.next(high_ready))
                pool.tensor_tensor(h_lo[:, k], prob[:, k % 2], h_hi[:, k].bitcast(F32), ALU.subtract).then_inc(low_ready, 1)

        def ffn(base, norm_stage=False):
            def up_low(n):
                w, s = ring[:, (base + n) % SLOTS, 0:2048], W_UP[:, n % 2]
                pool.wait_ge(w_high, c.next(w_high))
                pool.tensor_tensor(s[:, 1], w, s[:, 0].bitcast(F32), ALU.subtract).then_inc(up_split, 1)

            def down_low(n):
                w, s = ring[:, (base + n) % SLOTS, 2048:3072], W_DOWN[:, n % 2]
                pool.wait_ge(w_high, c.next(w_high))
                pool.tensor_tensor(s[:, 1], w, s[:, 0].bitcast(F32), ALU.subtract).then_inc(down_split, 1)

            if norm_stage:
                up_low(0)
                low_parts()
                up_low(1)
                down_low(0)
                return
            for n in range(SLOTS):
                up_low(n + 2)
                down_low(n + 1)
            with pool.Fori(0, FFN_TRIPS) as i:
                c.loop(i, {w_high: 2 * SLOTS})
                for r in range(SLOTS):
                    up_low(r + 2)
                    down_low(r + 1)
                c.looped(FFN_TRIPS)
            for n in range(SLOTS * (FFN_TRIPS + 1), FFN_ITEMS - 1):
                if n + 2 < FFN_ITEMS:
                    up_low(n + 2)
                down_low(n + 1)

        for l in range(LAYERS):
            b = l * per_layer
            ffn(b, norm_stage=True)
            meet(pool, c, "pool")
            ffn(b)
            for stage in ("FFN", "norm", "projections"):
                meet(pool, c, "pool")
            ropes(ropes_first())
            meet(pool, c, "pool")
            for m in range(A_HEADS):
                pool.tensor_copy(KA[64:96, m], KPE[64:96, 0])
            meet(pool, c, "pool")
            ropes(ropes_mla())
            meet(pool, c, "pool")
            units = mixer_units()
            for n, u in enumerate(units):
                if u["mode"] == "set":
                    c.skip(o_done)
                    continue
                pool.wait_ge(o_done, c.next(o_done))
                pool.wait_ge(share_used, c.made(share_used))
                pool.tensor_tensor(u["out"], u["out"], share_of(units, n), ALU.add).then_inc(share_used, c.one(share_used))
            for stage in ("attention", "sub-norm", "transposes", "output projection"):
                meet(pool, c, "pool")
            ffn(b + FFN_ITEMS + MIX_ITEMS, norm_stage=True)
            meet(pool, c, "pool")
            ffn(b + FFN_ITEMS + MIX_ITEMS)
            meet(pool, c, "pool")
        pool.dma_start(table[:, 0:N_CONST2], const2_in).then_inc(second_in, 16)
        pool.wait_ge(second_in, 16)
        for stage in ("final norm", "norm", "projections", "head norms", "attention", "gates"):
            meet(pool, c, "pool")
        for m in range(H_HEADS):
            pool.wait_ge(head_mm, c.next(head_mm, 1, lag=1))
            pool.memset(AT, 0.0).then_inc(keys_ready, 1)
            pool.tensor_tensor(KSUM, K2[0][:, m].rearrange("p (i n) -> p i n", i=NT),
                               K2[1][:, m].rearrange("p (i n) -> p i n", i=NT), ALU.add).then_inc(keys_ready, 1)
        for stage in ("HGRN2", "out norm", "transposes", "output projection", "norm", "router", "selection",
                      "gather", "scatter matrices", "transposes", "experts"):
            meet(pool, c, "pool")

    @block.scalar
    def _(act):
        c = Count()
        meet(act, c, "act")

        def arrived(n):
            act.wait_ge(w_in[n % SLOTS], c.next(w_in[n % SLOTS], 16))

        def up_high(base, n):
            arrived(base + n)
            act.activation(W_UP[:, n % 2, 0], ring[:, (base + n) % SLOTS, 0:2048], ACT.Copy).then_inc(w_high, 1)

        def down_high(base, n):
            act.wait_ge(down_ready, c.next(down_ready, KC, lag=2 * KC))
            act.activation(W_DOWN[:, n % 2, 0], ring[:, (base + n) % SLOTS, 2048:3072], ACT.Copy).then_inc(w_high, 1)

        def norm(groups, first=None):
            for g in groups:
                for s, r in zip(g["src"], g["rows"]):
                    b = c.own.get(sq_ready.name, 0) % 2
                    act.wait_ge(sq_used, c.next(sq_used, 1, lag=2))
                    act.activation(sq[0:r, b], s, ACT.Square).then_inc(sq_ready, c.one(sq_ready))
                if first is not None:
                    up_high(first, 0)
                act.wait_ge(ms_ready, c.next(ms_ready))
                act.activation(rms, rms, ACT.Sqrt).then_inc(rms_ready, 1)
            for k in range(0 if first is None else KC):
                act.wait_ge(normed, c.next(normed))
                act.activation(h_hi[:, k], prob[:, k % 2], ACT.Copy).then_inc(high_ready, 1)
            if first is not None:
                up_high(first, 1)
                down_high(first, 0)

        def gemm(jobs):
            for n, j in enumerate(jobs):
                if n % 2:
                    c.skip(prod_ready)
                    continue
                act.wait_ge(prod_ready, c.next(prod_ready))
                act.activation(j["dst"], bank[n % 4][j["p0"]:j["p0"] + j["rows"], 0:j["n"]], ACT.Copy,
                               scale=j["scale"] or 1.0).then_inc(taken_act, 1)

        def transposed(dst):
            for q in range(KC):
                act.wait_ge(fold_ready, c.next(fold_ready))
                act.activation(dst[q], bank[4 + q % 2], ACT.Copy).then_inc(fold_copied, 1)

        def ffn(base):
            def silu(n):
                act.wait_ge(gu_ready, c.next(gu_ready, lag=2))
                act.wait_ge(up_ready, c.next(up_ready))
                act.activation(SILU[:, n % 2], bank[n % 2], ACT.Silu).then_inc(silu_ready, 1)

            for n in range(SLOTS):
                silu(n)
                up_high(base, n + 2)
                down_high(base, n + 1)
            with act.Fori(0, FFN_TRIPS) as i:
                c.loop(i, {gu_ready: SLOTS, up_ready: SLOTS, down_ready: SLOTS * KC, **{s: 16 for s in w_in}})
                for r in range(SLOTS):
                    silu(r)
                    up_high(base, r + 2)
                    down_high(base, r + 1)
                c.looped(FFN_TRIPS)
            for n in range(SLOTS * (FFN_TRIPS + 1), FFN_ITEMS):
                silu(n)
                if n + 2 < FFN_ITEMS:
                    up_high(base, n + 2)
                if n + 1 < FFN_ITEMS:
                    down_high(base, n + 1)

        def attention(units):
            for a in range(NT * len(units)):
                u, n = units[a // NT], units[a // NT]["tiles"][a % NT]["n"]
                act.wait_ge(max_ready, c.next(max_ready))
                act.wait_ge(pT_ready, c.next(pT_ready, lag=3))
                src = SB[:, a % 2, 0:n] if u["bias"] is not None else SCORES[a % 3][:, 0:n]
                act.activation(prob[:, a % 3, 0:n], src, ACT.Exp, bias=NM[:, a % 4:a % 4 + 1],
                               accum_out=DEN[:, a % 8:a % 8 + 1]).then_inc(probs_ready, 1)

        def root(v):
            act.wait_ge(for_act, c.next(for_act))
            act.activation(v, v, ACT.Sqrt).then_inc(for_dve, 1)

        for n in range(3):
            for q in range(2):
                act.wait_ge(for_act, c.next(for_act))
                act.activation((SIN, COS)[q][n], ANGLE[n][q], ACT.Sin)
        meet(act, c, "act")

        for l in range(LAYERS):
            b = l * per_layer
            norm(norm_x(COL_FFN1 + 8 * l), first=b)
            meet(act, c, "act")
            ffn(b)
            for n in range(b + FFN_ITEMS, b + FFN_ITEMS + MIX_ITEMS):
                c.skip(w_in[n % SLOTS], 16)
            meet(act, c, "act")
            norm(norm_x(COL_MIX + 8 * l))
            meet(act, c, "act")
            gemm(project_one(0))
            meet(act, c, "act")
            norm(norm_mla(l))
            c.skip(normed, KC + 3)
            act.wait_ge(for_act, c.next(for_act))
            act.activation(LAM[:, 0:2], LAM[:, 0:2], ACT.Exp).then_inc(for_dve, 1)
            act.activation(GATE, GATE, ACT.Sigmoid).then_inc(for_dve, 1)
            meet(act, c, "act")
            gemm(project_mla(0))
            meet(act, c, "act")
            for part in range(2):
                for g in range(B_GROUPS):
                    s = slice(64 * g, 64 * g + 64)
                    act.wait_ge(cmp_bias, c.next(cmp_bias))
                    act.activation(HID[s, part], bank[4 + 2 * part + g][s, 0:N_CMP], ACT.Silu,
                                   bias=CB[s, part:part + 1]).then_inc(cmp_hid, 1)
            meet(act, c, "act")
            attention(mixer_units())
            meet(act, c, "act")
            root(MS16)
            meet(act, c, "act")
            transposed([OT[:, q] for q in range(KC)])
            meet(act, c, "act")
            c.skip(prod_ready, KC)
            meet(act, c, "act")
            norm(norm_x(COL_FFN2 + 8 * l), first=b + FFN_ITEMS + MIX_ITEMS)
            meet(act, c, "act")
            ffn(b + FFN_ITEMS + MIX_ITEMS)
            meet(act, c, "act")
        norm(norm_final())
        meet(act, c, "act")
        norm(norm_x(COL_N1))
        meet(act, c, "act")
        gemm(project_second(0))
        meet(act, c, "act")
        norm(norm_heads())
        meet(act, c, "act")
        attention(dilated_units())
        meet(act, c, "act")

        act.wait_ge(for_act, c.next(for_act))
        act.activation(LBT, LBT, ACT.Exp).then_inc(for_dve, 1)
        for d in range(2):
            act.activation(K2[d], Z[d], ACT.Sigmoid, scale=-1.0).then_inc(step_act, c.one(step_act))
        act.wait_ge(step_act, c.made(step_act))
        for d in range(2):
            act.activation(Z[d], Z[d], ACT.Sigmoid).then_inc(for_dve, 1)
        act.activation(HQ, HQ, ACT.Silu)
        act.activation(GG, GG, ACT.Silu)
        for d in range(2):
            act.wait_ge(for_act, c.next(for_act))
            act.activation(Z[d], Z[d], ACT.Ln)
        meet(act, c, "act")

        for m in range(H_HEADS):
            for d in range(2):
                act.wait_ge(lvl_ready, c.next(lvl_ready, 0))
                act.wait_ge(scan_ready, c.next(scan_ready))
                act.activation(EE[:, 0].rearrange("p (i n) -> p i n", i=NT), cum(d), ACT.Exp)
                act.activation(ET, BC[:, :, P], ACT.Exp)
                act.wait_ge(diff_ready, c.next(diff_ready))
                act.activation(EE[:, 1], DD[:, 0], ACT.Exp).then_inc(fac_ready, 1)
                act.wait_ge(off_ready, c.next(off_ready))
                if m and d == 0:
                    act.wait_ge(head_mm, c.next(head_mm, 0))
                act.activation(AO[d][:, 0:3].rearrange("p i n -> p (i n)"), bank[0][:, 0:384], ACT.Copy)
                act.activation(AO[d][:, 3:6].rearrange("p i n -> p (i n)"), bank[1][:, 0:384], ACT.Copy).then_inc(off_copied, 1)
                for n, w in enumerate(LEVELS):
                    act.wait_ge(diff_ready, c.next(diff_ready))
                    act.wait_ge(lvl_ready, c.next(lvl_ready, 1, lag=2))
                    for src, dst, sign in zip(halves(DD[:, n % 2], w), halves(EE[:, n % 2], w), (-1.0, 1.0)):
                        last = act.activation(dst, src, ACT.Exp, scale=sign)
                    last.then_inc(decay_ready, 1)
            act.wait_ge(head_mm, c.next(head_mm))
            act.activation(O[:, :, 512 + P * m:512 + P * m + P], bank[7].rearrange("p (i n) -> p i n", i=NT),
                           ACT.Copy).then_inc(head_out, 1)
        meet(act, c, "act")
        root(MS16)
        meet(act, c, "act")
        transposed([OT[:, q] for q in range(KC)])
        meet(act, c, "act")
        meet(act, c, "act")
        norm(norm_x(COL_N2))
        meet(act, c, "act")
        act.wait_ge(logit_max, c.next(logit_max))
        for i in range(NT):
            act.activation(AFF[:, i], bank[0][:, 16 * i:16 * i + 16], ACT.Exp, bias=NM[:, i:i + 1],
                           accum_out=DEN[:, i:i + 1]).then_inc(logit_exp, 1)
        transposed([HTOK[:, :, P * q:P * q + P] for q in range(KC)])
        meet(act, c, "act")
        meet(act, c, "act")
        c.skip(prod_ready, KC)
        gemm(gathered())
        meet(act, c, "act")
        meet(act, c, "act")
        transposed([GT[:, q] for q in range(KC)])
        meet(act, c, "act")
        with act.Fori(0, N_EXPERTS // 2) as i:
            c.loop(i, {gu_ready: 16, up_ready: 16, y_ready: 16})
            for n in range(16):
                act.wait_ge(gu_ready, c.next(gu_ready, 1, lag=2))
                act.wait_ge(up_ready, c.next(up_ready))
                act.activation(MG[:, n % 2, 0:64], bank[n % 2][:, 0:64], ACT.Silu).then_inc(silu_ready, 1)
            act.wait_ge(y_ready, c.next(y_ready, 16))
            act.activation(YS[:, 0:T], bank[2], ACT.Copy).then_inc(y_copied, 1)
            c.looped(N_EXPERTS // 2)
        meet(act, c, "act")

    @block.tensor
    def _(pe):
        c = Count()
        mm = nc.tensor.matmul
        meet(pe, c, "pe")
        meet(pe, c, "pe")

        def norm(groups):
            for g in groups:
                pe.wait_ge(ms_ready, c.next(ms_ready, 1, lag=1))
                for k, (s, r) in enumerate(zip(g["src"], g["rows"])):
                    b = c.at.get(sq_ready.name, 0) % 2
                    pe.wait_ge(sq_ready, c.next(sq_ready))
                    mm(bank[7], g["ones"][0:r, :], sq[0:r, b], start=k == 0, stop=k == len(g["src"]) - 1).then_inc(sq_used, 1)

        def arrived(n):
            pe.wait_ge(w_in[n % SLOTS], c.next(w_in[n % SLOTS], 16))

        def gemm(jobs, split=True):
            for n, j in enumerate(jobs):
                for item in j["need"]:
                    arrived(item)
                if split:
                    taken = (taken_act, taken_dve)[n % 2]
                    pe.wait_ge(taken, c.next(taken, 1, lag=2))
                else:
                    pe.wait_ge(taken_dve, c.next(taken_dve, 1, lag=4))
                o = bank[n % 4][j["p0"]:j["p0"] + j["rows"], 0:j["n"]]
                for k, (w, r) in enumerate(j["terms"]):
                    last = mm(o, w, r, start=k == 0, stop=k == len(j["terms"]) - 1)
                last.then_inc(prod_ready, 1)

        def transposed(src):
            for q in range(KC):
                pe.wait_ge(fold_copied, c.next(fold_copied, 1, lag=2))
                for i in range(NT):
                    last = nc.tensor.transpose(bank[4 + q % 2][:, P * i:P * i + P], src(q, i), ident)
                last.then_inc(fold_ready, 1)

        def ropes(list_):
            for n, (X, R, cos, sin) in enumerate(list_):
                pe.wait_ge(rope_done, c.next(rope_done, 1, lag=4))
                p0, r = X.start_partition(), X.shape[0]
                mm(bank[n % 4][p0:p0 + r, :], R, X, start=True, stop=True).then_inc(rot_ready, 1)

        def ffn(base):
            for n in range(FFN_ITEMS):
                c.skip(w_in[(base + n) % SLOTS], 16)

            def up(n):
                pe.wait_ge(up_split, c.next(up_split))
                w = W_UP[:, n % 2].rearrange("p s (a k n) -> p s a k n", a=2, k=KC)
                for a in range(2):
                    for k in range(KC):
                        mm(bank[n % 2 + 2 * a], w[:, 0, a, k], h_lo[:, k], start=k == 0, stop=False)
                        mm(bank[n % 2 + 2 * a], w[:, 0, a, k], h_hi[:, k], start=False, stop=False)
                        last = mm(bank[n % 2 + 2 * a], w[:, 1, a, k], h_hi[:, k], start=False, stop=k == KC - 1)
                last.then_inc(up_ready, 1)

            def down(n):
                w, g = W_DOWN[:, n % 2], GU_PARTS[:, n % 2]
                pe.wait_ge(down_split, c.next(down_split))
                pe.wait_ge(gu_ready, c.next(gu_ready))
                for q in range(KC):
                    pe.wait_ge(down_used, c.next(down_used, 1, lag=4))
                    mm(bank[4 + q % 4], w[:, 0, P * q:P * q + P], g[:, 1], start=True, stop=False)
                    mm(bank[4 + q % 4], w[:, 0, P * q:P * q + P], g[:, 0], start=False, stop=False)
                    mm(bank[4 + q % 4], w[:, 1, P * q:P * q + P], g[:, 0], start=False, stop=True).then_inc(down_ready, 1)

            up(0)
            for n in range(SLOTS):
                up(n + 1)
                down(n)
            with pe.Fori(0, FFN_TRIPS) as i:
                c.loop(i, {gu_ready: SLOTS, down_used: SLOTS * KC, up_split: SLOTS, down_split: SLOTS})
                for r in range(SLOTS):
                    up(r + 1)
                    down(r)
                c.looped(FFN_TRIPS)
            for n in range(SLOTS * (FFN_TRIPS + 1), FFN_ITEMS):
                if n + 1 < FFN_ITEMS:
                    up(n + 1)
                down(n)

        def attention(units):
            tiles = [t for u in units for t in u["tiles"]]

            def scores(a):
                t = tiles[a]
                o = SCORES[a % 3]
                last = mm(o[:, 0:t["n"]], t["q"], t["k"], start=True, stop=True)
                if t["mask"] is not None:
                    m, at = t["mask"]
                    last = mm(o[:, at:at + m.shape[1]], ident16, m, start=False, stop=True, skip_group_check=True)
                last.then_inc(scores_ready, 1)

            def turn(a):
                t = tiles[a]
                pe.wait_ge(probs_ready, c.next(probs_ready))
                for j in range(len(t["v"])):
                    last = nc.tensor.transpose(bank[2 + a % 2][0:t["rows"], P * j:P * j + P],
                                               prob[:, a % 3, P * j:P * j + t["rows"]], ident)
                last.then_inc(pT_ready, 1)

            def values(a):
                t = tiles[a]
                o = bank[4 + a // NT % 2][:, 64 * (a % NT):64 * (a % NT) + 64]
                pe.wait_ge(pT_copied, c.next(pT_copied))
                if a % NT == 0:
                    pe.wait_ge(o_done, c.next(o_done, lag=2))
                for j, v in enumerate(t["v"]):
                    last = mm(o, probT[0:t["rows"], a % 2, P * j:P * j + P], v, start=j == 0, stop=j == len(t["v"]) - 1)
                last.then_inc(pv_ready, 1)

            for a in range(len(tiles) + 3):
                if a < len(tiles):
                    scores(a)
                if 0 <= a - 2 < len(tiles):
                    turn(a - 2)
                if a >= 3:
                    values(a - 3)

        for l in range(LAYERS):
            b = l * per_layer
            norm(norm_x(COL_FFN1 + 8 * l))
            meet(pe, c, "pe")
            ffn(b)
            meet(pe, c, "pe")
            b += FFN_ITEMS
            norm(norm_x(COL_MIX + 8 * l))
            meet(pe, c, "pe")
            gemm(project_one(b))
            meet(pe, c, "pe")
            norm(norm_mla(l))
            ropes(ropes_first())
            meet(pe, c, "pe")
            gemm(project_mla(b))
            meet(pe, c, "pe")
            ropes(ropes_mla())
            w = [ring[:, (b + 8 + part) % SLOTS, :] for part in range(2)]
            for part in range(2):
                arrived(b + 8 + part)
                for g in range(B_GROUPS):
                    s = slice(64 * g, 64 * g + 64)
                    o = bank[4 + 2 * part + g]
                    for i in range(CMP_LEN):
                        mm(o[s, 0:N_CMP], w[part][s, 64 * i:64 * i + 64], KB[s, part, i:i + CMP_STRIDE * (N_CMP - 1) + 1:CMP_STRIDE],
                           start=i == 0, stop=i == CMP_LEN - 1)
                    pe0 = COL_PE + (2 * l + part) * CMP_LEN
                    for i in range(CMP_LEN):
                        last = mm(o[s, 32:33], w[part][s, 64 * i:64 * i + 64], cols[s, pe0 + i:pe0 + i + 1],
                                  start=i == 0, stop=i == CMP_LEN - 1)
                    last.then_inc(cmp_ready, 1)
            pe.wait_ge(cmp_hid, c.next(cmp_hid, 4))
            for g in range(B_GROUPS):
                s = slice(64 * g, 64 * g + 64)
                mm(bank[4][s, 64:64 + N_CMP], w[0][s, 2048:2112], HID[s, 0], start=True, stop=True)
                last = mm(bank[5 + g][0:N_CMP, 64:128], HID[s, 1], w[1][s, 2048:2112], start=True, stop=True)
            last.then_inc(cmp_ready, 1)
            meet(pe, c, "pe")
            attention(mixer_units())
            meet(pe, c, "pe")
            meet(pe, c, "pe")
            transposed(lambda q, i: O[:, i, P * q:P * q + P])
            meet(pe, c, "pe")
            gemm(project_out(b + 10), split=False)
            meet(pe, c, "pe")
            norm(norm_x(COL_FFN2 + 8 * l))
            meet(pe, c, "pe")
            ffn(b + MIX_ITEMS)
            meet(pe, c, "pe")
        norm(norm_final())
        meet(pe, c, "pe")
        norm(norm_x(COL_N1))
        meet(pe, c, "pe")
        gemm(project_second(base_second))
        meet(pe, c, "pe")
        norm(norm_heads())
        meet(pe, c, "pe")
        attention(dilated_units())
        meet(pe, c, "pe")
        meet(pe, c, "pe")

        for m in range(H_HEADS):
            for d in range(2):
                pe.wait_ge(qk_ready, c.next(qk_ready))
                pe.wait_ge(off_copied, c.next(off_copied, 1, lag=1))
                for n, (I, J) in enumerate(PAIRS[d]):
                    q = QT[:, I] if n < 3 else QX[:, n - 3]
                    last = mm(bank[n // 3][:, P * (n % 3):P * (n % 3) + P], KT[:, J], q, start=True, stop=True)
                last.then_inc(off_ready, 1)
                for n, w in enumerate(LEVELS):
                    pe.wait_ge(lvl_ready, c.next(lvl_ready))
                    pe.wait_ge(lvl_put, c.next(lvl_put, 1, lag=2))
                    for i in range(NT):
                        blk = MM[:, n % 2, P * i:P * i + P]
                        last = mm(bank[2 + n % 2][:, 64 * i:64 * i + 64], blk, halves(blk, w)[1 - d], start=True, stop=True)
                    last.then_inc(lvl_mm, 1)
            pe.wait_ge(keys_ready, c.next(keys_ready, 2))
            for i in range(NT):
                last = mm(bank[6][:, P * i:P * i + P], KSUM[:, i], HQ[:, m, P * i:P * i + P], start=True, stop=True)
            last.then_inc(diag_mm, 1)
            pe.wait_ge(diag_put, c.next(diag_put))
            pe.wait_ge(off_copied, c.next(off_copied, 0))
            pe.wait_ge(head_out, c.next(head_out, 1, lag=1))
            for I in range(NT):
                terms = [(AT[:, I], I)] + [(AO[d][:, n], J) for d in range(2) for n, (i, J) in enumerate(PAIRS[d]) if i == I]
                for k, (w, J) in enumerate(terms):
                    last = mm(bank[7][:, P * I:P * I + P], w, VI[:, J, P * m:P * m + P], start=k == 0, stop=k == len(terms) - 1)
            last.then_inc(head_mm, 1)
        meet(pe, c, "pe")
        meet(pe, c, "pe")
        transposed(lambda q, i: O[:, i, P * q:P * q + P])
        meet(pe, c, "pe")
        gemm(project_out(base_second + 11), split=False)
        meet(pe, c, "pe")
        norm(norm_x(COL_N2))
        meet(pe, c, "pe")
        for i in range(NT):
            for k in range(KC):
                last = mm(bank[0][:, 16 * i:16 * i + 16], h[:, k, P * i:P * i + P], RW[:, k, :], start=k == 0, stop=k == KC - 1)
        last.then_inc(logit_ready, 1)
        transposed(lambda q, i: h[:, q, P * i:P * i + P])
        pe.wait_ge(aff_ready, c.next(aff_ready))
        for i in range(NT):
            last = nc.tensor.transpose(bank[1][0:16, P * i:P * i + P], AFF[:, i], ident)
        last.then_inc(affT_ready, 1)
        pe.wait_ge(slotT_ready, c.next(slotT_ready))
        for i in range(NT):
            last = nc.tensor.transpose(bank[2][:, 16 * i:16 * i + 16], SLOTT[0:16, P * i:P * i + P], ident[0:16, 0:16])
        last.then_inc(slot_ready, 1)
        meet(pe, c, "pe")
        meet(pe, c, "pe")
        gemm(gathered())
        meet(pe, c, "pe")
        meet(pe, c, "pe")
        transposed(lambda q, i: SEL[:, i, P * q:P * q + P])
        meet(pe, c, "pe")
        with pe.Fori(0, N_EXPERTS // 2) as i:
            c.loop(i, {gu_ready: 16, y_copied: 2, down_used: KC, **{s: 32 for s in moe_in}})

            def up(n):
                pe.wait_ge(moe_in[n % MOE_SLOTS], c.next(moe_in[n % MOE_SLOTS], 16))
                w = MOE_SLOT[n % MOE_SLOTS][:, 0:2048].rearrange("p (a k n) -> p a k n", a=2, k=KC)
                for a in range(2):
                    for k in range(KC):
                        last = mm(bank[n % 2][:, 64 * a:64 * a + 64], w[:, a, k, :],
                                  XIN[:, k, bass.ds(i * P + 64 * (n // MOE_ITEMS), 64)], start=k == 0, stop=k == KC - 1)
                last.then_inc(up_ready, 1)

            up(0)
            for n in range(16):
                if n < 15:
                    up(n + 1)
                e = n // MOE_ITEMS
                pe.wait_ge(gu_ready, c.next(gu_ready))
                for s in range(2):
                    last = mm(bank[2 + s][64 * e:64 * e + 64, :], MGU[:, n % 2, 0:64],
                              MOE_SLOT[n % MOE_SLOTS][:, 2048 + 512 * s:2560 + 512 * s], start=n % 8 == 0, stop=n % 8 == 7)
                last.then_inc(y_ready, 1)
            pe.wait_ge(y_copied, c.next(y_copied, 2))
            for q in range(KC):
                pe.wait_ge(down_used, c.next(down_used, 1, lag=4))
                mm(bank[4 + q % 4], YS[:, P * q:P * q + P], GT[:, bass.ds(i, 1), :].rearrange("p a n -> p (a n)"),
                   start=True, stop=True).then_inc(down_ready, 1)
            c.looped(N_EXPERTS // 2)
        meet(pe, c, "pe")

    @block.vector
    def _(dve):
        c = Count()
        V = nc.vector
        meet(dve, c, "dve")

        def step(ins):
            ins.then_inc(step_dve, c.one(step_dve))
            dve.wait_ge(step_dve, c.made(step_dve))

        V.tensor_copy(ident16, ident)
        V.tensor_copy(tri16, cst(C_TRI, P))
        V.tensor_copy(mask16[:, 2 * P:], cst(C_CMP, NT * N_CMP))
        posf, ang, rnd, tmp = (mix[:, 512 * n:512 * n + 512] for n in range(1, 5))
        step(V.tensor_copy(posf, mix[:, 0:T].bitcast(I32)))
        for n in range(3):
            s, k = ANGLE[n]
            step(V.tensor_scalar(ang, posf, cst(C_INV + n), None, ALU.mult))
            step(V.tensor_scalar(rnd, ang, 1 / (2 * math.pi), ROUND, ALU.mult, ALU.add))
            step(V.tensor_scalar(rnd, rnd, -ROUND, None, ALU.add))
            for part in TWO_PI:
                step(V.scalar_tensor_tensor(ang, rnd, -part, ang, ALU.mult, ALU.add))
            step(V.tensor_scalar(tmp, ang, math.pi / 2, None, ALU.add))
            step(V.tensor_scalar(rnd, tmp, math.pi, -2 * math.pi, ALU.is_gt, ALU.mult))
            step(V.tensor_tensor(tmp, tmp, rnd, ALU.add))
            V.tensor_scalar(s, ang, SIN_MAX, -SIN_MAX, ALU.min, ALU.max).then_inc(for_act, 1)
            V.tensor_scalar(k, tmp, SIN_MAX, -SIN_MAX, ALU.min, ALU.max).then_inc(for_act, 1)
            dve.wait_ge(for_act, 2 * n + 2)
        meet(dve, c, "dve")

        def norm(groups, split=False):
            for g in groups:
                dve.wait_ge(sq_used, c.next(sq_used, len(g["src"])))
                dve.wait_ge(normed, c.made(normed))
                V.tensor_scalar(rms, bank[7], 1.0 / g["width"], EPS, ALU.mult, ALU.add).then_inc(ms_ready, 1)
                dve.wait_ge(rms_ready, c.next(rms_ready))
                step(V.reciprocal(rms, rms))
                for k, (s, o, gain, r) in enumerate(zip(g["src"], g["dst"], g["gain"], g["rows"])):
                    if split:
                        o = prob[:, k % 2]
                        dve.wait_ge(low_ready, c.next(low_ready, lag=2))
                    V.scalar_tensor_tensor(o, s, gain, rms[0:r, :], ALU.mult, ALU.mult).then_inc(normed, c.one(normed))

        def gemm(jobs, split=True):
            for n, j in enumerate(jobs):
                if split and n % 2 == 0:
                    c.skip(prod_ready)
                    continue
                dve.wait_ge(prod_ready, c.next(prod_ready))
                src = bank[n % 4][j["p0"]:j["p0"] + j["rows"], 0:j["n"]]
                if j["add"]:
                    ins = V.tensor_tensor(j["dst"], src, j["dst"], ALU.add)
                elif j["scale"]:
                    ins = V.tensor_scalar(j["dst"], src, j["scale"], None, ALU.mult)
                else:
                    ins = V.tensor_copy(j["dst"], src)
                ins.then_inc(taken_dve, 1)

        def ropes(list_):
            for n, (X, R, cos, sin) in enumerate(list_):
                p0, r = X.start_partition(), X.shape[0]
                t = sq[p0:p0 + r, n % 2]
                dve.wait_ge(rot_ready, c.next(rot_ready))
                step(V.tensor_tensor(t, bank[n % 4][p0:p0 + r, :], sin, ALU.mult))
                dve.wait_ge(cos_done, c.next(cos_done))
                V.tensor_tensor(X, X, t, ALU.add).then_inc(rope_done, c.one(rope_done))

        def hidden(n, silu_, up_, dst):
            dve.wait_ge(silu_ready, c.next(silu_ready))
            V.tensor_tensor(dst, silu_, up_, ALU.mult).then_inc(gu_ready, c.one(gu_ready))

        def hidden_parts(n):
            g = GU_PARTS[:, n % 2]
            dve.wait_ge(silu_ready, c.next(silu_ready))
            V.tensor_tensor(GU[:, n % 2], SILU[:, n % 2], bank[2 + n % 2], ALU.mult)
            step(V.tensor_tensor(g[:, 0], SILU[:, n % 2], bank[2 + n % 2], ALU.mult))
            V.tensor_tensor(g[:, 1], GU[:, n % 2], g[:, 0].bitcast(F32), ALU.subtract).then_inc(gu_ready, c.one(gu_ready))

        def add_down(scale):
            for q in range(KC):
                dve.wait_ge(down_ready, c.next(down_ready))
                dve.wait_ge(down_used, c.made(down_used, lag=KC - 1))
                V.scalar_tensor_tensor(x[:, q], bank[4 + q % 4], scale, x[:, q], ALU.mult, ALU.add).then_inc(down_used, c.one(down_used))

        def ffn():
            def both(n):
                add_down(0.5)
                hidden_parts(n + 1)
            hidden_parts(0)
            for n in range(SLOTS):
                both(n)
            with dve.Fori(0, FFN_TRIPS) as i:
                c.loop(i, {silu_ready: SLOTS, gu_ready: SLOTS, down_ready: SLOTS * KC, down_used: SLOTS * KC, step_dve: SLOTS})
                for r in range(SLOTS):
                    both(r)
                c.looped(FFN_TRIPS)
            for n in range(SLOTS * (FFN_TRIPS + 1), FFN_ITEMS - 1):
                both(n)
            add_down(0.5)

        def attention(units):
            tiles = [t for u in units for t in u["tiles"]]
            before = c.at.get(pv_ready.name, 0)

            def maximum(a):
                bias, i, n = units[a // NT]["bias"], a % NT, tiles[a]["n"]
                src = SCORES[a % 3][:, 0:n]
                if bias is not None:
                    hb = HB[:, bias % 2]
                    if i == 0:
                        step(V.scalar_tensor_tensor(hb, table[:, C2_DIST:C2_DIST + 896], -(2.0 ** -(bias + 1)),
                                                    table[:, C2_MULT:C2_MULT + 896], ALU.mult, ALU.add))
                    at = 384 - P * i
                    dve.wait_ge(scores_ready, c.next(scores_ready))
                    dve.wait_ge(probs_ready, c.next(probs_ready, lag=2))
                    step(V.scalar_tensor_tensor(SB[:, a % 2], src, E_DH ** -0.5, hb[:, at:at + T], ALU.mult, ALU.add))
                    src = SB[:, a % 2]
                else:
                    dve.wait_ge(scores_ready, c.next(scores_ready))
                    c.skip(probs_ready)
                V.tensor_reduce(NM[:, a % 4:a % 4 + 1], src, AX.X, ALU.max, negate=True).then_inc(max_ready, 1)

            def copied(a):
                t = tiles[a]
                n = P * len(t["v"])
                dve.wait_ge(pT_ready, c.next(pT_ready))
                dve.wait_ge(pv_ready, c.next(pv_ready, lag=2))
                V.tensor_copy(probT[0:t["rows"], a % 2, 0:n], bank[2 + a % 2][0:t["rows"], 0:n]).then_inc(pT_copied, 1)

            def result(n):
                u = units[n]
                d = DEN[:, 4 * (n % 2):4 * (n % 2) + 4]
                src = bank[4 + n % 2][:, 0:64 * NT].rearrange("p (i n) -> p i n", i=NT)
                w = RDEN
                step(V.reciprocal(RDEN, d))
                if u["gate"] is not None:
                    w = WGT
                    step(V.tensor_tensor(WGT, RDEN, u["gate"], ALU.mult))
                w = w.unsqueeze(2).to_broadcast([P, NT, 64])
                dve.wait_ge(pv_ready, before + NT * (n + 1))
                to = u["out"]
                if u["mode"] == "add":
                    to = share_of(units, n)
                    dve.wait_ge(share_used, c.next(share_used, lag=2))
                V.tensor_tensor(to, src, w, ALU.mult).then_inc(o_done, 1)

            for a in range(len(tiles) + 3):
                if a < len(tiles):
                    maximum(a)
                if 0 <= a - 2 < len(tiles):
                    copied(a - 2)
                if a >= 3 and (a - 3) % NT == NT - 1:
                    result((a - 3) // NT)

        def head_norm(col0, heads, n, gain, factor, gate=None):
            v = O[:, :, col0:col0 + heads * n].rearrange("p i (m n) -> p i m n", m=heads)
            sqv = SUBSQ[:, 0:NT * heads * n]
            step(V.tensor_tensor(sqv.rearrange("p (i m n) -> p i m n", i=NT, m=heads), v, v, ALU.mult))
            step(V.tensor_reduce(MS16, sqv.rearrange("p (a n) -> p a n", n=n), AX.X, ALU.add))
            V.tensor_scalar(MS16, MS16, 1.0 / n, EPS, ALU.mult, ALU.add).then_inc(for_act, 1)
            dve.wait_ge(for_dve, c.next(for_dve))
            step(V.reciprocal(MS16, MS16))
            g = SUBSQ[:, 0:n]
            step(V.tensor_scalar(g, gain, factor, None, ALU.mult))
            r = MS16.rearrange("p (i m) -> p i m", i=NT).unsqueeze(3).to_broadcast([P, NT, heads, n])
            step(V.tensor_tensor(v, v, r, ALU.mult))
            step(V.tensor_tensor(v, v, g.unsqueeze(1).unsqueeze(1).to_broadcast([P, NT, heads, n]), ALU.mult))
            if gate is not None:
                o = O[:, :, col0:col0 + heads * n]
                step(V.tensor_tensor(o, o, gate, ALU.mult))

        for l in range(LAYERS):
            lam_init = 0.8 - 0.6 * math.exp(-0.3 * l)
            norm(norm_x(COL_FFN1 + 8 * l), split=True)
            meet(dve, c, "dve")
            ffn()
            meet(dve, c, "dve")
            norm(norm_x(COL_MIX + 8 * l))
            meet(dve, c, "dve")
            gemm(project_one(0))
            meet(dve, c, "dve")
            norm(norm_mla(l))
            r0 = ROW_LAM + 4 * C_DH * l
            lp = small[:, 256:256 + 2 * C_DH]
            step(V.tensor_tensor(lp, rows[:, r0:r0 + 2 * C_DH], rows[:, r0 + 2 * C_DH:r0 + 4 * C_DH], ALU.mult))
            V.tensor_reduce(LAM[:, 0:2], lp.rearrange("p (a n) -> p a n", a=2), AX.X, ALU.add).then_inc(for_act, 1)
            ropes(ropes_first())
            dve.wait_ge(for_dve, c.next(for_dve))
            step(V.tensor_tensor(LAM[:, 2:3], LAM[:, 0:1], LAM[:, 1:2], ALU.subtract))
            V.tensor_scalar(LAM[:, 3:4], LAM[:, 2:3], -1.0, -lam_init, ALU.mult, ALU.add)
            dve.wait_ge(for_dve, c.next(for_dve))
            g0 = GATE[:, 0, 0:3 * B_HEADS:3]
            V.tensor_scalar(g0, g0, cst(C_ROWM), None, ALU.mult)
            meet(dve, c, "dve")
            gemm(project_mla(0))
            meet(dve, c, "dve")
            ropes(ropes_mla())
            for part in range(2):
                for g in range(B_GROUPS):
                    s = slice(64 * g, 64 * g + 64)
                    dve.wait_ge(cmp_ready, c.next(cmp_ready))
                    V.tensor_copy(CB[s, part:part + 1], bank[4 + 2 * part + g][s, 32:33]).then_inc(cmp_bias, 1)
            dve.wait_ge(cmp_ready, c.next(cmp_ready))
            V.tensor_copy(KCMP, bank[4][:, 64:64 + N_CMP])
            for g in range(B_GROUPS):
                V.tensor_copy(VCMP[0:N_CMP, g], bank[5 + g][0:N_CMP, 64:128])
            meet(dve, c, "dve")
            attention(mixer_units())
            meet(dve, c, "dve")
            head_norm(768, C_HEADS, 2 * C_DH, rows[:, ROW_SUB + 64 * l:ROW_SUB + 64 * l + 64], 1.0 - lam_init)
            meet(dve, c, "dve")
            meet(dve, c, "dve")
            gemm(project_out(0), split=False)
            meet(dve, c, "dve")
            norm(norm_x(COL_FFN2 + 8 * l), split=True)
            meet(dve, c, "dve")
            ffn()
            meet(dve, c, "dve")
        norm(norm_final())
        meet(dve, c, "dve")
        norm(norm_x(COL_N1))
        meet(dve, c, "dve")
        gemm(project_second(0))
        meet(dve, c, "dve")
        norm(norm_heads())
        meet(dve, c, "dve")
        attention(dilated_units())
        meet(dve, c, "dve")

        V.tensor_tensor(LBT, cols[:, COL_LB + 8:COL_LB + 16], cols[:, COL_LB:COL_LB + 8], ALU.subtract).then_inc(for_act, 1)
        dve.wait_ge(for_dve, c.next(for_dve))
        step(V.tensor_scalar(LBT, LBT, 1.0, None, ALU.add))
        step(V.reciprocal(LB, LBT))
        step(V.tensor_scalar(OMLB, LB, -1.0, 1.0, ALU.mult, ALU.add))
        for d in range(2):
            dve.wait_ge(for_dve, c.next(for_dve))
            for m in range(H_HEADS):
                u = 4 * d + m
                V.tensor_scalar(K2[d][:, m], K2[d][:, m], OMLB[:, u:u + 1], None, ALU.mult)
                last = V.tensor_scalar(Z[d][:, m], Z[d][:, m], OMLB[:, u:u + 1], LB[:, u:u + 1], ALU.mult, ALU.add)
            last.then_inc(for_act, 1)
        V.memset(BC[:, :, 0:1], 0.0)
        meet(dve, c, "dve")

        for m in range(H_HEADS):
            q = HQ[:, m]
            for d in range(2):
                k = K2[d][:, m]
                for i in range(NT):
                    last = V.tensor_tensor_scan(BC[:, i, 1:P + 1], ones, Z[d][:, m, P * i:P * i + P], 0.0, ALU.mult, ALU.add)
                last.then_inc(scan_ready, c.one(scan_ready))
                dve.wait_ge(scan_ready, c.made(scan_ready))
                V.tensor_tensor(DD[:, 0].rearrange("p (i n) -> p i n", i=NT), BC[:, :, P:P + 1].to_broadcast([P, NT, P]),
                                cum(d), ALU.subtract).then_inc(diff_ready, c.one(diff_ready))
                dve.wait_ge(fac_ready, c.next(fac_ready))
                if m or d:
                    dve.wait_ge(off_ready, c.next(off_ready, 0))
                V.tensor_tensor(QT.rearrange("p i n -> p (i n)"), q, EE[:, d], ALU.mult).then_inc(step_dve, c.one(step_dve))
                V.tensor_tensor(KT.rearrange("p i n -> p (i n)"), k, EE[:, 1 - d], ALU.mult).then_inc(step_dve, c.one(step_dve))
                dve.wait_ge(step_dve, c.made(step_dve))
                step(V.tensor_scalar(QX[:, 0], QT[:, 0 if d else 2], ET[:, 1:2], None, ALU.mult))
                step(V.tensor_scalar(QX[:, 1], QT[:, 1 if d else 3], ET[:, 2:3], None, ALU.mult))
                V.tensor_scalar(QX[:, 2], QX[:, 1 - d], ET[:, 1 + d:2 + d], None, ALU.mult).then_inc(qk_ready, 1)
                dve.wait_ge(off_ready, c.next(off_ready))
                if d == 0:
                    dve.wait_ge(keys_ready, c.next(keys_ready, 2))

                def diff(n):
                    w = LEVELS[n]
                    v = cum(d).rearrange("p i (j w) -> p i j w", w=2 * w)
                    r = w if d else w - 1
                    V.tensor_tensor(DD[:, n % 2].rearrange("p (i j w) -> p i j w", i=NT, w=2 * w), v,
                                    v[:, :, :, r:r + 1].to_broadcast([P, NT, 64 // w, 2 * w]), ALU.subtract).then_inc(diff_ready, c.one(diff_ready))

                def product(n):
                    w = LEVELS[n]
                    dve.wait_ge(decay_ready, c.next(decay_ready))
                    e, o = halves(EE[:, n % 2], w), halves(MM[:, n % 2], w)
                    left, right = (q, k) if d else (k, q)
                    V.tensor_tensor(o[0], halves(left, w)[0], e[0], ALU.mult)
                    V.tensor_tensor(o[1], halves(right, w)[1], e[1], ALU.mult).then_inc(lvl_ready, 1)

                def put(n):
                    w = LEVELS[n]
                    dve.wait_ge(lvl_mm, c.next(lvl_mm))
                    at = C2_LVL + (d * len(LEVELS) + n) * 64
                    mask = table[:, at:at + 64].bitcast(I32).rearrange("p (j w) -> p j w", w=w)
                    o = AT.rearrange("p i (j w) -> p i j w", w=2 * w)
                    o = o[:, :, :, 0:w] if d else o[:, :, :, w:2 * w]
                    dve.wait_ge(lvl_put, c.made(lvl_put))
                    for i in range(NT):
                        ins = V.copy_predicated(o[:, i], mask, bank[2 + n % 2][:, 64 * i:64 * i + 64].rearrange("p (j w) -> p j w", w=w))
                    ins.then_inc(lvl_put, c.one(lvl_put))

                for n in range(len(LEVELS) + 2):
                    if n < len(LEVELS):
                        diff(n)
                    if 0 <= n - 1 < len(LEVELS):
                        product(n - 1)
                    if n >= 2:
                        put(n - 2)
            dve.wait_ge(diag_mm, c.next(diag_mm))
            dve.wait_ge(lvl_put, c.made(lvl_put))
            for i in range(NT):
                ins = V.copy_predicated(AT[:, i], ident.bitcast(I32), bank[6][:, P * i:P * i + P])
            ins.then_inc(diag_put, 1)
            dve.wait_ge(head_mm, c.next(head_mm))
        meet(dve, c, "dve")
        head_norm(512, H_HEADS, P, rows[:, ROW_OUT:ROW_OUT + P], 1.0, GG)
        meet(dve, c, "dve")
        meet(dve, c, "dve")
        gemm(project_out(0), split=False)
        meet(dve, c, "dve")
        norm(norm_x(COL_N2))
        meet(dve, c, "dve")

        dve.wait_ge(logit_ready, c.next(logit_ready))
        for i in range(NT):
            last = V.tensor_reduce(NM[:, i:i + 1], bank[0][:, 16 * i:16 * i + 16], AX.X, ALU.max, negate=True)
        last.then_inc(logit_max, 1)
        dve.wait_ge(logit_exp, c.next(logit_exp, NT))
        step(V.reciprocal(RDEN, DEN[:, 0:NT]))
        for i in range(NT):
            last = V.tensor_scalar(AFF[:, i], AFF[:, i], RDEN[:, i:i + 1], None, ALU.mult)
        last.then_inc(aff_ready, 1)
        best, work, chosen, place = small[0:16, 256:264], rms[0:16, :], probT[0:16, 0], probT[0:16, 1]
        dve.wait_ge(affT_ready, c.next(affT_ready))
        step(V.tensor_copy(work, bank[1][0:16, :]))
        for n in range(CAP // 8):
            step(V.max(best, work))
            step(V.match_replace(work, best, work, NEG))
        step(V.tensor_scalar(chosen, work, NEG / 2, None, ALU.is_lt))
        step(V.tensor_tensor_scan(place, chosen, chosen, 0.0, ALU.add, ALU.max))
        step(V.tensor_tensor(place, place, chosen, ALU.mult))
        V.tensor_scalar(SLOTT[0:16], place, -1.0, None, ALU.add).then_inc(slotT_ready, 1)
        dve.wait_ge(slot_ready, c.next(slot_ready))
        V.tensor_copy(SLOT, bank[2][:, 0:64].rearrange("p (i e) -> p i e", i=NT))
        meet(dve, c, "dve")
        iota = cst(C_IOTA, CAP).unsqueeze(1).to_broadcast([P, N_EXPERTS, CAP])
        for i in range(NT):
            V.tensor_tensor(SEL[:, i].rearrange("p (e n) -> p e n", e=N_EXPERTS),
                            SLOT[:, i].unsqueeze(2).to_broadcast([P, N_EXPERTS, CAP]), iota, ALU.is_equal)
        meet(dve, c, "dve")
        gemm(gathered())
        meet(dve, c, "dve")
        for i in range(NT):
            s = SEL[:, i].rearrange("p (e n) -> p e n", e=N_EXPERTS)
            V.tensor_tensor(s, s, AFF[:, i].unsqueeze(2).to_broadcast([P, N_EXPERTS, CAP]), ALU.mult)
        meet(dve, c, "dve")
        meet(dve, c, "dve")
        with dve.Fori(0, N_EXPERTS // 2) as i:
            c.loop(i, {silu_ready: 16, gu_ready: 16, y_ready: 16, down_ready: KC, down_used: KC})
            for n in range(16):
                hidden(n, MG[:, n % 2, 0:64], bank[n % 2][:, 64:128], MGU[:, n % 2, 0:64])
            dve.wait_ge(y_ready, c.next(y_ready, 16))
            V.tensor_copy(YS[:, T:2 * T], bank[3]).then_inc(y_copied, 1)
            add_down(1.0)
            c.looped(N_EXPERTS // 2)
        meet(dve, c, "dve")

    block_cm.__exit__(None, None, None)


def kernel(**inputs):
    import concourse.bacc as bacc
    from concourse.bass_utils import run_bass_kernel_spmd

    a = {k: np.asarray(v) for k, v in inputs.items()}
    f32 = np.float32

    def tiled(w):
        k, n = w.shape
        return w.reshape(k // P, P, n).transpose(1, 0, 2).reshape(P, -1)

    def columns(v):
        return v.reshape(-1, P).T

    def units(wg, wu, wd):
        n = wg.shape[1] // P
        up = [w.reshape(KC, P, n, P).transpose(2, 1, 0, 3).reshape(n, P, D) for w in (wg, wu)]
        return np.concatenate(up + [wd.reshape(n, P, D)], axis=2)

    ffn_w = np.stack([units(a[f"ffn{f}_wg"][l], a[f"ffn{f}_wu"][l], a[f"ffn{f}_wd"][l]) for l in range(LAYERS) for f in (1, 2)])
    moe_w = np.concatenate([units(a["w_expert_gate_2"][0, e], a["w_expert_up_2"][0, e], a["w_expert_down_2"][0, e])
                            for e in range(N_EXPERTS)])

    def items(list_):
        r = np.zeros((len(list_), P, ITEM), f32)
        for n, v in enumerate(list_):
            r[n, :, :v.shape[1]] = v
        return r

    def by_columns(w):
        return [tiled(w[:, n:n + WCOLS]) for n in range(0, w.shape[1], WCOLS)]

    mixes = []
    for l in range(LAYERS):
        w = a["w_in"][l]
        wb, wc = w[:, A_COLS:A_COLS + B_COLS], w[:, A_COLS + B_COLS:]
        qb = wb[:, :384].reshape(D, B_GROUPS, B_HPG, B_DH).transpose(0, 2, 1, 3).reshape(D, 384)
        kv = [wb[:, 384 + 128 * n:512 + 128 * n] for n in range(6)]
        parts = [w[:, :A_COLS], qb, np.concatenate([kv[0], kv[1], kv[2]], 1), np.concatenate([kv[4], kv[3], kv[5]], 1),
                 np.concatenate([wc[:, :256], wb[:, 1152:]], 1), wc[:, 256:512], wc[:, 512:]]
        uq = np.zeros((256, 576), f32)
        uq[:A_QR] = a["mla_w_uq"][l]
        mla = np.concatenate([tiled(uq), a["mla_w_ukv"][l]], 1)
        phi = [np.tile(np.concatenate([a[f"nsa_phi_{s}1"][l].reshape(CMP_LEN, B_DH, B_DH).transpose(1, 0, 2).reshape(B_DH, -1),
                                       a[f"nsa_phi_{s}2"][l]], 1), (2, 1)) for s in "kv"]
        mixes.append(items([tiled(v) for v in parts] + [mla] + phi + by_columns(a["w_out"][l])))
    second = items(by_columns(a["w_in_2"][0]) + by_columns(a["w_out_2"][0]))

    cols = np.zeros((P, N_COLS), f32)
    for l in range(LAYERS):
        cols[:, COL_FFN1 + 8 * l:COL_FFN1 + 8 * l + 8] = columns(a["ffn1_norm"][l])
        cols[:, COL_MIX + 8 * l:COL_MIX + 8 * l + 8] = columns(a["mix_norm"][l])
        cols[:, COL_FFN2 + 8 * l:COL_FFN2 + 8 * l + 8] = columns(a["ffn2_norm"][l])
        cols[:, COL_MLAQ + 2 * l] = a["mla_q_norm"][l, :P]
        cols[:A_QR - P, COL_MLAQ + 2 * l + 1] = a["mla_q_norm"][l, P:]
        cols[:, COL_MLAKV + l] = a["mla_kv_norm"][l]
        for n, s in enumerate("kv"):
            at = COL_PE + (2 * l + n) * CMP_LEN
            cols[:, at:at + CMP_LEN] = np.tile(a[f"nsa_pe_{s}"][l].T, (2, 1))
    cols[:, COL_FINAL:COL_FINAL + 8] = columns(a["final_norm"])
    cols[:, COL_N1:COL_N1 + 8] = columns(a["norm1_w_2"][0])
    cols[:, COL_N2:COL_N2 + 8] = columns(a["norm2_w_2"][0])
    cols[:, COL_DQ] = np.tile(a["attn_q_norm_w_2"][0], 2)
    cols[:, COL_DK] = np.tile(a["attn_k_norm_w_2"][0], 2)
    for r in range(2):
        for n, s in enumerate(("fwd", "bwd")):
            cols[:, COL_LB + 8 * r + 4 * n:COL_LB + 8 * r + 4 * n + 4] = columns(a[f"hgrn_lb_{s}_2"][r])
    cols[:, COL_ROUTER:] = tiled(a["w_router_2"][0])
    row = np.concatenate([a[f"diff_{s}"][l] for l in range(LAYERS) for s in ("lq1", "lq2", "lk1", "lk2")]
                         + [a["diff_sub_norm"][l] for l in range(LAYERS)] + [a["hgrn_out_norm_w_2"][0]])
    const, const2 = constants()
    arrays = dict(
        ffn_w=ffn_w, mix_w=np.stack(mixes), second_w=second, moe_w=moe_w,
        x_in=np.ascontiguousarray(a["x"][0].T.reshape(KC, P, T).transpose(1, 0, 2)),
        pos_in=np.ascontiguousarray(np.broadcast_to(a["positions"], (P, T))),
        cols_in=cols, rows_in=np.ascontiguousarray(np.broadcast_to(row, (P, N_ROWS))), const_in=const, const2_in=const2)
    nc = bacc.Bacc("TRN2", target_bir_lowering=False, num_devices=1)
    args = [nc.dram_tensor(n, v.shape, mybir.dt.from_np(v.dtype), kind="ExternalInput").ap() for n, v in arrays.items()]
    out = nc.dram_tensor("out", (P, KC, T), F32, kind="ExternalOutput").ap()
    program(nc, *args, out)
    r = run_bass_kernel_spmd(nc, [arrays], core_ids=[0]).results[0]["out"]
    return np.ascontiguousarray(np.asarray(r).transpose(2, 1, 0).reshape(1, T, D))
```

```python
import math

import numpy as np

import concourse.bass as bass
from concourse import mybir

F32 = mybir.dt.float32
F32R = mybir.dt.float32r
BF16 = mybir.dt.bfloat16
I32 = mybir.dt.int32
ALU = mybir.AluOpType
ACT = mybir.ActivationFunctionType
AX = mybir.AxisListType

P = 128
D = 1024
T = 512
LAYERS = 2
KC = D // P
NT = T // P
D_FF = 2816
FFN_ITEMS = D_FF // P
EPS = 1e-6
THETA = 500000.0
NEG = -1e30

A_HEADS, A_QR, A_NOPE, A_ROPE = 6, 192, 64, 32
A_DK = A_NOPE + A_ROPE
B_GROUPS, B_HPG, B_DH = 2, 3, 64
B_HEADS = B_GROUPS * B_HPG
B_ROT = B_DH // 4
CMP_LEN, CMP_STRIDE = 32, 16
N_CMP = (T - CMP_LEN) // CMP_STRIDE + 1
C_HEADS, C_DH = 4, 32
C_ROT = C_DH // 4
A_COLS = A_QR + 128 + A_ROPE
B_COLS = B_HEADS * B_DH + 6 * B_GROUPS * B_DH + 3 * B_HEADS

E_HEADS, E_DH = 8, 64
H_HEADS, H_DK = 4, 128
N_EXPERTS = 16
CAP = 2 * T // N_EXPERTS
MOE_ITEMS = D // P
PATTERNS = ((128, 1), (512, 4), (2048, 16))
LEVELS = (64, 32, 16, 8, 4, 2, 1)

SLOTS = 4
ITEM = 3 * D
WCOLS = ITEM // KC
MOE_SLOTS = 8
MIX_ITEMS = 13
SECOND_ITEMS = 14
FFN_TRIPS = FFN_ITEMS // SLOTS - 1

ROUND = 12582912.0
TWO_PI = (6.28125, 0.0019350051879882812, 3.0199159819e-07)
SIN_MAX = 3.1415925

COL_FFN1, COL_MIX, COL_FFN2 = 0, 16, 32
COL_FINAL, COL_N1, COL_N2 = 48, 56, 64
COL_MLAQ, COL_MLAKV = 72, 76
COL_DQ, COL_DK = 78, 79
COL_LB = 80
COL_PE = 96
COL_ROUTER = COL_PE + LAYERS * 2 * CMP_LEN
N_COLS = COL_ROUTER + KC * N_EXPERTS
ROW_LAM = 0
ROW_SUB = LAYERS * 4 * C_DH
ROW_OUT = ROW_SUB + LAYERS * 2 * C_DH
N_ROWS = ROW_OUT + H_DK
C_ID, C_BLK, C_TRI = 0, 128, 256
C_RA, C_RB, C_RC = 384, 512, 640
C_CMP = 768
C_ROWM = C_CMP + NT * N_CMP
C_INV = C_ROWM + 1
C_IOTA = C_INV + 3
N_CONST = C_IOTA + CAP
C2_DIST, C2_MULT = 0, 896
C2_LVL = 1792
N_CONST2 = C2_LVL + 2 * len(LEVELS) * 64


def constants():
    c = np.zeros((P, N_CONST), np.float32)
    c[:, C_ID:C_ID + P] = np.eye(P)
    for b in range(2):
        c[64 * b:64 * b + 64, C_BLK + 64 * b:C_BLK + 64 * b + 64] = 1
    p = np.arange(P)
    c[:, C_TRI:C_TRI + P] = np.where(p[None, :] <= p[:, None], 0, NEG)
    for at, period, first, half in ((C_RA, P, 64, 16), (C_RB, 64, 0, 8), (C_RC, 32, 0, 4)):
        for b in range(0, P, period):
            for i in range(half):
                c[b + first + half + i, at + b + first + i] = -1
                c[b + first + i, at + b + first + half + i] = 1
    for i in range(NT):
        last = np.arange(N_CMP) * CMP_STRIDE + CMP_LEN - 1
        c[:, C_CMP + i * N_CMP:C_CMP + (i + 1) * N_CMP] = np.where(last[None] <= (i * P + p)[:, None], 0, NEG)
    c[:, C_ROWM] = p >= CMP_LEN - 1
    for n, (period, first, rot) in enumerate(((P, 64, A_ROPE), (64, 0, B_ROT), (32, 0, C_ROT))):
        inv = (1.0 / (np.float32(THETA) ** (np.arange(0, rot, 2, dtype=np.float32) / np.float32(rot)))).astype(np.float32)
        for b in range(0, P, period):
            c[b + first:b + first + rot, C_INV + n] = np.concatenate([inv, inv])
    c[:, C_IOTA:C_IOTA + CAP] = np.arange(CAP)
    d = np.zeros((P, N_CONST2), np.float32)
    dist = np.abs(p[:, None] - np.arange(896)[None] + 384)
    mult = np.zeros(dist.shape)
    for window, dil in PATTERNS:
        mult += (dist % dil == 0) & (dist <= window // 2)
    d[:, C2_DIST:C2_DIST + 896] = dist
    d[:, C2_MULT:C2_MULT + 896] = np.where(mult > 0, np.log(np.maximum(mult, 1)), NEG)
    for back in range(2):
        for n, m in enumerate(LEVELS):
            blk = np.arange(64) // m
            half = (p % (2 * m) >= m) if back else (p % (2 * m) < m)
            at = C2_LVL + (back * len(LEVELS) + n) * 64
            d[:, at:at + 64] = (p[:, None] // (2 * m) == blk[None]) & half[:, None]
    return c, d


class Count:

    def __init__(self):
        self.at, self.own, self.reg, self.rate, self.mark = {}, {}, None, {}, {}

    def value(self, sem, v):
        if self.reg is None:
            return max(v, 0)
        assert v > 0
        return self.reg * self.rate[sem.name] + v

    def next(self, sem, n=1, lag=0):
        self.at[sem.name] = self.at.get(sem.name, 0) + n
        return self.value(sem, self.at[sem.name] - lag)

    def skip(self, sem, n=1):
        self.at[sem.name] = self.at.get(sem.name, 0) + n

    def one(self, sem, n=1):
        self.own[sem.name] = self.own.get(sem.name, 0) + n
        return n

    def made(self, sem, lag=0):
        return self.value(sem, self.own.get(sem.name, 0) - lag)

    def loop(self, reg, rate):
        self.reg, self.rate = reg, {s.name: n for s, n in rate.items()}
        self.mark = (dict(self.at), dict(self.own))

    def looped(self, trips):
        for now, then in zip((self.at, self.own), self.mark):
            for k in now:
                d = now[k] - then.get(k, 0)
                assert d == 0 or d == self.rate[k], (k, d)
                now[k] += d * (trips - 1)
        self.reg = None


def program(nc, ffn_w, mix_w, second_w, moe_w, x_in, pos_in, cols_in, rows_in, const_in, const2_in, out):
    place = {}

    def sb(name, n, dt=F32):
        t = nc.alloc_sbuf_tensor(name, [P, n], dt)
        place[name] = nc.lookup_mloc(t).addr
        return t.ap()

    def rounded(name, over, at, n):
        return nc.alloc_sbuf_tensor_at(name, [P, n], F32R, offset=place[over] + 4 * at).ap()

    x = sb("x", KC * T).rearrange("p (k t) -> p k t", k=KC)
    h = sb("h", KC * T).rearrange("p (k t) -> p k t", k=KC)
    h_hi = rounded("h_hi", "h", 0, KC * T).rearrange("p (k t) -> p k t", k=KC)
    h_lo = sb("h_lo", KC * T, F32R).rearrange("p (k t) -> p k t", k=KC)
    ring = sb("ring", SLOTS * ITEM).rearrange("p (s n) -> p s n", s=SLOTS)
    mix = sb("mix", 18432)
    const = sb("const", N_CONST)
    table = sb("table", 3072)
    cols = sb("cols", N_COLS)
    rows = sb("rows", N_ROWS)
    prob = sb("prob", 3 * T).rearrange("p (b n) -> p b n", b=3)
    share = sb("share", T).rearrange("p (b n) -> p b n", b=2)
    probT = sb("probT", 2 * T).rearrange("p (b n) -> p b n", b=2)
    sq = sb("sq", 2 * T).rearrange("p (b n) -> p b n", b=2)
    rms = sb("rms", T)
    small = sb("small", 320)
    ones = sb("ones", P)

    assert place["sq"] + 8 * T - place["prob"] == 32 * T
    PIECE_HI = rounded("piece_hi", "prob", 0, 8 * T).rearrange("p (b n) -> p b n", b=2)
    ring_lo = rounded("ring_lo", "ring", 0, SLOTS * ITEM).rearrange("p (s n) -> p s n", s=SLOTS)

    bank = [nc.alloc_psum_tensor(f"bank{i}", [P, T], F32).ap() for i in range(8)]

    def new(*names):
        made = [nc.alloc_semaphore(n) for n in names]
        return made if len(names) > 1 else made[0]

    consts_in, second_in, stored = new("consts_in", "second_in", "stored")
    w_in = [new(f"w_in{s}") for s in range(SLOTS)]
    moe_in = [new(f"moe_in{s}") for s in range(MOE_SLOTS)]
    met = {e: new(f"met_{e}") for e in ("pe", "act", "dve", "pool")}
    step_dve, step_act, for_act, for_dve = new("step_dve", "step_act", "for_act", "for_dve")
    sq_ready, sq_used, ms_ready, rms_ready, normed = new("sq_ready", "sq_used", "ms_ready", "rms_ready", "normed")
    high_ready, low_ready = new("high_ready", "low_ready")
    w_high, up_split, down_split = new("w_high", "up_split", "down_split")
    up_ready, silu_ready, gu_ready, down_ready, down_used = new("up_ready", "silu_ready", "gu_ready", "down_ready", "down_used")
    y_ready, y_copied = new("y_ready", "y_copied")
    piece_high, piece_split = new("piece_high", "piece_split")
    prod_ready, taken_act, taken_dve = new("prod_ready", "taken_act", "taken_dve")
    rot_ready, cos_done, rope_done = new("rot_ready", "cos_done", "rope_done")
    fold_ready, fold_copied, fold_split = new("fold_ready", "fold_copied", "fold_split")
    cmp_ready, cmp_bias, cmp_hid = new("cmp_ready", "cmp_bias", "cmp_hid")
    scores_ready, max_ready, probs_ready = new("scores_ready", "max_ready", "probs_ready")
    pT_ready, pT_copied, pv_ready, o_done = new("pT_ready", "pT_copied", "pv_ready", "o_done")
    share_used = new("share_used")
    scan_ready, fac_ready, qk_ready, off_ready, off_copied = new("scan_ready", "fac_ready", "qk_ready", "off_ready", "off_copied")
    diff_ready, decay_ready, lvl_ready, lvl_mm, lvl_put = new("diff_ready", "decay_ready", "lvl_ready", "lvl_mm", "lvl_put")
    keys_ready, diag_mm, diag_put, head_mm, head_out = new("keys_ready", "diag_mm", "diag_put", "head_mm", "head_out")
    logit_ready, logit_max, logit_exp, aff_ready = new("logit_ready", "logit_max", "logit_exp", "aff_ready")
    affT_ready, slotT_ready, slot_ready = new("affT_ready", "slotT_ready", "slot_ready")

    def view(at, n, **k):
        v = mix[:, at:at + n]
        return v.rearrange("p (a n) -> p a n", **k) if k else v

    def chunks(at, n):
        return view(at, n * T, a=n)

    cst = lambda at, n=1, r=slice(0, P): const[r, at:at + n]
    ident = cst(C_ID, P)
    mask16 = nc.alloc_sbuf_tensor("mask16", [P, 2 * P + NT * N_CMP], BF16).ap()
    ident16, tri16 = mask16[:, 0:P], mask16[:, P:2 * P]
    cmp16 = lambda i: mask16[:, 2 * P + i * N_CMP:2 * P + (i + 1) * N_CMP]
    col = lambda at, r=slice(0, P): cols[r, at:at + 1]

    QA, KA = chunks(0, 6), chunks(3072, 6)
    VA = view(6144, NT * 384, a=NT)
    CQ, CKV, KPE = chunks(7680, 2), chunks(8704, 1), chunks(9216, 1)
    QB, KB = chunks(9728, 3), chunks(11264, 4)
    VB = view(13312, NT * 256, a=NT)
    GATE = view(14336, NT * 18, a=NT)
    KCMP, VCMP, HID = view(14408, N_CMP), view(14440, 2 * 64, a=2), view(14568, 2 * N_CMP, a=2)
    QC, KCc = chunks(14640, 2), chunks(15664, 2)
    VC = view(16688, NT * 256, a=NT)
    assert 16688 + 1024 <= 18432
    LAM, CB = small[:, 0:4], small[:, 4:8]
    O = h.rearrange("p k t -> p (k t)").rearrange("p (i n) -> p i n", i=NT)
    OT = chunks(0, KC)
    OT_LO = rounded("mixed_lo", "mix", 0, KC * T).rearrange("p (k t) -> p k t", k=KC)
    OT_HI = h_lo
    SILU, GU = chunks(0, 2), chunks(1024, 2)
    parts = rounded("ffn_parts", "mix", 2048, 14336)
    W_UP = parts[:, 0:8192].rearrange("p (b s n) -> p b s n", b=2, s=2)
    W_DOWN = parts[:, 8192:12288].rearrange("p (b s n) -> p b s n", b=2, s=2)
    GU_PARTS = parts[:, 12288:14336].rearrange("p (b s n) -> p b s n", b=2, s=2)
    NM, RDEN, WGT = small[:, 8:12], small[:, 12:16], small[:, 16:20]
    DEN = small[:, 264:272]
    SCORES = [bank[n] for n in (0, 1, 6)]
    SUBSQ = view(4096, 2048)
    MS16 = small[:, 64:80]
    SLOTT = sq[:, 0]
    ANGLE = [[mix[:, 2560 + 1024 * n + 512 * q:3072 + 1024 * n + 512 * q] for q in range(2)] for n in range(3)]
    COS = [table[:, 1024 * n:1024 * n + 512] for n in range(3)]
    SIN = [table[:, 1024 * n + 512:1024 * n + 1024] for n in range(3)]

    QD, KD = chunks(0, 4), chunks(2048, 4)
    VD = view(4096, NT * 512, a=NT)
    HQ, ZF, ZB = chunks(6144, 4), chunks(8192, 4), chunks(10240, 4)
    VI, GG = view(12288, NT * 512, a=NT), view(14336, NT * 512, a=NT)
    Z = [ZF, ZB]
    K2 = [QD, KD]
    MM = view(4096, 2 * T, a=2)
    EE = view(5120, 2 * T, a=2)
    AT = view(16384, T, a=NT)
    QT = view(16896, T, a=NT)
    KT = view(17408, T, a=NT)
    KSUM = view(17920, T, a=NT)
    BC = prob.rearrange("p b n -> p (b n)")[:, 0:516].rearrange("p (i n) -> p i n", i=NT)
    DD = probT
    QX = sq.rearrange("p b n -> p (b n)")[:, 0:384].rearrange("p (i n) -> p i n", i=3)
    AO = [table[:, 0:768].rearrange("p (i n) -> p i n", i=6), table[:, 768:1536].rearrange("p (i n) -> p i n", i=6)]
    ET, LB, OMLB, LBT = small[:, 24:28], small[:, 32:40], small[:, 40:48], small[:, 48:56]
    XIN = view(0, 8192, a=KC)
    HTOK = view(8192, 4096, a=NT)
    HTOK_LO = rounded("tokens_lo", "mix", 8192, 4096).rearrange("p (i n) -> p i n", i=NT)
    HTOK_HI = h_lo.rearrange("p k t -> p (k t)").rearrange("p (i n) -> p i n", i=NT)
    GT = view(14336, 4096, a=8)
    SEL = h.rearrange("p k t -> p (k t)").rearrange("p (i n) -> p i n", i=NT)
    CHOICE = h_hi.rearrange("p k t -> p (k t)").rearrange("p (i n) -> p i n", i=NT)
    AFF = small[:, 128:192].rearrange("p (i e) -> p i e", i=NT)
    SLOT = small[:, 192:256].rearrange("p (i e) -> p i e", i=NT)
    RW = cols[:, COL_ROUTER:COL_ROUTER + KC * N_EXPERTS].rearrange("p (k e) -> p k e", k=KC)
    MOE_SLOT = [ring[:, s] for s in range(SLOTS)] + [table, h.rearrange("p k t -> p (k t)")[:, 0:ITEM],
                                                     view(8192, ITEM), view(8192 + ITEM, ITEM)]
    MG = sq
    MGU = probT
    YS = prob.rearrange("p b n -> p (b n)")

    def job(terms, p0, rows_, n, dst, scale=None, need=(), free=0, add=False, piece=None):
        return dict(terms=terms, p0=p0, rows=rows_, n=n, dst=dst, scale=scale, need=need, free=free, add=add, piece=piece)

    FRESH_HI = rounded("fresh_hi", "mix", 14336, 4096).rearrange("p (b n) -> p b n", b=2)

    def piece(item, at, width, c0, n, jobs, fresh=2):
        cut = lambda a: a[:, item % SLOTS, 0:KC * width].rearrange("p (k n) -> p k n", k=KC)[:, :, c0:c0 + n]
        hi = FRESH_HI[:, 1 - at % 2] if at < fresh else PIECE_HI[:, at % 2]
        hi = hi[:, 0:KC * n].rearrange("p (k n) -> p k n", k=KC)
        lo = cut(ring_lo)
        r = jobs(hi, lo)
        r[0]["piece"] = dict(item=item, first=c0 == 0, raw=cut(ring), hi=hi, lo=lo)
        return r

    def in_parts(w_hi, w_lo, v_hi, v_lo):
        return [(w_hi, v_lo), (w_hi, v_hi), (w_lo, v_hi)]

    def feats(outs, v_hi=h_hi, v_lo=h_lo, add=False):
        return lambda hi, lo: [job([t for k in range(KC) for t in in_parts(hi[:, k, c:c + p0 + m], lo[:, k, c:c + p0 + m], v_hi[:, k, :], v_lo[:, k, :])],
                                   p0, m, T, dst, scale, add=add) for c, m, dst, p0, scale in outs]

    def toks(n, dsts):
        def jobs(hi, lo):
            r = []
            for i in range(NT):
                s = slice(i * P, (i + 1) * P)
                r.append(job([t for k in range(KC) for t in in_parts(h_hi[:, k, s], h_lo[:, k, s], hi[:, k, :], lo[:, k, :])],
                             0, P, n, dsts[i]))
            return r
        return jobs

    def pieces(plan, width, item, at, fresh=2):
        r = []
        for n, (c0, m, jobs) in enumerate(plan):
            r += piece(item, at + n, width, c0, m, jobs, fresh)
        r[-1]["free"] = 1
        return r

    def with_items(jobs, item):
        jobs[0]["need"] = (item,)
        jobs[-1]["free"] = 1
        return jobs

    def project_one(b):
        qs, both = B_DH ** -0.5, lambda dst, scale=None: feats([(P * j, P, d, 0, scale) for j, d in enumerate(dst)])
        tk = lambda V, n: toks(n, [V[:, i] for i in range(NT)])
        plans = [
            (352, [(0, 192, feats([(0, 128, CQ[:, 0], 0, None), (128, 64, CQ[0:64, 1], 0, None)])),
                   (192, 160, feats([(0, 128, CKV[:, 0], 0, None), (64, 32, KPE[64:96, 0], 64, None)]))]),
            (384, [(0, 256, both([QB[:, 0], QB[:, 1]], qs)), (256, 128, both([QB[:, 2]], qs))]),
            (384, [(0, 256, both([KB[:, 0], KB[:, 1]])), (256, 128, both([KB[:, 2]]))]),
            (384, [(0, 128, both([KB[:, 3]])), (128, 256, tk(VB, 256))]),
            (274, [(0, 256, both([QC[:, 0], QC[:, 1]], C_DH ** -0.5)), (256, 18, tk(GATE, 18))]),
            (256, [(0, 256, both([KCc[:, 0], KCc[:, 1]]))]),
            (256, [(0, 256, tk(VC, 256))])]
        r, at = [], 0
        for n, (width, plan) in enumerate(plans):
            r += pieces(plan, width, b + n, at)
            at += len(plan)
        return r

    def project_mla(b):
        w = ring[:, (b + 7) % SLOTS, :]
        uq = w[:, 0:1152].rearrange("p (k n) -> p k n", k=2)
        ukv = w[:, 1152:1920].rearrange("p (m n) -> p m n", m=A_HEADS)
        r = []
        for m in range(A_HEADS):
            r.append(job([(uq[:, 0, 96 * m:96 * m + 96], CQ[:, 0]), (uq[0:64, 1, 96 * m:96 * m + 96], CQ[0:64, 1])],
                         0, 96, T, QA[0:96, m], scale=A_DK ** -0.5))
        for m in range(A_HEADS):
            r.append(job([(ukv[:, m, 0:64], CKV[:, 0])], 0, 64, T, KA[0:64, m]))
        for i in range(NT):
            r.append(job([(CKV[:, 0, i * P:(i + 1) * P], ukv[:, :, 64:128])], 0, P, 384, VA[:, i]))
        return with_items(r, b + 7)

    def project_out(b):
        r, at = [], 0
        for n, width in enumerate((384, 384, 256)):
            plan = [(c, min(256, width - c), feats([(P * j, P, x[:, 3 * n + c // P + j], 0, None) for j in range(min(2, (width - c) // P))],
                                                   OT_HI, OT_LO, add=True)) for c in range(0, width, 256)]
            r += pieces(plan, width, b + n, at, fresh=ITEM)
            at += len(plan)
        return r

    def project_second(b):
        tok = [V[:, :, c:c + 256] for V in (VD, VI, GG) for c in (0, 256)]
        dst = [X[:, j] for X in (QD, KD, HQ, ZF, ZB) for j in range(4)]
        take = lambda n: feats([(P * j, P, dst.pop(0), 0, None) for j in range(n)])
        r, at = [], 0
        for n in range(11):
            if n < 6:
                plan = [(0, 256, toks(256, [tok[n][:, i] for i in range(NT)])), (256, 128, take(1))]
            else:
                plan = [(0, 256, take(2))] + ([(256, 128, take(1))] if n < 10 else [])
            r += pieces(plan, 384 if n < 10 else 256, b + n, at)
            at += len(plan)
        return r

    def unit(tiles, c0, mode, gate=None, bias=None):
        return dict(tiles=tiles, out=O[:, :, c0:c0 + 64], mode=mode, gate=gate, bias=bias)

    def causal(q, k, v):
        return [dict(q=q[:, i * P:(i + 1) * P], k=k[:, 0:(i + 1) * P], n=(i + 1) * P, mask=(tri16, i * P),
                     v=[v(j) for j in range(i + 1)], rows=P) for i in range(NT)]

    def mixer_units():
        r = []
        for m in range(A_HEADS):
            r.append(unit(causal(QA[0:96, m], KA[0:96, m], lambda j: VA[:, j, 64 * m:64 * m + 64]), 64 * m, "set"))
        for g in range(B_GROUPS):
            s = slice(64 * g, 64 * g + 64)
            for j in range(B_HPG):
                m = g * B_HPG + j
                c0 = 384 + 64 * m
                r.append(unit([dict(q=QB[s, j, i * P:(i + 1) * P], k=KCMP[s, :], n=N_CMP, mask=(cmp16(i), 0),
                                    v=[VCMP[0:N_CMP, g, :]], rows=N_CMP) for i in range(NT)], c0, "set", GATE[:, :, 3 * m]))
                for w in (1, 2):
                    r.append(unit(causal(QB[s, j], KB[s, 1 + w], lambda t: VB[:, t, 128 * (w - 1) + 64 * g:128 * (w - 1) + 64 * g + 64]),
                                  c0, "add", GATE[:, :, 3 * m + w]))
        for m in range(C_HEADS):
            for comp in range(2):
                r0 = 64 * (m % 2) + 32 * comp
                s = slice(r0, r0 + 32)
                r.append(unit(causal(QC[s, m // 2], KCc[s, m // 2], lambda j: VC[:, j, 64 * m:64 * m + 64]),
                              768 + 64 * m, "add" if comp else "set", LAM[:, 3:4].to_broadcast([P, NT]) if comp else None))
        return r

    def share_of(units, n):
        b = sum(u["mode"] == "add" for u in units[:n]) % 2
        return share[:, b].rearrange("p (i n) -> p i n", i=NT)

    def dilated_units():
        r = []
        for m in range(E_HEADS):
            s = slice(64 * (m % 2), 64 * (m % 2) + 64)
            r.append(unit([dict(q=QD[s, m // 2, i * P:(i + 1) * P], k=KD[s, m // 2], n=T, mask=None,
                                v=[VD[:, j, 64 * m:64 * m + 64] for j in range(NT)], rows=P) for i in range(NT)],
                          64 * m, "set", bias=m))
        return r

    HB = view(16384, 2 * 896, a=2)
    SB = sq

    def norm_x(at):
        return [dict(src=[x[:, k] for k in range(KC)], dst=[h[:, k] for k in range(KC)], gain=[col(at + k) for k in range(KC)],
                     rows=[P] * KC, ones=ones, width=D)]

    def norm_final():
        return [dict(norm_x(COL_FINAL)[0], dst=[x[:, k] for k in range(KC)])]

    def norm_mla(l):
        a = COL_MLAQ + 2 * l
        return [dict(src=[CQ[:, 0], CQ[0:64, 1]], dst=[CQ[:, 0], CQ[0:64, 1]], gain=[col(a), col(a + 1, slice(0, 64))],
                     rows=[P, 64], ones=ones, width=A_QR),
                dict(src=[CKV[:, 0]], dst=[CKV[:, 0]], gain=[col(COL_MLAKV + l)], rows=[P], ones=ones, width=128)]

    def norm_heads():
        return [dict(src=[X[:, j]], dst=[X[:, j]], gain=[col(g)], rows=[P], ones=cst(C_BLK, P), width=64)
                for X, g in ((QD, COL_DQ), (KD, COL_DK)) for j in range(4)]

    def ropes_first():
        r = [(QB[:, j], cst(C_RB, P), COS[1], SIN[1]) for j in range(3)]
        r += [(KB[:, j], cst(C_RB, P), COS[1], SIN[1]) for j in (0, 2, 3)]
        r += [(X[:, j], cst(C_RC, P), COS[2], SIN[2]) for X in (QC, KCc) for j in range(2)]
        s = slice(64, 96)
        r += [(KPE[s, 0], const[s, C_RA + 64:C_RA + 96], COS[0][s, :], SIN[0][s, :])]
        return r

    def ropes_mla():
        s = slice(0, 96)
        return [(QA[s, m], const[s, C_RA:C_RA + 96], COS[0][s, :], SIN[0][s, :]) for m in range(A_HEADS)]

    def meet(e, c, own):
        e.drain().then_inc(met[own], c.one(met[own]))
        for s in met.values():
            e.wait_ge(s, c.own[met[own].name])


    PAIRS = [[(1, 0), (2, 1), (3, 2), (2, 0), (3, 1), (3, 0)], [(0, 1), (1, 2), (2, 3), (0, 2), (1, 3), (0, 3)]]

    def cum(d):
        o = 1 - d
        return BC[:, :, o:o + P]

    def halves(buf, m):
        v = buf.rearrange("p (j w) -> p j w", w=2 * m)
        return v[:, :, 0:m], v[:, :, m:2 * m]

    def gathered():
        return [job([(H[:, i, P * q:P * q + P], CHOICE[:, i, 512 * s:512 * s + 512]) for i in range(NT) for H in (HTOK_HI, HTOK_LO)],
                    0, P, 512, XIN[:, q, 512 * s:512 * s + 512]) for q in range(KC) for s in range(2)]

    block_cm = nc.Block()
    block = block_cm.__enter__()
    per_layer = 2 * FFN_ITEMS + MIX_ITEMS
    base_second = LAYERS * per_layer
    base_moe = base_second + SECOND_ITEMS
    STAGES_BEFORE_ROUTER = 2 + 6 * LAYERS + 7
    STAGES_BEFORE_MOE = STAGES_BEFORE_ROUTER + 5
    assert base_moe % SLOTS == 0

    released, counts = [], {}

    def release(sem_, n):
        counts[sem_.name] = counts.get(sem_.name, 0) + n
        return sem_, counts[sem_.name]

    def release_jobs(jobs):
        for j in jobs:
            r = release(prod_ready, 1)
            if j["free"]:
                released.append(r)

    for l in range(LAYERS):
        released += [release(down_split, 1) for n in range(FFN_ITEMS)]
        release_jobs(project_one(0))
        release_jobs(project_mla(0))
        released += [release(cmp_ready, 2 * B_GROUPS + 1)] * 2
        release_jobs(project_out(0))
        released += [release(down_split, 1) for n in range(FFN_ITEMS)]
    release_jobs(project_second(0))
    release_jobs(project_out(0))
    assert len(released) == base_moe

    @block.sync
    def _(sp):
        for dst, src in ((cols, cols_in), (rows, rows_in), (const, const_in)):
            sp.dma_start(dst, src).then_inc(consts_in, 16)
        sp.dma_start(x, x_in).then_inc(consts_in, 16)
        sp.dma_start(mix[:, 0:T].bitcast(I32), pos_in).then_inc(consts_in, 16)

        def load(n, src):
            if n >= SLOTS:
                sp.wait_ge(*released[n - SLOTS])
            sp.dma_start(ring[:, n % SLOTS, :], src).then_inc(w_in[n % SLOTS], 16)

        def load_loop(n, src, trips):
            with sp.Fori(1, 1 + trips) as i:
                for r in range(SLOTS):
                    done, v = released[n + r]
                    each = released[n + r + 1][1] - v
                    sp.wait_ge(done, (i - 1) * (SLOTS * each) + v)
                    sp.dma_start(ring[:, (n + r) % SLOTS, :],
                                 src[bass.ds(i * SLOTS + r, 1)].rearrange("a p n -> (a p) n")).then_inc(w_in[(n + r) % SLOTS], 16)

        def load_ffn(n, src):
            for r in range(SLOTS):
                load(n + r, src[r])
            load_loop(n, src, FFN_TRIPS)
            for r in range(SLOTS * (FFN_TRIPS + 1), FFN_ITEMS):
                load(n + r, src[r])

        for l in range(LAYERS):
            b = l * per_layer
            load_ffn(b, ffn_w[2 * l])
            for r in range(MIX_ITEMS):
                load(b + FFN_ITEMS + r, mix_w[l, r])
            load_ffn(b + FFN_ITEMS + MIX_ITEMS, ffn_w[2 * l + 1])
        for r in range(SECOND_ITEMS):
            load(base_second + r, second_w[r])
        for r in range(MOE_SLOTS):
            if r < SLOTS:
                sp.wait_ge(*released[base_moe + r - SLOTS])
            elif r == SLOTS:
                sp.wait_ge(met["dve"], STAGES_BEFORE_ROUTER)
            elif r == SLOTS + 1:
                for s in met.values():
                    sp.wait_ge(s, STAGES_BEFORE_MOE)
            sp.dma_start(MOE_SLOT[r], moe_w[r]).then_inc(moe_in[r], 16)
        with sp.Fori(1, N_EXPERTS * MOE_ITEMS // MOE_SLOTS) as i:
            for r in range(MOE_SLOTS):
                sp.wait_ge(y_ready, i * MOE_SLOTS + (r + 1 - MOE_SLOTS))
                sp.dma_start(MOE_SLOT[r], moe_w[bass.ds(i * MOE_SLOTS + r, 1)].rearrange("a p n -> (a p) n")).then_inc(moe_in[r], 16)
        sp.wait_ge(down_used, LAYERS * 2 * FFN_ITEMS * KC + (N_EXPERTS // 2) * KC)
        sp.dma_start(out, x).then_inc(stored, 16)
        sp.wait_ge(stored, 16)

    @block.gpsimd
    def _(pool):
        c = Count()
        pool.memset(ones, 1.0)
        pool.wait_ge(consts_in, 80)
        meet(pool, c, "pool")
        meet(pool, c, "pool")

        def ropes(list_):
            for X, R, cos, sin in list_:
                pool.wait_ge(cos_done, c.made(cos_done))
                pool.wait_ge(rot_ready, c.next(rot_ready))
                pool.tensor_tensor(X, X, cos, ALU.mult).then_inc(cos_done, c.one(cos_done))

        def low_parts():
            for k in range(KC):
                pool.wait_ge(high_ready, c.next(high_ready))
                pool.tensor_tensor(h_lo[:, k], prob[:, k % 2], h_hi[:, k].bitcast(F32), ALU.subtract).then_inc(low_ready, 1)

        def gemm(jobs, parts):
            for n, q in enumerate([j["piece"] for j in jobs if j["piece"]]):
                if n == 1:
                    parts()
                pool.wait_ge(piece_high, c.next(piece_high))
                pool.tensor_tensor(q["lo"], q["raw"], q["hi"].bitcast(F32), ALU.subtract).then_inc(piece_split, 1)

        def transposed(raw, hi, lo):
            for q in range(KC):
                pool.wait_ge(fold_copied, c.next(fold_copied))
                pool.tensor_tensor(lo(q), raw(q), hi(q).bitcast(F32), ALU.subtract).then_inc(fold_split, 1)

        def mixed_parts():
            transposed(lambda q: OT[:, q], lambda q: OT_HI[:, q], lambda q: OT_LO[:, q])

        def ffn(base, norm_stage=False):
            def up_low(n):
                w, s = ring[:, (base + n) % SLOTS, 0:2048], W_UP[:, n % 2]
                pool.wait_ge(w_high, c.next(w_high))
                pool.tensor_tensor(s[:, 1], w, s[:, 0].bitcast(F32), ALU.subtract).then_inc(up_split, 1)

            def down_low(n):
                w, s = ring[:, (base + n) % SLOTS, 2048:3072], W_DOWN[:, n % 2]
                pool.wait_ge(w_high, c.next(w_high))
                pool.tensor_tensor(s[:, 1], w, s[:, 0].bitcast(F32), ALU.subtract).then_inc(down_split, 1)

            if norm_stage:
                up_low(0)
                low_parts()
                up_low(1)
                down_low(0)
                return
            for n in range(SLOTS):
                up_low(n + 2)
                down_low(n + 1)
            with pool.Fori(0, FFN_TRIPS) as i:
                c.loop(i, {w_high: 2 * SLOTS})
                for r in range(SLOTS):
                    up_low(r + 2)
                    down_low(r + 1)
                c.looped(FFN_TRIPS)
            for n in range(SLOTS * (FFN_TRIPS + 1), FFN_ITEMS - 1):
                if n + 2 < FFN_ITEMS:
                    up_low(n + 2)
                down_low(n + 1)

        for l in range(LAYERS):
            b = l * per_layer
            ffn(b, norm_stage=True)
            ffn(b)
            gemm(project_one(b + FFN_ITEMS), low_parts)
            meet(pool, c, "pool")
            ropes(ropes_first())
            meet(pool, c, "pool")
            for m in range(A_HEADS):
                pool.tensor_copy(KA[64:96, m], KPE[64:96, 0])
            meet(pool, c, "pool")
            ropes(ropes_mla())
            meet(pool, c, "pool")
            units = mixer_units()
            for n, u in enumerate(units):
                if u["mode"] == "set":
                    c.skip(o_done)
                    continue
                pool.wait_ge(o_done, c.next(o_done))
                pool.wait_ge(share_used, c.made(share_used))
                pool.tensor_tensor(u["out"], u["out"], share_of(units, n), ALU.add).then_inc(share_used, c.one(share_used))
            meet(pool, c, "pool")
            meet(pool, c, "pool")
            gemm(project_out(b + FFN_ITEMS + 10), mixed_parts)
            ffn(b + FFN_ITEMS + MIX_ITEMS, norm_stage=True)
            ffn(b + FFN_ITEMS + MIX_ITEMS)
        pool.dma_start(table[:, 0:N_CONST2], const2_in).then_inc(second_in, 16)
        pool.wait_ge(second_in, 16)
        gemm(project_second(base_second), low_parts)
        for stage in ("projections", "head norms", "attention", "gates"):
            meet(pool, c, "pool")
        for m in range(H_HEADS):
            pool.wait_ge(head_mm, c.next(head_mm, 1, lag=1))
            pool.memset(AT, 0.0).then_inc(keys_ready, 1)
            pool.tensor_tensor(KSUM, K2[0][:, m].rearrange("p (i n) -> p i n", i=NT),
                               K2[1][:, m].rearrange("p (i n) -> p i n", i=NT), ALU.add).then_inc(keys_ready, 1)
        meet(pool, c, "pool")
        meet(pool, c, "pool")
        gemm(project_out(base_second + 11), mixed_parts)
        meet(pool, c, "pool")
        transposed(lambda q: HTOK[:, :, P * q:P * q + P], lambda q: HTOK_HI[:, :, P * q:P * q + P],
                   lambda q: HTOK_LO[:, :, P * q:P * q + P])
        for stage in ("router", "selection", "gather", "scatter matrices", "transposes", "experts"):
            meet(pool, c, "pool")

    @block.scalar
    def _(act):
        c = Count()
        meet(act, c, "act")

        def arrived(n):
            act.wait_ge(w_in[n % SLOTS], c.next(w_in[n % SLOTS], 16))

        def up_high(base, n):
            arrived(base + n)
            act.activation(W_UP[:, n % 2, 0], ring[:, (base + n) % SLOTS, 0:2048], ACT.Copy).then_inc(w_high, 1)

        def down_high(base, n):
            act.wait_ge(down_ready, c.next(down_ready, KC, lag=2 * KC))
            act.activation(W_DOWN[:, n % 2, 0], ring[:, (base + n) % SLOTS, 2048:3072], ACT.Copy).then_inc(w_high, 1)

        def norm(groups, split=False, after=None, splits=()):
            for g in groups:
                for s, r in zip(g["src"], g["rows"]):
                    if after is not None:
                        act.wait_ge(after, c.next(after))
                    b = c.own.get(sq_ready.name, 0) % 2
                    act.wait_ge(sq_used, c.next(sq_used, 1, lag=2))
                    act.activation(sq[0:r, b], s, ACT.Square).then_inc(sq_ready, c.one(sq_ready))
                for high in splits[:1]:
                    high()
                act.wait_ge(ms_ready, c.next(ms_ready))
                act.activation(rms, rms, ACT.Sqrt).then_inc(rms_ready, 1)
            for k in range(KC if split else 0):
                act.wait_ge(normed, c.next(normed))
                act.activation(h_hi[:, k], prob[:, k % 2], ACT.Copy).then_inc(high_ready, 1)
            for high in splits[1:]:
                high()

        def ffn_splits(base):
            return lambda: up_high(base, 0), lambda: up_high(base, 1), lambda: down_high(base, 0)

        def highs(jobs):
            todo = [j["piece"] for j in jobs if j["piece"]]

            def high():
                if todo:
                    q = todo.pop(0)
                    if q["first"]:
                        arrived(q["item"])
                    act.wait_ge(prod_ready, c.next(prod_ready, 0))
                    act.activation(q["hi"], q["raw"], ACT.Copy).then_inc(piece_high, 1)
            return high

        def gemm(jobs, high=None):
            for n, j in enumerate(jobs):
                if j["piece"] and n:
                    high()
                if n % 2 or j["add"]:
                    c.skip(prod_ready)
                    if not j["add"]:
                        c.skip(taken_dve)
                    continue
                act.wait_ge(prod_ready, c.next(prod_ready))
                act.activation(j["dst"], bank[n % 4][j["p0"]:j["p0"] + j["rows"], 0:j["n"]], ACT.Copy,
                               scale=j["scale"] or 1.0).then_inc(taken_act, 1)

        def transposed(dst, high=None):
            for q in range(KC):
                act.wait_ge(fold_ready, c.next(fold_ready))
                src = bank[4 + q % 2].rearrange("p (i n) -> p i n", i=NT) if len(dst[q].shape) == 3 else bank[4 + q % 2]
                if high:
                    act.activation(high[q], src, ACT.Copy)
                act.activation(dst[q], src, ACT.Copy).then_inc(fold_copied, 1)

        def project_mixed(jobs):
            high = highs(jobs)
            high()
            transposed([OT[:, q] for q in range(KC)], [OT_HI[:, q] for q in range(KC)])
            high()
            gemm(jobs, high)

        def ffn(base):
            def silu(n):
                act.wait_ge(gu_ready, c.next(gu_ready, lag=2))
                act.wait_ge(up_ready, c.next(up_ready))
                act.activation(SILU[:, n % 2], bank[n % 2], ACT.Silu).then_inc(silu_ready, 1)

            for n in range(SLOTS):
                silu(n)
                up_high(base, n + 2)
                down_high(base, n + 1)
            with act.Fori(0, FFN_TRIPS) as i:
                c.loop(i, {gu_ready: SLOTS, up_ready: SLOTS, down_ready: SLOTS * KC, **{s: 16 for s in w_in}})
                for r in range(SLOTS):
                    silu(r)
                    up_high(base, r + 2)
                    down_high(base, r + 1)
                c.looped(FFN_TRIPS)
            for n in range(SLOTS * (FFN_TRIPS + 1), FFN_ITEMS):
                silu(n)
                if n + 2 < FFN_ITEMS:
                    up_high(base, n + 2)
                if n + 1 < FFN_ITEMS:
                    down_high(base, n + 1)

        def attention(units):
            for a in range(NT * len(units)):
                u, n = units[a // NT], units[a // NT]["tiles"][a % NT]["n"]
                act.wait_ge(max_ready, c.next(max_ready))
                act.wait_ge(pT_ready, c.next(pT_ready, lag=3))
                src = SB[:, a % 2, 0:n] if u["bias"] is not None else SCORES[a % 3][:, 0:n]
                act.activation(prob[:, a % 3, 0:n], src, ACT.Exp, bias=NM[:, a % 4:a % 4 + 1],
                               accum_out=DEN[:, a % 8:a % 8 + 1]).then_inc(probs_ready, 1)

        def root(v):
            act.wait_ge(for_act, c.next(for_act))
            act.activation(v, v, ACT.Sqrt).then_inc(for_dve, 1)

        for n in range(3):
            for q in range(2):
                act.wait_ge(for_act, c.next(for_act))
                act.activation((SIN, COS)[q][n], ANGLE[n][q], ACT.Sin)
        meet(act, c, "act")

        for l in range(LAYERS):
            b = l * per_layer
            norm(norm_x(COL_FFN1 + 8 * l), split=True, after=down_used if l else None, splits=ffn_splits(b))
            ffn(b)
            c.skip(down_used, (FFN_ITEMS - 1) * KC)
            b += FFN_ITEMS
            jobs = project_one(b)
            high = highs(jobs)
            norm(norm_x(COL_MIX + 8 * l), split=True, after=down_used, splits=(high, high))
            gemm(jobs, high)
            for n in range(b + 7, b + 10):
                c.skip(w_in[n % SLOTS], 16)
            meet(act, c, "act")
            norm(norm_mla(l))
            c.skip(normed, 3)
            act.wait_ge(for_act, c.next(for_act))
            act.activation(LAM[:, 0:2], LAM[:, 0:2], ACT.Exp).then_inc(for_dve, 1)
            act.activation(GATE, GATE, ACT.Sigmoid).then_inc(for_dve, 1)
            meet(act, c, "act")
            gemm(project_mla(0))
            meet(act, c, "act")
            for part in range(2):
                for g in range(B_GROUPS):
                    s = slice(64 * g, 64 * g + 64)
                    act.wait_ge(cmp_bias, c.next(cmp_bias))
                    act.activation(HID[s, part], bank[4 + 2 * part + g][s, 0:N_CMP], ACT.Silu,
                                   bias=CB[s, part:part + 1]).then_inc(cmp_hid, 1)
            meet(act, c, "act")
            attention(mixer_units())
            meet(act, c, "act")
            root(MS16)
            meet(act, c, "act")
            project_mixed(project_out(b + 10))
            norm(norm_x(COL_FFN2 + 8 * l), split=True, after=taken_dve, splits=ffn_splits(b + MIX_ITEMS))
            ffn(b + MIX_ITEMS)
            c.skip(down_used, (FFN_ITEMS - 1) * KC)
        norm(norm_final(), after=down_used)
        jobs = project_second(base_second)
        high = highs(jobs)
        norm(norm_x(COL_N1), split=True, after=normed, splits=(high, high))
        gemm(jobs, high)
        meet(act, c, "act")
        norm(norm_heads())
        meet(act, c, "act")
        attention(dilated_units())
        meet(act, c, "act")

        act.wait_ge(for_act, c.next(for_act))
        act.activation(LBT, LBT, ACT.Exp).then_inc(for_dve, 1)
        for d in range(2):
            act.activation(K2[d], Z[d], ACT.Sigmoid, scale=-1.0).then_inc(step_act, c.one(step_act))
        act.wait_ge(step_act, c.made(step_act))
        for d in range(2):
            act.activation(Z[d], Z[d], ACT.Sigmoid).then_inc(for_dve, 1)
        act.activation(HQ, HQ, ACT.Silu)
        act.activation(GG, GG, ACT.Silu)
        for d in range(2):
            act.wait_ge(for_act, c.next(for_act))
            act.activation(Z[d], Z[d], ACT.Ln)
        meet(act, c, "act")

        for m in range(H_HEADS):
            for d in range(2):
                act.wait_ge(lvl_ready, c.next(lvl_ready, 0))
                act.wait_ge(scan_ready, c.next(scan_ready))
                act.activation(EE[:, 0].rearrange("p (i n) -> p i n", i=NT), cum(d), ACT.Exp)
                act.activation(ET, BC[:, :, P], ACT.Exp)
                act.wait_ge(diff_ready, c.next(diff_ready))
                act.activation(EE[:, 1], DD[:, 0], ACT.Exp).then_inc(fac_ready, 1)
                act.wait_ge(off_ready, c.next(off_ready))
                if m and d == 0:
                    act.wait_ge(head_mm, c.next(head_mm, 0))
                act.activation(AO[d][:, 0:3].rearrange("p i n -> p (i n)"), bank[0][:, 0:384], ACT.Copy)
                act.activation(AO[d][:, 3:6].rearrange("p i n -> p (i n)"), bank[1][:, 0:384], ACT.Copy).then_inc(off_copied, 1)
                for n, w in enumerate(LEVELS):
                    act.wait_ge(diff_ready, c.next(diff_ready))
                    act.wait_ge(lvl_ready, c.next(lvl_ready, 1, lag=2))
                    for src, dst, sign in zip(halves(DD[:, n % 2], w), halves(EE[:, n % 2], w), (-1.0, 1.0)):
                        last = act.activation(dst, src, ACT.Exp, scale=sign)
                    last.then_inc(decay_ready, 1)
            act.wait_ge(head_mm, c.next(head_mm))
            act.activation(O[:, :, 512 + P * m:512 + P * m + P], bank[7].rearrange("p (i n) -> p i n", i=NT),
                           ACT.Copy).then_inc(head_out, 1)
        meet(act, c, "act")
        root(MS16)
        meet(act, c, "act")
        project_mixed(project_out(base_second + 11))
        norm(norm_x(COL_N2), after=taken_dve)
        meet(act, c, "act")
        act.wait_ge(logit_max, c.next(logit_max))
        for i in range(NT):
            act.activation(AFF[:, i], bank[0][:, 16 * i:16 * i + 16], ACT.Exp, bias=NM[:, i:i + 1],
                           accum_out=DEN[:, i:i + 1]).then_inc(logit_exp, 1)
        transposed([HTOK[:, :, P * q:P * q + P] for q in range(KC)], [HTOK_HI[:, :, P * q:P * q + P] for q in range(KC)])
        meet(act, c, "act")
        meet(act, c, "act")
        gemm(gathered())
        meet(act, c, "act")
        meet(act, c, "act")
        transposed([GT[:, q] for q in range(KC)])
        meet(act, c, "act")
        with act.Fori(0, N_EXPERTS // 2) as i:
            c.loop(i, {gu_ready: 16, up_ready: 16, y_ready: 16})
            for n in range(16):
                act.wait_ge(gu_ready, c.next(gu_ready, 1, lag=2))
                act.wait_ge(up_ready, c.next(up_ready))
                act.activation(MG[:, n % 2, 0:64], bank[n % 2][:, 0:64], ACT.Silu).then_inc(silu_ready, 1)
            act.wait_ge(y_ready, c.next(y_ready, 16))
            act.activation(YS[:, 0:T], bank[2], ACT.Copy).then_inc(y_copied, 1)
            c.looped(N_EXPERTS // 2)
        meet(act, c, "act")

    @block.tensor
    def _(pe):
        c = Count()
        mm = nc.tensor.matmul
        meet(pe, c, "pe")
        meet(pe, c, "pe")

        def norm(groups, into=bank[7]):
            for g in groups:
                pe.wait_ge(ms_ready, c.next(ms_ready, 1, lag=1))
                for k, (s, r) in enumerate(zip(g["src"], g["rows"])):
                    b = c.at.get(sq_ready.name, 0) % 2
                    pe.wait_ge(sq_ready, c.next(sq_ready))
                    mm(into, g["ones"][0:r, :], sq[0:r, b], start=k == 0, stop=k == len(g["src"]) - 1).then_inc(sq_used, 1)

        def arrived(n):
            pe.wait_ge(w_in[n % SLOTS], c.next(w_in[n % SLOTS], 16))

        def gemm(jobs, split=True, parts=None):
            for n, j in enumerate(jobs):
                for item in j["need"]:
                    arrived(item)
                if j["piece"]:
                    pe.wait_ge(piece_split, c.next(piece_split))
                    if j["piece"]["first"]:
                        c.skip(w_in[j["piece"]["item"] % SLOTS], 16)
                if split:
                    taken = (taken_act, taken_dve)[n % 2]
                    pe.wait_ge(taken, c.next(taken, 1, lag=2))
                else:
                    pe.wait_ge(taken_dve, c.next(taken_dve, 1, lag=4))
                o = bank[n % 4][0:j["p0"] + j["rows"], 0:j["n"]]
                for k, (w, r) in enumerate(j["terms"]):
                    if parts is not None and n == 0 and k % 3 == 0:
                        pe.wait_ge(parts, c.next(parts))
                    last = mm(o, w, r, start=k == 0, stop=k == len(j["terms"]) - 1)
                last.then_inc(prod_ready, 1)

        def transposed(src):
            for q in range(KC):
                pe.wait_ge(fold_copied, c.next(fold_copied, 1, lag=2))
                for i in range(NT):
                    last = nc.tensor.transpose(bank[4 + q % 2][:, P * i:P * i + P], src(q, i), ident)
                last.then_inc(fold_ready, 1)

        def ropes(list_):
            for n, (X, R, cos, sin) in enumerate(list_):
                pe.wait_ge(rope_done, c.next(rope_done, 1, lag=4))
                p0, r = X.start_partition(), X.shape[0]
                mm(bank[n % 4][p0:p0 + r, :], R, X, start=True, stop=True).then_inc(rot_ready, 1)

        def ffn(base):
            for n in range(FFN_ITEMS):
                c.skip(w_in[(base + n) % SLOTS], 16)

            def up(n, first=False):
                pe.wait_ge(up_split, c.next(up_split))
                w = W_UP[:, n % 2].rearrange("p s (a k n) -> p s a k n", a=2, k=KC)
                for a in range(2):
                    for k in range(KC):
                        if first and a == 0:
                            pe.wait_ge(low_ready, c.next(low_ready))
                        mm(bank[n % 2 + 2 * a], w[:, 0, a, k], h_lo[:, k], start=k == 0, stop=False)
                        mm(bank[n % 2 + 2 * a], w[:, 0, a, k], h_hi[:, k], start=False, stop=False)
                        last = mm(bank[n % 2 + 2 * a], w[:, 1, a, k], h_hi[:, k], start=False, stop=k == KC - 1)
                last.then_inc(up_ready, 1)

            def down(n):
                w, g = W_DOWN[:, n % 2], GU_PARTS[:, n % 2]
                pe.wait_ge(down_split, c.next(down_split))
                pe.wait_ge(gu_ready, c.next(gu_ready))
                for q in range(KC):
                    pe.wait_ge(down_used, c.next(down_used, 1, lag=4))
                    mm(bank[4 + q % 4], w[:, 0, P * q:P * q + P], g[:, 1], start=True, stop=False)
                    mm(bank[4 + q % 4], w[:, 0, P * q:P * q + P], g[:, 0], start=False, stop=False)
                    mm(bank[4 + q % 4], w[:, 1, P * q:P * q + P], g[:, 0], start=False, stop=True).then_inc(down_ready, 1)

            up(0, first=True)
            for n in range(SLOTS):
                up(n + 1)
                down(n)
            with pe.Fori(0, FFN_TRIPS) as i:
                c.loop(i, {gu_ready: SLOTS, down_used: SLOTS * KC, up_split: SLOTS, down_split: SLOTS})
                for r in range(SLOTS):
                    up(r + 1)
                    down(r)
                c.looped(FFN_TRIPS)
            for n in range(SLOTS * (FFN_TRIPS + 1), FFN_ITEMS):
                if n + 1 < FFN_ITEMS:
                    up(n + 1)
                down(n)

        def attention(units):
            tiles = [t for u in units for t in u["tiles"]]

            def scores(a):
                t = tiles[a]
                o = SCORES[a % 3]
                last = mm(o[:, 0:t["n"]], t["q"], t["k"], start=True, stop=True)
                if t["mask"] is not None:
                    m, at = t["mask"]
                    last = mm(o[:, at:at + m.shape[1]], ident16, m, start=False, stop=True, skip_group_check=True)
                last.then_inc(scores_ready, 1)

            def turn(a):
                t = tiles[a]
                pe.wait_ge(probs_ready, c.next(probs_ready))
                for j in range(len(t["v"])):
                    last = nc.tensor.transpose(bank[2 + a % 2][0:t["rows"], P * j:P * j + P],
                                               prob[:, a % 3, P * j:P * j + t["rows"]], ident)
                last.then_inc(pT_ready, 1)

            def values(a):
                t = tiles[a]
                o = bank[4 + a // NT % 2][:, 64 * (a % NT):64 * (a % NT) + 64]
                pe.wait_ge(pT_copied, c.next(pT_copied))
                if a % NT == 0:
                    pe.wait_ge(o_done, c.next(o_done, lag=2))
                for j, v in enumerate(t["v"]):
                    last = mm(o, probT[0:t["rows"], a % 2, P * j:P * j + P], v, start=j == 0, stop=j == len(t["v"]) - 1)
                last.then_inc(pv_ready, 1)

            for a in range(len(tiles) + 3):
                if a < len(tiles):
                    scores(a)
                if 0 <= a - 2 < len(tiles):
                    turn(a - 2)
                if a >= 3:
                    values(a - 3)

        for l in range(LAYERS):
            b = l * per_layer
            norm(norm_x(COL_FFN1 + 8 * l), into=bank[0])
            ffn(b)
            b += FFN_ITEMS
            norm(norm_x(COL_MIX + 8 * l), into=bank[0])
            gemm(project_one(b), parts=low_ready)
            meet(pe, c, "pe")
            norm(norm_mla(l))
            ropes(ropes_first())
            meet(pe, c, "pe")
            gemm(project_mla(b))
            meet(pe, c, "pe")
            ropes(ropes_mla())
            w = [ring[:, (b + 8 + part) % SLOTS, :] for part in range(2)]
            for part in range(2):
                arrived(b + 8 + part)
                for g in range(B_GROUPS):
                    s = slice(64 * g, 64 * g + 64)
                    o = bank[4 + 2 * part + g]
                    for i in range(CMP_LEN):
                        mm(o[s, 0:N_CMP], w[part][s, 64 * i:64 * i + 64], KB[s, part, i:i + CMP_STRIDE * (N_CMP - 1) + 1:CMP_STRIDE],
                           start=i == 0, stop=i == CMP_LEN - 1)
                    pe0 = COL_PE + (2 * l + part) * CMP_LEN
                    for i in range(CMP_LEN):
                        last = mm(o[s, 32:33], w[part][s, 64 * i:64 * i + 64], cols[s, pe0 + i:pe0 + i + 1],
                                  start=i == 0, stop=i == CMP_LEN - 1)
                    last.then_inc(cmp_ready, 1)
            pe.wait_ge(cmp_hid, c.next(cmp_hid, 4))
            for g in range(B_GROUPS):
                s = slice(64 * g, 64 * g + 64)
                mm(bank[4][s, 64:64 + N_CMP], w[0][s, 2048:2112], HID[s, 0], start=True, stop=True)
                last = mm(bank[5 + g][0:N_CMP, 64:128], HID[s, 1], w[1][s, 2048:2112], start=True, stop=True)
            last.then_inc(cmp_ready, 1)
            meet(pe, c, "pe")
            attention(mixer_units())
            meet(pe, c, "pe")
            meet(pe, c, "pe")
            transposed(lambda q, i: O[:, i, P * q:P * q + P])
            gemm(project_out(b + 10), split=False, parts=fold_split)
            norm(norm_x(COL_FFN2 + 8 * l))
            ffn(b + MIX_ITEMS)
        norm(norm_final(), into=bank[0])
        norm(norm_x(COL_N1))
        gemm(project_second(base_second), parts=low_ready)
        meet(pe, c, "pe")
        norm(norm_heads())
        meet(pe, c, "pe")
        attention(dilated_units())
        meet(pe, c, "pe")
        meet(pe, c, "pe")

        for m in range(H_HEADS):
            for d in range(2):
                pe.wait_ge(qk_ready, c.next(qk_ready))
                pe.wait_ge(off_copied, c.next(off_copied, 1, lag=1))
                for n, (I, J) in enumerate(PAIRS[d]):
                    q = QT[:, I] if n < 3 else QX[:, n - 3]
                    last = mm(bank[n // 3][:, P * (n % 3):P * (n % 3) + P], KT[:, J], q, start=True, stop=True)
                last.then_inc(off_ready, 1)
                for n, w in enumerate(LEVELS):
                    pe.wait_ge(lvl_ready, c.next(lvl_ready))
                    pe.wait_ge(lvl_put, c.next(lvl_put, 1, lag=2))
                    for i in range(NT):
                        blk = MM[:, n % 2, P * i:P * i + P]
                        last = mm(bank[2 + n % 2][:, 64 * i:64 * i + 64], blk, halves(blk, w)[1 - d], start=True, stop=True)
                    last.then_inc(lvl_mm, 1)
            pe.wait_ge(keys_ready, c.next(keys_ready, 2))
            for i in range(NT):
                last = mm(bank[6][:, P * i:P * i + P], KSUM[:, i], HQ[:, m, P * i:P * i + P], start=True, stop=True)
            last.then_inc(diag_mm, 1)
            pe.wait_ge(diag_put, c.next(diag_put))
            pe.wait_ge(off_copied, c.next(off_copied, 0))
            pe.wait_ge(head_out, c.next(head_out, 1, lag=1))
            for I in range(NT):
                terms = [(AT[:, I], I)] + [(AO[d][:, n], J) for d in range(2) for n, (i, J) in enumerate(PAIRS[d]) if i == I]
                for k, (w, J) in enumerate(terms):
                    last = mm(bank[7][:, P * I:P * I + P], w, VI[:, J, P * m:P * m + P], start=k == 0, stop=k == len(terms) - 1)
            last.then_inc(head_mm, 1)
        meet(pe, c, "pe")
        meet(pe, c, "pe")
        transposed(lambda q, i: O[:, i, P * q:P * q + P])
        gemm(project_out(base_second + 11), split=False, parts=fold_split)
        norm(norm_x(COL_N2))
        meet(pe, c, "pe")
        for i in range(NT):
            for k in range(KC):
                last = mm(bank[0][:, 16 * i:16 * i + 16], h[:, k, P * i:P * i + P], RW[:, k, :], start=k == 0, stop=k == KC - 1)
        last.then_inc(logit_ready, 1)
        transposed(lambda q, i: h[:, q, P * i:P * i + P])
        pe.wait_ge(aff_ready, c.next(aff_ready))
        for i in range(NT):
            last = nc.tensor.transpose(bank[1][0:16, P * i:P * i + P], AFF[:, i], ident)
        last.then_inc(affT_ready, 1)
        pe.wait_ge(slotT_ready, c.next(slotT_ready))
        for i in range(NT):
            last = nc.tensor.transpose(bank[2][:, 16 * i:16 * i + 16], SLOTT[0:16, P * i:P * i + P], ident[0:16, 0:16])
        last.then_inc(slot_ready, 1)
        meet(pe, c, "pe")
        meet(pe, c, "pe")
        gemm(gathered())
        meet(pe, c, "pe")
        meet(pe, c, "pe")
        transposed(lambda q, i: SEL[:, i, P * q:P * q + P])
        meet(pe, c, "pe")
        with pe.Fori(0, N_EXPERTS // 2) as i:
            c.loop(i, {gu_ready: 16, y_copied: 2, down_used: KC, **{s: 32 for s in moe_in}})

            def up(n):
                pe.wait_ge(moe_in[n % MOE_SLOTS], c.next(moe_in[n % MOE_SLOTS], 16))
                w = MOE_SLOT[n % MOE_SLOTS][:, 0:2048].rearrange("p (a k n) -> p a k n", a=2, k=KC)
                for a in range(2):
                    for k in range(KC):
                        last = mm(bank[n % 2][:, 64 * a:64 * a + 64], w[:, a, k, :],
                                  XIN[:, k, bass.ds(i * P + 64 * (n // MOE_ITEMS), 64)], start=k == 0, stop=k == KC - 1)
                last.then_inc(up_ready, 1)

            up(0)
            for n in range(16):
                if n < 15:
                    up(n + 1)
                e = n // MOE_ITEMS
                pe.wait_ge(gu_ready, c.next(gu_ready))
                for s in range(2):
                    last = mm(bank[2 + s][64 * e:64 * e + 64, :], MGU[:, n % 2, 0:64],
                              MOE_SLOT[n % MOE_SLOTS][:, 2048 + 512 * s:2560 + 512 * s], start=n % 8 == 0, stop=n % 8 == 7)
                last.then_inc(y_ready, 1)
            pe.wait_ge(y_copied, c.next(y_copied, 2))
            for q in range(KC):
                pe.wait_ge(down_used, c.next(down_used, 1, lag=4))
                mm(bank[4 + q % 4], YS[:, P * q:P * q + P], GT[:, bass.ds(i, 1), :].rearrange("p a n -> p (a n)"),
                   start=True, stop=True).then_inc(down_ready, 1)
            c.looped(N_EXPERTS // 2)
        meet(pe, c, "pe")

    @block.vector
    def _(dve):
        c = Count()
        V = nc.vector
        meet(dve, c, "dve")

        def step(ins):
            ins.then_inc(step_dve, c.one(step_dve))
            dve.wait_ge(step_dve, c.made(step_dve))

        V.tensor_copy(ident16, ident)
        V.tensor_copy(tri16, cst(C_TRI, P))
        V.tensor_copy(mask16[:, 2 * P:], cst(C_CMP, NT * N_CMP))
        posf, ang, rnd, tmp = (mix[:, 512 * n:512 * n + 512] for n in range(1, 5))
        step(V.tensor_copy(posf, mix[:, 0:T].bitcast(I32)))
        for n in range(3):
            s, k = ANGLE[n]
            step(V.tensor_scalar(ang, posf, cst(C_INV + n), None, ALU.mult))
            step(V.tensor_scalar(rnd, ang, 1 / (2 * math.pi), ROUND, ALU.mult, ALU.add))
            step(V.tensor_scalar(rnd, rnd, -ROUND, None, ALU.add))
            for part in TWO_PI:
                step(V.scalar_tensor_tensor(ang, rnd, -part, ang, ALU.mult, ALU.add))
            step(V.tensor_scalar(tmp, ang, math.pi / 2, None, ALU.add))
            step(V.tensor_scalar(rnd, tmp, math.pi, -2 * math.pi, ALU.is_gt, ALU.mult))
            step(V.tensor_tensor(tmp, tmp, rnd, ALU.add))
            V.tensor_scalar(s, ang, SIN_MAX, -SIN_MAX, ALU.min, ALU.max).then_inc(for_act, 1)
            V.tensor_scalar(k, tmp, SIN_MAX, -SIN_MAX, ALU.min, ALU.max).then_inc(for_act, 1)
            dve.wait_ge(for_act, 2 * n + 2)
        meet(dve, c, "dve")

        def norm(groups, split=False, sums=bank[7]):
            for g in groups:
                dve.wait_ge(sq_used, c.next(sq_used, len(g["src"])))
                dve.wait_ge(normed, c.made(normed))
                V.tensor_scalar(rms, sums, 1.0 / g["width"], EPS, ALU.mult, ALU.add).then_inc(ms_ready, 1)
                dve.wait_ge(rms_ready, c.next(rms_ready))
                step(V.reciprocal(rms, rms))
                for k, (s, o, gain, r) in enumerate(zip(g["src"], g["dst"], g["gain"], g["rows"])):
                    if split:
                        o = prob[:, k % 2]
                        dve.wait_ge(low_ready, c.next(low_ready, lag=2))
                    V.scalar_tensor_tensor(o, s, gain, rms[0:r, :], ALU.mult, ALU.mult).then_inc(normed, c.one(normed))

        def gemm(jobs, split=True):
            for n, j in enumerate(jobs):
                if split and n % 2 == 0:
                    c.skip(prod_ready)
                    continue
                dve.wait_ge(prod_ready, c.next(prod_ready))
                src = bank[n % 4][j["p0"]:j["p0"] + j["rows"], 0:j["n"]]
                if j["add"]:
                    ins = V.tensor_tensor(j["dst"], src, j["dst"], ALU.add)
                elif j["scale"]:
                    ins = V.tensor_scalar(j["dst"], src, j["scale"], None, ALU.mult)
                else:
                    ins = V.tensor_copy(j["dst"], src)
                ins.then_inc(taken_dve, 1)

        def ropes(list_):
            for n, (X, R, cos, sin) in enumerate(list_):
                p0, r = X.start_partition(), X.shape[0]
                t = sq[p0:p0 + r, n % 2]
                dve.wait_ge(rot_ready, c.next(rot_ready))
                step(V.tensor_tensor(t, bank[n % 4][p0:p0 + r, :], sin, ALU.mult))
                dve.wait_ge(cos_done, c.next(cos_done))
                V.tensor_tensor(X, X, t, ALU.add).then_inc(rope_done, c.one(rope_done))

        def hidden(n, silu_, up_, dst):
            dve.wait_ge(silu_ready, c.next(silu_ready))
            V.tensor_tensor(dst, silu_, up_, ALU.mult).then_inc(gu_ready, c.one(gu_ready))

        def hidden_parts(n):
            g = GU_PARTS[:, n % 2]
            dve.wait_ge(silu_ready, c.next(silu_ready))
            V.tensor_tensor(GU[:, n % 2], SILU[:, n % 2], bank[2 + n % 2], ALU.mult)
            step(V.tensor_tensor(g[:, 0], SILU[:, n % 2], bank[2 + n % 2], ALU.mult))
            V.tensor_tensor(g[:, 1], GU[:, n % 2], g[:, 0].bitcast(F32), ALU.subtract).then_inc(gu_ready, c.one(gu_ready))

        def add_down(scale):
            for q in range(KC):
                dve.wait_ge(down_ready, c.next(down_ready))
                dve.wait_ge(down_used, c.made(down_used, lag=KC - 1))
                V.scalar_tensor_tensor(x[:, q], bank[4 + q % 4], scale, x[:, q], ALU.mult, ALU.add).then_inc(down_used, c.one(down_used))

        def ffn():
            def both(n):
                add_down(0.5)
                hidden_parts(n + 1)
            hidden_parts(0)
            for n in range(SLOTS):
                both(n)
            with dve.Fori(0, FFN_TRIPS) as i:
                c.loop(i, {silu_ready: SLOTS, gu_ready: SLOTS, down_ready: SLOTS * KC, down_used: SLOTS * KC, step_dve: SLOTS})
                for r in range(SLOTS):
                    both(r)
                c.looped(FFN_TRIPS)
            for n in range(SLOTS * (FFN_TRIPS + 1), FFN_ITEMS - 1):
                both(n)
            add_down(0.5)

        def attention(units):
            tiles = [t for u in units for t in u["tiles"]]
            before = c.at.get(pv_ready.name, 0)

            def maximum(a):
                bias, i, n = units[a // NT]["bias"], a % NT, tiles[a]["n"]
                src = SCORES[a % 3][:, 0:n]
                if bias is not None:
                    hb = HB[:, bias % 2]
                    if i == 0:
                        step(V.scalar_tensor_tensor(hb, table[:, C2_DIST:C2_DIST + 896], -(2.0 ** -(bias + 1)),
                                                    table[:, C2_MULT:C2_MULT + 896], ALU.mult, ALU.add))
                    at = 384 - P * i
                    dve.wait_ge(scores_ready, c.next(scores_ready))
                    dve.wait_ge(probs_ready, c.next(probs_ready, lag=2))
                    step(V.scalar_tensor_tensor(SB[:, a % 2], src, E_DH ** -0.5, hb[:, at:at + T], ALU.mult, ALU.add))
                    src = SB[:, a % 2]
                else:
                    dve.wait_ge(scores_ready, c.next(scores_ready))
                    c.skip(probs_ready)
                V.tensor_reduce(NM[:, a % 4:a % 4 + 1], src, AX.X, ALU.max, negate=True).then_inc(max_ready, 1)

            def copied(a):
                t = tiles[a]
                n = P * len(t["v"])
                dve.wait_ge(pT_ready, c.next(pT_ready))
                dve.wait_ge(pv_ready, c.next(pv_ready, lag=2))
                V.tensor_copy(probT[0:t["rows"], a % 2, 0:n], bank[2 + a % 2][0:t["rows"], 0:n]).then_inc(pT_copied, 1)

            def result(n):
                u = units[n]
                d = DEN[:, 4 * (n % 2):4 * (n % 2) + 4]
                src = bank[4 + n % 2][:, 0:64 * NT].rearrange("p (i n) -> p i n", i=NT)
                w = RDEN
                step(V.reciprocal(RDEN, d))
                if u["gate"] is not None:
                    w = WGT
                    step(V.tensor_tensor(WGT, RDEN, u["gate"], ALU.mult))
                w = w.unsqueeze(2).to_broadcast([P, NT, 64])
                dve.wait_ge(pv_ready, before + NT * (n + 1))
                to = u["out"]
                if u["mode"] == "add":
                    to = share_of(units, n)
                    dve.wait_ge(share_used, c.next(share_used, lag=2))
                V.tensor_tensor(to, src, w, ALU.mult).then_inc(o_done, 1)

            for a in range(len(tiles) + 3):
                if a < len(tiles):
                    maximum(a)
                if 0 <= a - 2 < len(tiles):
                    copied(a - 2)
                if a >= 3 and (a - 3) % NT == NT - 1:
                    result((a - 3) // NT)

        def head_norm(col0, heads, n, gain, factor, gate=None):
            v = O[:, :, col0:col0 + heads * n].rearrange("p i (m n) -> p i m n", m=heads)
            sqv = SUBSQ[:, 0:NT * heads * n]
            step(V.tensor_tensor(sqv.rearrange("p (i m n) -> p i m n", i=NT, m=heads), v, v, ALU.mult))
            step(V.tensor_reduce(MS16, sqv.rearrange("p (a n) -> p a n", n=n), AX.X, ALU.add))
            V.tensor_scalar(MS16, MS16, 1.0 / n, EPS, ALU.mult, ALU.add).then_inc(for_act, 1)
            dve.wait_ge(for_dve, c.next(for_dve))
            step(V.reciprocal(MS16, MS16))
            g = SUBSQ[:, 0:n]
            step(V.tensor_scalar(g, gain, factor, None, ALU.mult))
            r = MS16.rearrange("p (i m) -> p i m", i=NT).unsqueeze(3).to_broadcast([P, NT, heads, n])
            step(V.tensor_tensor(v, v, r, ALU.mult))
            step(V.tensor_tensor(v, v, g.unsqueeze(1).unsqueeze(1).to_broadcast([P, NT, heads, n]), ALU.mult))
            if gate is not None:
                o = O[:, :, col0:col0 + heads * n]
                step(V.tensor_tensor(o, o, gate, ALU.mult))

        for l in range(LAYERS):
            lam_init = 0.8 - 0.6 * math.exp(-0.3 * l)
            norm(norm_x(COL_FFN1 + 8 * l), split=True, sums=bank[0])
            ffn()
            norm(norm_x(COL_MIX + 8 * l), split=True, sums=bank[0])
            gemm(project_one(0))
            meet(dve, c, "dve")
            norm(norm_mla(l))
            r0 = ROW_LAM + 4 * C_DH * l
            lp = small[:, 256:256 + 2 * C_DH]
            step(V.tensor_tensor(lp, rows[:, r0:r0 + 2 * C_DH], rows[:, r0 + 2 * C_DH:r0 + 4 * C_DH], ALU.mult))
            V.tensor_reduce(LAM[:, 0:2], lp.rearrange("p (a n) -> p a n", a=2), AX.X, ALU.add).then_inc(for_act, 1)
            ropes(ropes_first())
            dve.wait_ge(for_dve, c.next(for_dve))
            step(V.tensor_tensor(LAM[:, 2:3], LAM[:, 0:1], LAM[:, 1:2], ALU.subtract))
            V.tensor_scalar(LAM[:, 3:4], LAM[:, 2:3], -1.0, -lam_init, ALU.mult, ALU.add)
            dve.wait_ge(for_dve, c.next(for_dve))
            g0 = GATE[:, 0, 0:3 * B_HEADS:3]
            V.tensor_scalar(g0, g0, cst(C_ROWM), None, ALU.mult)
            meet(dve, c, "dve")
            gemm(project_mla(0))
            meet(dve, c, "dve")
            ropes(ropes_mla())
            for part in range(2):
                for g in range(B_GROUPS):
                    s = slice(64 * g, 64 * g + 64)
                    dve.wait_ge(cmp_ready, c.next(cmp_ready))
                    V.tensor_copy(CB[s, part:part + 1], bank[4 + 2 * part + g][s, 32:33]).then_inc(cmp_bias, 1)
            dve.wait_ge(cmp_ready, c.next(cmp_ready))
            V.tensor_copy(KCMP, bank[4][:, 64:64 + N_CMP])
            for g in range(B_GROUPS):
                V.tensor_copy(VCMP[0:N_CMP, g], bank[5 + g][0:N_CMP, 64:128])
            meet(dve, c, "dve")
            attention(mixer_units())
            meet(dve, c, "dve")
            head_norm(768, C_HEADS, 2 * C_DH, rows[:, ROW_SUB + 64 * l:ROW_SUB + 64 * l + 64], 1.0 - lam_init)
            meet(dve, c, "dve")
            gemm(project_out(0), split=False)
            norm(norm_x(COL_FFN2 + 8 * l), split=True)
            ffn()
        norm(norm_final(), sums=bank[0])
        norm(norm_x(COL_N1), split=True)
        gemm(project_second(0))
        meet(dve, c, "dve")
        norm(norm_heads())
        meet(dve, c, "dve")
        attention(dilated_units())
        meet(dve, c, "dve")

        V.tensor_tensor(LBT, cols[:, COL_LB + 8:COL_LB + 16], cols[:, COL_LB:COL_LB + 8], ALU.subtract).then_inc(for_act, 1)
        dve.wait_ge(for_dve, c.next(for_dve))
        step(V.tensor_scalar(LBT, LBT, 1.0, None, ALU.add))
        step(V.reciprocal(LB, LBT))
        step(V.tensor_scalar(OMLB, LB, -1.0, 1.0, ALU.mult, ALU.add))
        for d in range(2):
            dve.wait_ge(for_dve, c.next(for_dve))
            for m in range(H_HEADS):
                u = 4 * d + m
                V.tensor_scalar(K2[d][:, m], K2[d][:, m], OMLB[:, u:u + 1], None, ALU.mult)
                last = V.tensor_scalar(Z[d][:, m], Z[d][:, m], OMLB[:, u:u + 1], LB[:, u:u + 1], ALU.mult, ALU.add)
            last.then_inc(for_act, 1)
        V.memset(BC[:, :, 0:1], 0.0)
        meet(dve, c, "dve")

        for m in range(H_HEADS):
            q = HQ[:, m]
            for d in range(2):
                k = K2[d][:, m]
                for i in range(NT):
                    last = V.tensor_tensor_scan(BC[:, i, 1:P + 1], ones, Z[d][:, m, P * i:P * i + P], 0.0, ALU.mult, ALU.add)
                last.then_inc(scan_ready, c.one(scan_ready))
                dve.wait_ge(scan_ready, c.made(scan_ready))
                V.tensor_tensor(DD[:, 0].rearrange("p (i n) -> p i n", i=NT), BC[:, :, P:P + 1].to_broadcast([P, NT, P]),
                                cum(d), ALU.subtract).then_inc(diff_ready, c.one(diff_ready))
                dve.wait_ge(fac_ready, c.next(fac_ready))
                if m or d:
                    dve.wait_ge(off_ready, c.next(off_ready, 0))
                V.tensor_tensor(QT.rearrange("p i n -> p (i n)"), q, EE[:, d], ALU.mult).then_inc(step_dve, c.one(step_dve))
                V.tensor_tensor(KT.rearrange("p i n -> p (i n)"), k, EE[:, 1 - d], ALU.mult).then_inc(step_dve, c.one(step_dve))
                dve.wait_ge(step_dve, c.made(step_dve))
                step(V.tensor_scalar(QX[:, 0], QT[:, 0 if d else 2], ET[:, 1:2], None, ALU.mult))
                step(V.tensor_scalar(QX[:, 1], QT[:, 1 if d else 3], ET[:, 2:3], None, ALU.mult))
                V.tensor_scalar(QX[:, 2], QX[:, 1 - d], ET[:, 1 + d:2 + d], None, ALU.mult).then_inc(qk_ready, 1)
                dve.wait_ge(off_ready, c.next(off_ready))
                if d == 0:
                    dve.wait_ge(keys_ready, c.next(keys_ready, 2))

                def diff(n):
                    w = LEVELS[n]
                    v = cum(d).rearrange("p i (j w) -> p i j w", w=2 * w)
                    r = w if d else w - 1
                    V.tensor_tensor(DD[:, n % 2].rearrange("p (i j w) -> p i j w", i=NT, w=2 * w), v,
                                    v[:, :, :, r:r + 1].to_broadcast([P, NT, 64 // w, 2 * w]), ALU.subtract).then_inc(diff_ready, c.one(diff_ready))

                def product(n):
                    w = LEVELS[n]
                    dve.wait_ge(decay_ready, c.next(decay_ready))
                    e, o = halves(EE[:, n % 2], w), halves(MM[:, n % 2], w)
                    left, right = (q, k) if d else (k, q)
                    V.tensor_tensor(o[0], halves(left, w)[0], e[0], ALU.mult)
                    V.tensor_tensor(o[1], halves(right, w)[1], e[1], ALU.mult).then_inc(lvl_ready, 1)

                def put(n):
                    w = LEVELS[n]
                    dve.wait_ge(lvl_mm, c.next(lvl_mm))
                    at = C2_LVL + (d * len(LEVELS) + n) * 64
                    mask = table[:, at:at + 64].bitcast(I32).rearrange("p (j w) -> p j w", w=w)
                    o = AT.rearrange("p i (j w) -> p i j w", w=2 * w)
                    o = o[:, :, :, 0:w] if d else o[:, :, :, w:2 * w]
                    dve.wait_ge(lvl_put, c.made(lvl_put))
                    for i in range(NT):
                        ins = V.copy_predicated(o[:, i], mask, bank[2 + n % 2][:, 64 * i:64 * i + 64].rearrange("p (j w) -> p j w", w=w))
                    ins.then_inc(lvl_put, c.one(lvl_put))

                for n in range(len(LEVELS) + 2):
                    if n < len(LEVELS):
                        diff(n)
                    if 0 <= n - 1 < len(LEVELS):
                        product(n - 1)
                    if n >= 2:
                        put(n - 2)
            dve.wait_ge(diag_mm, c.next(diag_mm))
            dve.wait_ge(lvl_put, c.made(lvl_put))
            for i in range(NT):
                ins = V.copy_predicated(AT[:, i], ident.bitcast(I32), bank[6][:, P * i:P * i + P])
            ins.then_inc(diag_put, 1)
            dve.wait_ge(head_mm, c.next(head_mm))
        meet(dve, c, "dve")
        head_norm(512, H_HEADS, P, rows[:, ROW_OUT:ROW_OUT + P], 1.0, GG)
        meet(dve, c, "dve")
        gemm(project_out(0), split=False)
        norm(norm_x(COL_N2))
        meet(dve, c, "dve")

        dve.wait_ge(logit_ready, c.next(logit_ready))
        for i in range(NT):
            last = V.tensor_reduce(NM[:, i:i + 1], bank[0][:, 16 * i:16 * i + 16], AX.X, ALU.max, negate=True)
        last.then_inc(logit_max, 1)
        dve.wait_ge(logit_exp, c.next(logit_exp, NT))
        step(V.reciprocal(RDEN, DEN[:, 0:NT]))
        for i in range(NT):
            last = V.tensor_scalar(AFF[:, i], AFF[:, i], RDEN[:, i:i + 1], None, ALU.mult)
        last.then_inc(aff_ready, 1)
        best, work, chosen, place = small[0:16, 256:264], rms[0:16, :], probT[0:16, 0], probT[0:16, 1]
        dve.wait_ge(affT_ready, c.next(affT_ready))
        step(V.tensor_copy(work, bank[1][0:16, :]))
        for n in range(CAP // 8):
            step(V.max(best, work))
            step(V.match_replace(work, best, work, NEG))
        step(V.tensor_scalar(chosen, work, NEG / 2, None, ALU.is_lt))
        step(V.tensor_tensor_scan(place, chosen, chosen, 0.0, ALU.add, ALU.max))
        step(V.tensor_tensor(place, place, chosen, ALU.mult))
        V.tensor_scalar(SLOTT[0:16], place, -1.0, None, ALU.add).then_inc(slotT_ready, 1)
        dve.wait_ge(slot_ready, c.next(slot_ready))
        V.tensor_copy(SLOT, bank[2][:, 0:64].rearrange("p (i e) -> p i e", i=NT))
        meet(dve, c, "dve")
        iota = cst(C_IOTA, CAP).unsqueeze(1).to_broadcast([P, N_EXPERTS, CAP])
        for i in range(NT):
            V.tensor_tensor(CHOICE[:, i].rearrange("p (e n) -> p e n", e=N_EXPERTS),
                            SLOT[:, i].unsqueeze(2).to_broadcast([P, N_EXPERTS, CAP]), iota, ALU.is_equal)
        meet(dve, c, "dve")
        gemm(gathered())
        meet(dve, c, "dve")
        for i in range(NT):
            s, o = (v[:, i].rearrange("p (e n) -> p e n", e=N_EXPERTS) for v in (CHOICE, SEL))
            V.tensor_tensor(o, s.bitcast(F32), AFF[:, i].unsqueeze(2).to_broadcast([P, N_EXPERTS, CAP]), ALU.mult)
        meet(dve, c, "dve")
        meet(dve, c, "dve")
        with dve.Fori(0, N_EXPERTS // 2) as i:
            c.loop(i, {silu_ready: 16, gu_ready: 16, y_ready: 16, down_ready: KC, down_used: KC})
            for n in range(16):
                hidden(n, MG[:, n % 2, 0:64], bank[n % 2][:, 64:128], MGU[:, n % 2, 0:64])
            dve.wait_ge(y_ready, c.next(y_ready, 16))
            V.tensor_copy(YS[:, T:2 * T], bank[3]).then_inc(y_copied, 1)
            add_down(1.0)
            c.looped(N_EXPERTS // 2)
        meet(dve, c, "dve")

    block_cm.__exit__(None, None, None)


def kernel(**inputs):
    import concourse.bacc as bacc
    from concourse.bass_utils import run_bass_kernel_spmd

    a = {k: np.asarray(v) for k, v in inputs.items()}
    f32 = np.float32

    def tiled(w):
        k, n = w.shape
        return w.reshape(k // P, P, n).transpose(1, 0, 2).reshape(P, -1)

    def columns(v):
        return v.reshape(-1, P).T

    def units(wg, wu, wd):
        n = wg.shape[1] // P
        up = [w.reshape(KC, P, n, P).transpose(2, 1, 0, 3).reshape(n, P, D) for w in (wg, wu)]
        return np.concatenate(up + [wd.reshape(n, P, D)], axis=2)

    ffn_w = np.stack([units(a[f"ffn{f}_wg"][l], a[f"ffn{f}_wu"][l], a[f"ffn{f}_wd"][l]) for l in range(LAYERS) for f in (1, 2)])
    moe_w = np.concatenate([units(a["w_expert_gate_2"][0, e], a["w_expert_up_2"][0, e], a["w_expert_down_2"][0, e])
                            for e in range(N_EXPERTS)])

    def items(list_):
        r = np.zeros((len(list_), P, ITEM), f32)
        for n, v in enumerate(list_):
            r[n, :, :v.shape[1]] = v
        return r

    def by_columns(w):
        return [tiled(w[:, n:n + WCOLS]) for n in range(0, w.shape[1], WCOLS)]

    mixes = []
    for l in range(LAYERS):
        w = a["w_in"][l]
        wb, wc = w[:, A_COLS:A_COLS + B_COLS], w[:, A_COLS + B_COLS:]
        qb = wb[:, :384].reshape(D, B_GROUPS, B_HPG, B_DH).transpose(0, 2, 1, 3).reshape(D, 384)
        kv = [wb[:, 384 + 128 * n:512 + 128 * n] for n in range(6)]
        parts = [w[:, :A_COLS], qb, np.concatenate([kv[0], kv[1], kv[2]], 1), np.concatenate([kv[4], kv[3], kv[5]], 1),
                 np.concatenate([wc[:, :256], wb[:, 1152:]], 1), wc[:, 256:512], wc[:, 512:]]
        uq = np.zeros((256, 576), f32)
        uq[:A_QR] = a["mla_w_uq"][l]
        mla = np.concatenate([tiled(uq), a["mla_w_ukv"][l]], 1)
        phi = [np.tile(np.concatenate([a[f"nsa_phi_{s}1"][l].reshape(CMP_LEN, B_DH, B_DH).transpose(1, 0, 2).reshape(B_DH, -1),
                                       a[f"nsa_phi_{s}2"][l]], 1), (2, 1)) for s in "kv"]
        mixes.append(items([tiled(v) for v in parts] + [mla] + phi + by_columns(a["w_out"][l])))
    w2 = a["w_in_2"][0]
    tok = [w2[:, 512 * n + c:512 * n + c + 256] for n in (2, 6, 7) for c in (0, 256)]
    feat = np.concatenate([w2[:, 512 * n:512 * n + 512] for n in (0, 1, 3, 4, 5)], 1)
    in_2 = [tiled(np.concatenate([tok[n], feat[:, P * n:P * n + P]], 1)) for n in range(6)] + by_columns(feat[:, 6 * P:])
    second = items(in_2 + by_columns(a["w_out_2"][0]))

    cols = np.zeros((P, N_COLS), f32)
    for l in range(LAYERS):
        cols[:, COL_FFN1 + 8 * l:COL_FFN1 + 8 * l + 8] = columns(a["ffn1_norm"][l])
        cols[:, COL_MIX + 8 * l:COL_MIX + 8 * l + 8] = columns(a["mix_norm"][l])
        cols[:, COL_FFN2 + 8 * l:COL_FFN2 + 8 * l + 8] = columns(a["ffn2_norm"][l])
        cols[:, COL_MLAQ + 2 * l] = a["mla_q_norm"][l, :P]
        cols[:A_QR - P, COL_MLAQ + 2 * l + 1] = a["mla_q_norm"][l, P:]
        cols[:, COL_MLAKV + l] = a["mla_kv_norm"][l]
        for n, s in enumerate("kv"):
            at = COL_PE + (2 * l + n) * CMP_LEN
            cols[:, at:at + CMP_LEN] = np.tile(a[f"nsa_pe_{s}"][l].T, (2, 1))
    cols[:, COL_FINAL:COL_FINAL + 8] = columns(a["final_norm"])
    cols[:, COL_N1:COL_N1 + 8] = columns(a["norm1_w_2"][0])
    cols[:, COL_N2:COL_N2 + 8] = columns(a["norm2_w_2"][0])
    cols[:, COL_DQ] = np.tile(a["attn_q_norm_w_2"][0], 2)
    cols[:, COL_DK] = np.tile(a["attn_k_norm_w_2"][0], 2)
    for r in range(2):
        for n, s in enumerate(("fwd", "bwd")):
            cols[:, COL_LB + 8 * r + 4 * n:COL_LB + 8 * r + 4 * n + 4] = columns(a[f"hgrn_lb_{s}_2"][r])
    cols[:, COL_ROUTER:] = tiled(a["w_router_2"][0])
    row = np.concatenate([a[f"diff_{s}"][l] for l in range(LAYERS) for s in ("lq1", "lq2", "lk1", "lk2")]
                         + [a["diff_sub_norm"][l] for l in range(LAYERS)] + [a["hgrn_out_norm_w_2"][0]])
    const, const2 = constants()
    arrays = dict(
        ffn_w=ffn_w, mix_w=np.stack(mixes), second_w=second, moe_w=moe_w,
        x_in=np.ascontiguousarray(a["x"][0].T.reshape(KC, P, T).transpose(1, 0, 2)),
        pos_in=np.ascontiguousarray(np.broadcast_to(a["positions"], (P, T))),
        cols_in=cols, rows_in=np.ascontiguousarray(np.broadcast_to(row, (P, N_ROWS))), const_in=const, const2_in=const2)
    nc = bacc.Bacc("TRN2", target_bir_lowering=False, num_devices=1)
    args = [nc.dram_tensor(n, v.shape, mybir.dt.from_np(v.dtype), kind="ExternalInput").ap() for n, v in arrays.items()]
    out = nc.dram_tensor("out", (P, KC, T), F32, kind="ExternalOutput").ap()
    program(nc, *args, out)
    r = run_bass_kernel_spmd(nc, [arrays], core_ids=[0]).results[0]["out"]
    return np.ascontiguousarray(np.asarray(r).transpose(2, 1, 0).reshape(1, T, D))
```
